# Optimizing a Trainium2 kernel written in Bass

```python
import jax, jax.numpy as jnp
from jax import lax
import numpy as np

D_MODEL = 1024
BATCH = 1
SEQ = 512
DEPTH = 2

N_A = DEPTH // 2
N_B = DEPTH - N_A
N_VRES = max(N_A - 1, 0)
HEAD_DIM = 64
N_HEADS = D_MODEL // HEAD_DIM
D_FF = 4 * D_MODEL
DECAY_LORA = 64
AAA_LORA = 64
MV_LORA = 32
GATE_LORA = 160
Q_BLOCK = 128
N_MOD = 6
NORM_EPS = 1e-6
GN_EPS = 64e-5
L2_EPS = 1e-12


def rms_norm(x, g):
    xf = x.astype(jnp.float32)
    y = xf * lax.rsqrt(jnp.mean(xf * xf, axis=-1, keepdims=True) + NORM_EPS)
    return (y * g.astype(jnp.float32)).astype(x.dtype)

def modulate(h, shift, scale):
    return h * (1.0 + scale) + shift

def token_shift(x):
    return jnp.pad(x, ((0, 0), (1, 0), (0, 0)))[:, :-1, :]

def split_heads(t):
    return t.reshape(t.shape[0], t.shape[1], N_HEADS, HEAD_DIM)

def wkv7_scan(r, decay, k, v, a_vec, b_vec):
    bsz = r.shape[0]
    xs = tuple(jnp.moveaxis(t.astype(jnp.float32), 1, 0) for t in (r, decay, k, v, a_vec, b_vec))

    def step(S, inp):
        r_t, w_t, k_t, v_t, a_t, b_t = inp
        sa = jnp.einsum('bhvk,bhk->bhv', S, a_t)
        S = S * w_t[:, :, None, :] + sa[..., :, None] * b_t[..., None, :] + v_t[..., :, None] * k_t[..., None, :]
        y = jnp.einsum('bhvk,bhk->bhv', S, r_t)
        return S, y

    S0 = jnp.zeros((bsz, N_HEADS, HEAD_DIM, HEAD_DIM), jnp.float32)
    _, ys = lax.scan(step, S0, xs)
    return jnp.moveaxis(ys, 0, 1)

def rwkv7_time_mix(h, v_first, vres, mu, wr, wk, wv, wo, w0, w1, w2, a0, a1, a2,
                   g1, g2, k_k, k_a, r_k, ln_w, ln_b):
    bsz, T, _ = h.shape
    xx = token_shift(h) - h
    xr, xw, xk, xv, xa, xg = (h + xx * mu[j] for j in range(6))
    r = xr @ wr
    w_log = -jax.nn.softplus(-(w0 + jnp.tanh(xw @ w1) @ w2)) - 0.5
    k = xk @ wk
    v = xv @ wv
    if vres is None:
        v_first = v
    else:
        v0, v1, v2 = vres
        v = v + (v_first - v) * jax.nn.sigmoid(v0 + (xv @ v1) @ v2)
    a = jax.nn.sigmoid(a0 + (xa @ a1) @ a2)
    g = jax.nn.sigmoid(xg @ g1) @ g2
    kk = split_heads(k * k_k).astype(jnp.float32)
    kk = kk / jnp.maximum(jnp.sqrt(jnp.sum(kk * kk, axis=-1, keepdims=True)), L2_EPS)
    k = k * (1.0 + (a - 1.0) * k_a)
    decay = jnp.exp(-jnp.exp(w_log.astype(jnp.float32)))
    rh, kh, vh = split_heads(r), split_heads(k), split_heads(v)
    ah = split_heads(a).astype(jnp.float32)
    y = wkv7_scan(rh, split_heads(decay), kh, vh, -kk, kk * ah)
    mean = jnp.mean(y, axis=-1, keepdims=True)
    var = jnp.mean(jnp.square(y - mean), axis=-1, keepdims=True)
    y = ((y - mean) * lax.rsqrt(var + GN_EPS)).reshape(bsz, T, D_MODEL)
    y = y * ln_w.astype(jnp.float32) + ln_b.astype(jnp.float32)
    bonus = jnp.sum((rh * kh * r_k).astype(jnp.float32), axis=-1, keepdims=True) * vh.astype(jnp.float32)
    y = (y + bonus.reshape(bsz, T, D_MODEL)).astype(h.dtype)
    return (y * g) @ wo, v_first

def shared_kv(x, shift, scale, norm_g, w_kv, f_bias, k_gain):
    h = modulate(rms_norm(x, norm_g), shift, scale)
    kvf = h @ w_kv
    k = kvf[..., :D_MODEL]
    v = kvf[..., D_MODEL:2 * D_MODEL]
    f_logit = kvf[..., 2 * D_MODEL:]
    k = rms_norm(split_heads(k), k_gain)
    log_f = jax.nn.log_sigmoid(f_logit.astype(jnp.float32) + f_bias.astype(jnp.float32))
    F = jnp.cumsum(log_f, axis=1)
    return (k.transpose(0, 2, 1, 3), split_heads(v).transpose(0, 2, 1, 3).astype(jnp.float32),
            F.transpose(0, 2, 1))

def forgetting_attention(h, k, v, F, w_qg, q_gain, w_o):
    bsz, T, _ = h.shape
    qg = h @ w_qg
    q, gate = qg[..., :D_MODEL], qg[..., D_MODEL:]
    q = rms_norm(split_heads(q), q_gain).transpose(0, 2, 1, 3)
    sm_scale = HEAD_DIM ** -0.5
    kpos = jnp.arange(T)

    def block(start):
        qb = lax.dynamic_slice_in_dim(q, start, Q_BLOCK, axis=2)
        Fq = lax.dynamic_slice_in_dim(F, start, Q_BLOCK, axis=2)
        s = jnp.einsum('bhqd,bhkd->bhqk', qb, k).astype(jnp.float32) * sm_scale
        s = s + Fq[..., :, None] - F[..., None, :]
        qpos = start + jnp.arange(Q_BLOCK)
        s = jnp.where(kpos[None, :] <= qpos[:, None], s, -jnp.inf)
        p = jax.nn.softmax(s, axis=-1)
        return jnp.einsum('bhqk,bhkd->bhqd', p, v)

    starts = jnp.arange(T // Q_BLOCK) * Q_BLOCK
    o = lax.map(block, starts)
    o = o.transpose(1, 0, 3, 2, 4).reshape(bsz, T, D_MODEL).astype(h.dtype)
    return (o * jax.nn.sigmoid(gate)) @ w_o

def sq_relu_mlp(h, w_up, w_down):
    return jnp.square(jax.nn.relu(h @ w_up)) @ w_down

def first_inputs(seed: int = 0) -> dict:
    key = jax.random.key(seed)
    keys = iter(jax.random.split(key, 48))
    f32 = jnp.float32

    def nrm(shape, scale):
        return jax.random.normal(next(keys), shape, f32) * scale

    def unif(shape, lo, hi):
        return jax.random.uniform(next(keys), shape, f32, lo, hi)

    D = D_MODEL
    return {
        'x': nrm((BATCH, SEQ, D), 1.0),
        'c': nrm((BATCH, D), 1.0),
        'mod_w': nrm((DEPTH, D, N_MOD * D), 0.2 * D ** -0.5),
        'mod_b': nrm((DEPTH, N_MOD * D), 0.01),
        'norm_mix_g': 1.0 + nrm((DEPTH, D), 0.02),
        'norm_mlp_g': 1.0 + nrm((DEPTH, D), 0.02),
        'mlp_up': nrm((DEPTH, D, D_FF), D ** -0.5),
        'mlp_down': nrm((DEPTH, D_FF, D), D_FF ** -0.5),
        'rw_mu': unif((N_A, 6, D), 0.0, 1.0),
        'rw_wr': nrm((N_A, D, D), D ** -0.5),
        'rw_wk': nrm((N_A, D, D), D ** -0.5),
        'rw_wv': nrm((N_A, D, D), D ** -0.5),
        'rw_wo': nrm((N_A, D, D), D ** -0.5),
        'rw_w0': unif((N_A, D), -6.0, 0.0),
        'rw_w1': nrm((N_A, D, DECAY_LORA), D ** -0.5),
        'rw_w2': nrm((N_A, DECAY_LORA, D), 0.1 * DECAY_LORA ** -0.5),
        'rw_a0': nrm((N_A, D), 0.1),
        'rw_a1': nrm((N_A, D, AAA_LORA), D ** -0.5),
        'rw_a2': nrm((N_A, AAA_LORA, D), 0.1 * AAA_LORA ** -0.5),
        'rw_g1': nrm((N_A, D, GATE_LORA), D ** -0.5),
        'rw_g2': nrm((N_A, GATE_LORA, D), GATE_LORA ** -0.5),
        'rw_kk': 0.85 + nrm((N_A, D), 0.02),
        'rw_ka': 1.0 + nrm((N_A, D), 0.02),
        'rw_rk': nrm((N_A, N_HEADS, HEAD_DIM), 0.1),
        'rw_lnw': 1.0 + nrm((N_A, D), 0.02),
        'rw_lnb': nrm((N_A, D), 0.01),
        'rw_v0': 1.0 + nrm((N_VRES, D), 0.02),
        'rw_v1': nrm((N_VRES, D, MV_LORA), D ** -0.5),
        'rw_v2': nrm((N_VRES, MV_LORA, D), 0.1 * MV_LORA ** -0.5),
        'kv_norm_g': 1.0 + nrm((D,), 0.02),
        'kv_mod_w': nrm((D, 2 * D), 0.2 * D ** -0.5),
        'kv_mod_b': nrm((2 * D,), 0.01),
        'kv_w': nrm((D, 2 * D + N_HEADS), D ** -0.5),
        'kv_fb': unif((N_HEADS,), 1.0, 5.0),
        'kv_kg': 1.0 + nrm((HEAD_DIM,), 0.02),
        'fx_wqg': nrm((N_B, D, 2 * D), D ** -0.5),
        'fx_qg': 1.0 + nrm((N_B, HEAD_DIM), 0.02),
        'fx_wo': nrm((N_B, D, D), D ** -0.5),
        'final_g': 1.0 + nrm((D,), 0.02),
    }

def first_block(x, c, mod_w, mod_b, norm_mix_g, norm_mlp_g, mlp_up, mlp_down,
              rw_mu, rw_wr, rw_wk, rw_wv, rw_wo, rw_w0, rw_w1, rw_w2, rw_a0, rw_a1, rw_a2,
              rw_g1, rw_g2, rw_kk, rw_ka, rw_rk, rw_lnw, rw_lnb, rw_v0, rw_v1, rw_v2,
              kv_norm_g, kv_mod_w, kv_mod_b, kv_w, kv_fb, kv_kg,
              fx_wqg, fx_qg, fx_wo, final_g):
    c_act = jax.nn.silu(c)
    v_first = None
    k_sh = v_sh = F_sh = None
    for i in range(DEPTH):
        mod = (c_act @ mod_w[i] + mod_b[i])[:, None, :]
        sh1, sc1, gt1, sh2, sc2, gt2 = jnp.split(mod, N_MOD, axis=-1)
        if i == N_A:
            kvm = (c_act @ kv_mod_w + kv_mod_b)[:, None, :]
            kv_shift, kv_scale = jnp.split(kvm, 2, axis=-1)
            k_sh, v_sh, F_sh = shared_kv(x, kv_shift, kv_scale, kv_norm_g, kv_w, kv_fb, kv_kg)
        h = modulate(rms_norm(x, norm_mix_g[i]), sh1, sc1)
        if i < N_A:
            vres = None if i == 0 else (rw_v0[i - 1], rw_v1[i - 1], rw_v2[i - 1])
            y, v_first = rwkv7_time_mix(h, v_first, vres, rw_mu[i], rw_wr[i], rw_wk[i], rw_wv[i], rw_wo[i],
                                        rw_w0[i], rw_w1[i], rw_w2[i], rw_a0[i], rw_a1[i], rw_a2[i],
                                        rw_g1[i], rw_g2[i], rw_kk[i], rw_ka[i], rw_rk[i],
                                        rw_lnw[i], rw_lnb[i])
        else:
            j = i - N_A
            y = forgetting_attention(h, k_sh, v_sh, F_sh, fx_wqg[j], fx_qg[j], fx_wo[j])
        x = x + (1.0 + gt1) * y
        h = modulate(rms_norm(x, norm_mlp_g[i]), sh2, sc2)
        x = x + (1.0 + gt2) * sq_relu_mlp(h, mlp_up[i], mlp_down[i])
    return rms_norm(x, final_g)


CTX_LEN = 256
GRID_W = 64
N_MIXERS = 2
EXPAND = 2
D_INNER = EXPAND * D_MODEL
MLSTM_HEADS = 4
MLSTM_HEAD_DIM = D_INNER // MLSTM_HEADS
CHUNK = 64
CONV_K = 3
FOURIER_GROUPS = 8
FOURIER_GROUP_DIM = D_INNER // FOURIER_GROUPS
N_MLSTM_LAYERS = (DEPTH + 1) // 2
N_FOURIER_LAYERS = DEPTH // 2
LAST_MLSTM = ((DEPTH - 1) // N_MIXERS) * N_MIXERS
EPS = 1e-6


H = MLSTM_HEADS
DH = MLSTM_HEAD_DIM

def rmsnorm(x, g):
    xf = x.astype(jnp.float32)
    y = xf * lax.rsqrt(jnp.mean(xf * xf, axis=-1, keepdims=True) + EPS)
    return (y * g.astype(jnp.float32)).astype(x.dtype)

def mlstm_chunk_scan(q, k, v, li, lf, state, emit):
    b, h, n, d = q.shape
    nc = n // CHUNK

    def to_chunks(a):
        a = a.reshape(b, h, nc, CHUNK, *a.shape[3:])
        return jnp.moveaxis(a, 2, 0)

    lower = jnp.tril(jnp.ones((CHUNK, CHUNK), dtype=bool))

    def step(carry, inp):
        C, nv, m = carry
        qc, kc, vc, lic, lfc = inp
        bcum = jnp.cumsum(lfc, axis=-1)
        logw = bcum[..., :, None] - bcum[..., None, :] + lic[..., None, :]
        logw = jnp.where(lower, logw, -jnp.inf)
        log_prev = bcum + m[..., None]
        m_new = jnp.maximum(log_prev, jnp.max(logw, axis=-1))
        w_intra = jnp.exp(logw - m_new[..., None])
        w_prev = jnp.exp(log_prev - m_new)
        out = None
        if emit:
            scores = jnp.einsum('bhjd,bhsd->bhjs', qc, kc) * w_intra
            num = jnp.einsum('bhjs,bhsd->bhjd', scores, vc) + \
                w_prev[..., None] * jnp.einsum('bhvk,bhjk->bhjv', C, qc)
            den = jnp.sum(scores, axis=-1) + w_prev * jnp.einsum('bhk,bhjk->bhj', nv, qc)
            out = num / jnp.maximum(jnp.abs(den), jnp.exp(-m_new))[..., None]
        m_end = m_new[..., -1]
        w_src = jnp.exp(bcum[..., -1:] - bcum + lic - m_end[..., None])
        decay = jnp.exp(bcum[..., -1] + m - m_end)
        C_new = decay[..., None, None] * C + jnp.einsum('bhsv,bhsk->bhvk', w_src[..., None] * vc, kc)
        n_new = decay[..., None] * nv + jnp.einsum('bhs,bhsk->bhk', w_src, kc)
        return (C_new, n_new, m_end), out

    state, hs = lax.scan(step, state, tuple(to_chunks(a) for a in (q, k, v, li, lf)))
    if emit:
        hs = jnp.moveaxis(hs, 0, 2).reshape(b, h, n, d)
    return hs, state

def mlstm_inputs(hmod, grid_rows, grid_cols, w_in, conv_w, conv_b, w_q, w_k, w_if, b_i, b_f):
    b, n, _ = hmod.shape
    xm, o_pre, z = jnp.split(hmod @ w_in, 3, axis=-1)
    xg = xm.reshape(b, grid_rows, grid_cols, D_INNER)
    xconv = lax.conv_general_dilated(xg, conv_w, (1, 1), 'SAME',
                                     dimension_numbers=('NHWC', 'HWIO', 'NHWC'),
                                     feature_group_count=D_INNER)
    xconv = jax.nn.silu(xconv.reshape(b, n, D_INNER) + conv_b)
    xh = xconv.reshape(b, n, H, DH)
    q = jnp.einsum('bnhd,hde->bhne', xh, w_q).astype(jnp.float32)
    k = (jnp.einsum('bnhd,hde->bhne', xh, w_k) * (DH ** -0.5)).astype(jnp.float32)
    v = xm.reshape(b, n, H, DH).transpose(0, 2, 1, 3).astype(jnp.float32)
    wq_g = w_if[:, 0].reshape(2, H, DH, 2 * H).astype(jnp.float32)
    wk_g = w_if[:, 1].reshape(2, H, DH, 2 * H).astype(jnp.float32)
    wv_g = w_if[:, 2].reshape(2, H, DH, 2 * H).astype(jnp.float32)
    gates = (jnp.einsum('bhne,rheg->rbng', q, wq_g) + jnp.einsum('bhne,rheg->rbng', k, wk_g)
             + jnp.einsum('bhne,rheg->rbng', v, wv_g))
    li = gates[..., :H] + b_i.astype(jnp.float32)[:, None, None, :]
    lf = jax.nn.log_sigmoid(gates[..., H:] + b_f.astype(jnp.float32)[:, None, None, :])
    li = jnp.moveaxis(li, -1, 2)
    lf = jnp.moveaxis(lf, -1, 2)
    return (q, k, v, li, lf), o_pre, z, xconv

def mlstm_output(hsum, o_pre, z, xconv, ln_w, skip, w_out, dtype):
    b, _, n, _ = hsum.shape
    hh = hsum.transpose(0, 2, 1, 3)
    mu = jnp.mean(hh, axis=-1, keepdims=True)
    var = jnp.mean(jnp.square(hh - mu), axis=-1, keepdims=True)
    hn = ((hh - mu) * lax.rsqrt(var + EPS)).reshape(b, n, D_INNER) * ln_w.astype(jnp.float32)
    hn = jax.nn.sigmoid(o_pre.astype(jnp.float32)) * hn
    y = (hn.astype(dtype) + skip * xconv) * jax.nn.silu(z)
    return y @ w_out

def mlstm_branch(h_lat, h_ctx, rows, emit_ctx, w_in, conv_w, conv_b, w_q, w_k, w_if,
                 b_i, b_f, ln_w, skip, w_out):
    lat, o_l, z_l, xc_l = mlstm_inputs(h_lat, rows, GRID_W, w_in, conv_w, conv_b, w_q, w_k, w_if, b_i, b_f)
    ctx, o_c, z_c, xc_c = mlstm_inputs(h_ctx, 1, h_ctx.shape[1], w_in, conv_w, conv_b, w_q, w_k, w_if, b_i, b_f)
    b = h_lat.shape[0]
    zero = (jnp.zeros((b, H, DH, DH), jnp.float32), jnp.zeros((b, H, DH), jnp.float32),
            jnp.zeros((b, H), jnp.float32))
    h_lat_sum = 0.0
    h_ctx_sum = 0.0
    for r, rev in ((0, False), (1, True)):
        fl = (lambda a: jnp.flip(a, 2)) if rev else (lambda a: a)
        qc, kc, vc, lic, lfc = ctx
        ql, kl, vl, lil, lfl = lat
        hc, st = mlstm_chunk_scan(fl(qc), fl(kc), fl(vc), fl(lic[r]), fl(lfc[r]), zero, emit_ctx)
        hl, _ = mlstm_chunk_scan(fl(ql), fl(kl), fl(vl), fl(lil[r]), fl(lfl[r]), st, True)
        h_lat_sum = h_lat_sum + fl(hl)
        if emit_ctx:
            h_ctx_sum = h_ctx_sum + fl(hc)
    y_lat = mlstm_output(h_lat_sum, o_l, z_l, xc_l, ln_w, skip, w_out, h_lat.dtype)
    y_ctx = mlstm_output(h_ctx_sum, o_c, z_c, xc_c, ln_w, skip, w_out, h_ctx.dtype) if emit_ctx else None
    return y_lat, y_ctx

def fourier_branch(hmod, w_in, w_out):
    b, n, _ = hmod.shape
    u, z = jnp.split(hmod @ w_in, 2, axis=-1)
    ug = u.astype(jnp.float32).reshape(b, n, FOURIER_GROUPS, FOURIER_GROUP_DIM)
    f = jnp.fft.fft2(ug, axes=(1, 3), norm='ortho').real
    y = f.reshape(b, n, D_INNER).astype(hmod.dtype) * jax.nn.silu(z)
    return y @ w_out

def second_inputs(seed: int = 0) -> dict:
    key = jax.random.key(seed)
    ks = jax.random.split(key, 24)
    nA, nB, E = N_MLSTM_LAYERS, N_FOURIER_LAYERS, D_INNER
    nrm = jax.random.normal
    return {
        "x": nrm(ks[0], (BATCH, SEQ, D_MODEL), jnp.float32),
        "c": nrm(ks[1], (BATCH, D_MODEL), jnp.float32),
        "ctx": nrm(ks[2], (BATCH, CTX_LEN, D_MODEL), jnp.float32),
        "c_ctx": nrm(ks[3], (D_MODEL,), jnp.float32),
        "norm_g": 1.0 + 0.1 * nrm(ks[4], (DEPTH, D_MODEL), jnp.float32),
        "w_ada": nrm(ks[5], (DEPTH, D_MODEL, 3 * D_MODEL), jnp.float32) * D_MODEL ** -0.5,
        "b_ada": 0.02 * nrm(ks[6], (DEPTH, 3 * D_MODEL), jnp.float32),
        "m_w_in": nrm(ks[7], (nA, D_MODEL, 3 * E), jnp.float32) * D_MODEL ** -0.5,
        "m_conv_w": nrm(ks[8], (nA, CONV_K, CONV_K, 1, E), jnp.float32) / CONV_K,
        "m_conv_b": 0.02 * nrm(ks[9], (nA, E), jnp.float32),
        "m_w_q": nrm(ks[10], (nA, H, DH, DH), jnp.float32) * DH ** -0.5,
        "m_w_k": nrm(ks[11], (nA, H, DH, DH), jnp.float32) * DH ** -0.5,
        "m_w_if": nrm(ks[12], (nA, 2, 3, E, 2 * H), jnp.float32) * (3 * E) ** -0.5,
        "m_b_i": 0.1 * nrm(ks[13], (nA, 2, H), jnp.float32),
        "m_b_f": jnp.linspace(3.0, 6.0, H, dtype=jnp.float32) + 0.1 * nrm(ks[14], (nA, 2, H), jnp.float32),
        "m_ln_w": 1.0 + 0.1 * nrm(ks[15], (nA, E), jnp.float32),
        "m_skip": 1.0 + 0.1 * nrm(ks[16], (nA, E), jnp.float32),
        "m_w_out": nrm(ks[17], (nA, E, D_MODEL), jnp.float32) * E ** -0.5,
        "f_w_in": nrm(ks[18], (nB, D_MODEL, 2 * E), jnp.float32) * D_MODEL ** -0.5,
        "f_w_out": nrm(ks[19], (nB, E, D_MODEL), jnp.float32) * E ** -0.5,
        "norm_f": 1.0 + 0.1 * nrm(ks[20], (D_MODEL,), jnp.float32),
    }

def second_block(x, c, ctx, c_ctx, norm_g, w_ada, b_ada, m_w_in, m_conv_w, m_conv_b, m_w_q, m_w_k,
              m_w_if, m_b_i, m_b_f, m_ln_w, m_skip, m_w_out, f_w_in, f_w_out, norm_f):
    rows = x.shape[1] // GRID_W
    xc = ctx
    sc_lat = jax.nn.silu(c)
    sc_ctx = jax.nn.silu(c_ctx)
    for i in range(DEPTH):
        j = i // N_MIXERS
        update_ctx = i < LAST_MLSTM
        sh, sc, g = jnp.split(sc_lat @ w_ada[i] + b_ada[i], 3, axis=-1)
        h = rmsnorm(x, norm_g[i]) * (1.0 + sc[:, None, :]) + sh[:, None, :]
        need_ctx_in = update_ctx or (i % N_MIXERS == 0)
        if need_ctx_in:
            shc, scc, gc = jnp.split(sc_ctx @ w_ada[i] + b_ada[i], 3, axis=-1)
            hc = rmsnorm(xc, norm_g[i]) * (1.0 + scc) + shc
        if i % N_MIXERS == 0:
            y, yc = mlstm_branch(h, hc, rows, update_ctx, m_w_in[j], m_conv_w[j], m_conv_b[j],
                                 m_w_q[j], m_w_k[j], m_w_if[j], m_b_i[j], m_b_f[j],
                                 m_ln_w[j], m_skip[j], m_w_out[j])
        else:
            y = fourier_branch(h, f_w_in[j], f_w_out[j])
            yc = fourier_branch(hc, f_w_in[j], f_w_out[j]) if update_ctx else None
        x = x + g[:, None, :] * y
        if update_ctx:
            xc = xc + gc * yc
    return rmsnorm(x, norm_f)


def setup_inputs(seed=0):
    out = dict(first_inputs(seed))
    for name, value in second_inputs(seed + 1).items():
        if name != "x":
            out[name + "_2"] = value
    return out


def reference(
    x, c, mod_w, mod_b, norm_mix_g, norm_mlp_g, mlp_up, mlp_down, rw_mu, rw_wr, rw_wk, rw_wv,
    rw_wo, rw_w0, rw_w1, rw_w2, rw_a0, rw_a1, rw_a2, rw_g1, rw_g2, rw_kk, rw_ka, rw_rk, rw_lnw,
    rw_lnb, rw_v0, rw_v1, rw_v2, kv_norm_g, kv_mod_w, kv_mod_b, kv_w, kv_fb, kv_kg, fx_wqg,
    fx_qg, fx_wo, final_g, c_2, ctx_2, c_ctx_2, norm_g_2, w_ada_2, b_ada_2, m_w_in_2,
    m_conv_w_2, m_conv_b_2, m_w_q_2, m_w_k_2, m_w_if_2, m_b_i_2, m_b_f_2, m_ln_w_2, m_skip_2,
    m_w_out_2, f_w_in_2, f_w_out_2, norm_f_2,
):
    x = first_block(
        x, c, mod_w, mod_b, norm_mix_g, norm_mlp_g, mlp_up, mlp_down, rw_mu, rw_wr, rw_wk,
        rw_wv, rw_wo, rw_w0, rw_w1, rw_w2, rw_a0, rw_a1, rw_a2, rw_g1, rw_g2, rw_kk, rw_ka,
        rw_rk, rw_lnw, rw_lnb, rw_v0, rw_v1, rw_v2, kv_norm_g, kv_mod_w, kv_mod_b, kv_w, kv_fb,
        kv_kg, fx_wqg, fx_qg, fx_wo, final_g,
    )
    return second_block(
        x, c_2, ctx_2, c_ctx_2, norm_g_2, w_ada_2, b_ada_2, m_w_in_2, m_conv_w_2, m_conv_b_2,
        m_w_q_2, m_w_k_2, m_w_if_2, m_b_i_2, m_b_f_2, m_ln_w_2, m_skip_2, m_w_out_2, f_w_in_2,
        f_w_out_2, norm_f_2,
    )


_drawn_inputs = setup_inputs


def setup_inputs(seed=0):
    import zlib

    import numpy as np

    out = dict(_drawn_inputs(seed))
    spreads = {}
    factors = {'rw_w1': 8.0,
     'rw_w2': 8.0,
     'rw_kk': 3.925,
     'rw_ka': 3.745,
     'rw_lnw': 4.175,
     'rw_lnb': 6.234,
     'kv_norm_g': 8.0,
     'kv_mod_b': 8.0,
     'kv_kg': 8.0,
     'fx_qg': 8.0,
     'm_conv_b_2': 2.97,
     'm_b_i_2': 8.0}
    for name, (base, spread) in spreads.items():
        noise = np.random.default_rng([zlib.crc32(name.encode()), seed]).standard_normal(out[name].shape)
        drawn = base * np.exp(spread * noise) if base else spread * noise
        out[name] = __import__('jax').numpy.asarray(drawn.astype(out[name].dtype))
    for name, factor in factors.items():
        out[name] = (out[name] * factor).astype(out[name].dtype)
    return out
```

```python
from contextlib import ExitStack

import numpy as np

import concourse.bass as bass
from concourse import mybir

F32 = mybir.dt.float32
F32R = mybir.dt.float32r
ACT = mybir.ActivationFunctionType
ALU = mybir.AluOpType
AX = mybir.AxisListType
ds = bass.ds

P = 128
T = 512
D = 1024
KT = D // P
TX = 256
TA = TX + T
NF = 4 * D // P
E2 = 2048
ET = E2 // P
CH = 64
NC = T // CH
BLK = 2048
RAW, SPL = 2, 2
NACC = 4
LAGGED = (*(f"acc_free{b}" for b in range(NACC)), "mat_by_act", "mat_by_dve", "mid_ready", "qk_sum", "qk_sum",
          "o_gated", "gates_read", "v_sent", "s_sent", "skip_sent0",
          "skip_sent1", "s_used", "v_used", "gt_used0", "gt_used1", "gt_used2", "gt_used3")
HALF = 0.6065306597126334
NORM_EPS, GN_EPS = 1e-6, 64e-5


def cols(v):
    return np.ascontiguousarray(np.asarray(v).reshape(-1, P).T)


def blocks(w, width=256, kt=8):
    w = np.asarray(w)
    rows, n = w.shape
    b = w.reshape(rows // (P * kt), kt, P, n // width, width).transpose(3, 0, 2, 1, 4)
    b = b.reshape(-1, P, kt * width)
    out = np.zeros((b.shape[0], P, BLK), w.dtype)
    out[:, :, :kt * width] = b
    return out


def padded(w, rows, n):
    out = np.zeros((rows, n), np.asarray(w).dtype)
    out[:w.shape[0], :w.shape[1]] = w
    return out


def stream(x):
    def mlp(i):
        up, down = x["mlp_up"][i], x["mlp_down"][i]
        u = [blocks(up[:, D * q:D * (q + 1)]) for q in range(4)]
        d = [blocks(down[D * q:D * (q + 1)]) for q in range(4)]
        return [u[0], u[1], d[0], u[2], d[1], u[3], d[2], d[3]]
    lora_w = np.zeros((1, P, BLK), np.float32)
    lora_w[0, :64, :D] = x["rw_w2"][0]
    lora_w[0, :64, D:] = x["rw_a2"][0]
    seq = [("raw", "mod0", blocks(x["mod_w"][0][:, :2 * D])),
           ("split", "w1", blocks(padded(x["rw_w1"][0], D, P), P)),
           ("split", "a1", blocks(padded(x["rw_a1"][0], D, P), P)),
           ("split", "w2a2", lora_w),
           ("split", "g1", blocks(padded(x["rw_g1"][0], D, 256))),
           ("split", "wr", blocks(x["rw_wr"][0])),
           ("split", "wk", blocks(x["rw_wk"][0])),
           ("split", "wv", blocks(x["rw_wv"][0])),
           ("raw", "mod0b", blocks(x["mod_w"][0][:, 2 * D:])),
           ("raw", "mod1", blocks(x["mod_w"][1])),
           ("raw", "kvm", blocks(x["kv_mod_w"])),
           ("raw", "ada0", blocks(x["w_ada_2"][0])),
           ("raw", "ada1", blocks(x["w_ada_2"][1])),
           ("split", "g2", blocks(padded(x["rw_g2"][0], 256, D), D, 2)),
           ("split", "wo", blocks(x["rw_wo"][0]))]
    seq += [("split", f"mlp0_{j}", b) for j, b in enumerate(mlp(0))]
    kv = x["kv_w"]
    wqg = x["fx_wqg"][0]
    seq += [("split", "kvk", blocks(kv[:, :D])),
            ("split", "kvf", blocks(padded(kv[:, 2 * D:], D, P), P)),
            ("split", "kvv", blocks(kv[:, D:2 * D])),
            ("split", "fq", blocks(wqg)),
            ("split", "fo", blocks(x["fx_wo"][0]))]
    seq += [("split", f"mlp1_{j}", b) for j, b in enumerate(mlp(1))]
    w_in = x["m_w_in_2"][0]
    wif = np.asarray(x["m_w_if_2"][0])
    for h in range(4):
        c = slice(512 * h, 512 * (h + 1))
        gate = np.zeros((1, P, 12, P), wif.dtype)
        for t in range(3):
            for d in range(2):
                part = wif[d, t, c].reshape(4, P, 8).transpose(1, 0, 2)
                gate[0, :, 4 * t:4 * t + 4, 64 * d:64 * d + 4] = part[:, :, :4]
                gate[0, :, 4 * t:4 * t + 4, 64 * d + 32:64 * d + 36] = part[:, :, 4:]
        g = np.zeros((1, P, BLK), wif.dtype)
        g[:, :, :12 * P] = gate.reshape(1, P, -1)
        seq += [("split", f"xm{h}", blocks(w_in[:, c])),
                ("split", f"q{h}", blocks(x["m_w_q_2"][0, h], 512, 4)),
                ("split", f"k{h}", blocks(x["m_w_k_2"][0, h], 512, 4)),
                ("raw", f"gate{h}", g)]
    f_in = x["f_w_in_2"][0]
    seq += [("split", "o", blocks(w_in[:, E2:2 * E2])),
            ("split", "z", blocks(w_in[:, 2 * E2:])),
            ("split", "mo", blocks(x["m_w_out_2"][0])),
            ("split", "fu", blocks(f_in[:, :E2])),
            ("split", "fz", blocks(f_in[:, E2:])),
            ("split", "fo2", blocks(x["f_w_out_2"][0]))]
    return seq


def vectors(x):
    v = {}
    for i in range(2):
        v[f"nmix{i}"] = cols(x["norm_mix_g"][i])
        v[f"nmlp{i}"] = cols(x["norm_mlp_g"][i])
        v[f"modb{i}"] = cols(x["mod_b"][i])
        v[f"adab{i}"] = cols(x["b_ada_2"][i])
        v[f"n2{i}"] = cols(x["norm_g_2"][i])
    v["c"] = cols(x["c"])
    v["c3"] = np.stack([cols(x["c"]), cols(x["c_2"]), cols(x["c_ctx_2"])], 2).reshape(P, -1)
    for j in range(6):
        v[f"mu{j}"] = cols(x["rw_mu"][0, j])
    v["w0"], v["a0"] = cols(x["rw_w0"][0]), cols(x["rw_a0"][0])
    pair = [cols(x[n][0]) for n in ("rw_kk", "rw_ka", "rw_rk", "rw_lnw", "rw_lnb")]
    v["pair"] = np.stack(pair, 2).reshape(P, -1)
    v["kvn"], v["kvmb"] = cols(x["kv_norm_g"]), cols(x["kv_mod_b"])
    v["kg"], v["qg"] = cols(np.tile(x["kv_kg"], 2)), cols(np.tile(x["fx_qg"][0], 2))
    v["fb"] = padded(np.asarray(x["kv_fb"])[:, None], P, 1)
    v["final"] = cols(x["final_g"])
    v["convw"] = np.asarray(x["m_conv_w_2"][0]).reshape(9, ET, P).transpose(2, 1, 0).reshape(P, -1)
    v["convb"] = cols(x["m_conv_b_2"][0])
    bias = np.zeros((P, 1), np.float32)
    for d in range(2):
        bias[64 * d:64 * d + 4, 0] = x["m_b_i_2"][0, d]
        bias[64 * d + 32:64 * d + 36, 0] = x["m_b_f_2"][0, d]
    v["bif"] = bias
    v["lnw2"], v["skip"] = cols(x["m_ln_w_2"][0]), cols(x["m_skip_2"][0])
    v["normf"] = cols(x["norm_f_2"])
    return v


def constants():
    c = {}
    i = np.arange(P)
    same = i[:, None] // 64 == i[None] // 64
    c["ident"] = np.eye(P)
    c["ones"] = np.ones((P, P))
    c["head"] = same * 1.0
    up, upi = same * (i[:, None] < i[None]), same * (i[:, None] <= i[None])
    c["mrec"] = np.concatenate([up, upi], 1)
    c["m16"] = i[:, None] // 16 == i[None] // 16
    c["mlow16"] = c["m16"] * (i[:, None] > i[None])
    c["keep"] = np.tile(np.arange(T) % CH != 0, (P, 1))
    c["causal"] = np.where(i[None] <= i[:, None], 0.0, -1e30)
    c["fwd"] = (i[:, None] <= i[None]) * 1.0
    c["rev"] = (i[:, None] >= i[None]) * 1.0
    c["epsn"] = np.full((P, 1), NORM_EPS)
    c["zero"] = np.zeros((P, 1))
    c["epsg"] = np.full((P, 1), GN_EPS)
    return {k: np.asarray(v, np.float32) for k, v in c.items()}


def dft_tables():
    a = 2 * np.pi * (np.arange(256)[:, None] * np.arange(256)[None] % 256) / 256
    ch = np.concatenate([np.cos(a), np.sin(a)], 1).reshape(2, P, 512).transpose(1, 0, 2)
    b = 2 * np.pi * (np.arange(T)[:, None] * np.arange(T)[None] % T) / T
    f = (T * 256) ** -0.5
    tok = np.stack([np.cos(b) * f, -np.sin(b) * f]).reshape(2, 4, P, T).transpose(2, 0, 1, 3)
    return ch.reshape(P, -1).astype(np.float32), tok.reshape(P, -1).astype(np.float32)


def layout(x):
    seq = stream(x)
    vec, con = vectors(x), constants()
    ch, tok = dft_tables()
    arrays = {
        "wst": np.concatenate([b for _, _, b in seq]),
        "vec": np.concatenate(list(vec.values()), 1),
        "con": np.concatenate(list(con.values()), 1),
        "xT": np.ascontiguousarray(np.asarray(x["x"])[0].T.reshape(KT, P, T).transpose(1, 0, 2)),
        "cT": np.ascontiguousarray(np.asarray(x["ctx_2"])[0].T.reshape(KT, P, TX).transpose(1, 0, 2)),
        "dch": ch, "dtok": tok,
    }
    plan = [(kind, name, b.shape[0]) for kind, name, b in seq]
    vat, cat = {}, {}
    for table, parts in ((vat, vec), (cat, con)):
        at = 0
        for k, a in parts.items():
            table[k] = (at, a.shape[1])
            at += a.shape[1]
    return arrays, plan, vat, cat


class Dry:

    def _same(self, *args, **kwargs):
        return self

    matmul = transpose = activation = tensor_tensor = tensor_scalar = scalar_tensor_tensor = _same
    tensor_copy = tensor_reduce = reciprocal = memset = dma_start = then_inc = wait_ge = nop = _same
    tensor_tensor_scan = affine_select = _same


class Engine:

    def __init__(self, book, name):
        self.book, self.name, self.latest = book, name, None
        self.made, self.took = {}, {}

    def up(self, sem):
        self.made[sem] = self.made.get(sem, 0) + 1
        self.latest = sem
        return sem, 1

    def up16(self, sem):
        self.made[sem] = self.made.get(sem, 0) + 16
        self.latest = sem
        return sem, 16

    def used(self, sem):
        return sem, self.book.base.get(sem, 0) + self.took[sem]

    def skip(self, sem, k):
        self.took[sem] = self.took.get(sem, 0) + k

    def last(self):
        return self.latest, self.book.base.get(self.latest, 0) + self.made[self.latest]

    def need(self, sem, k=1):
        self.took[sem] = self.took.get(sem, 0) + k
        return sem, self.book.base.get(sem, 0) + self.took[sem]

    def again(self, sem):
        n = self.took.get(sem, 0)
        self.took[sem] = n + 1
        if isinstance(n, int) and n == 0:
            return []
        return [(sem, self.book.base.get(sem, 0) + n)]

    def loop(self, e, n, body):
        made, took, latest = dict(self.made), dict(self.took), self.latest
        body(Dry(), 0)
        dm = {s: v - made.get(s, 0) for s, v in self.made.items()}
        dt = {s: v - took.get(s, 0) for s, v in self.took.items()}

        def at(start, step, i):
            return {s: start.get(s, 0) + (i * step[s] if step[s] else 0) for s in step}
        self.latest = latest
        with e.Fori(0, n) as i:
            self.made, self.took = at(made, dm, i), at(took, dt, i)
            body(e, i)
        self.made, self.took = at(made, dm, n), at(took, dt, n)


class Book:

    def __init__(self, nc, ctx):
        self.nc, self.ctx, self.base, self.sems = nc, ctx, {}, {}
        self.engines = [Engine(self, n) for n in ("pe", "act", "dve", "pool", "sp")]

    def sem(self, name):
        if name not in self.sems:
            self.sems[name] = self.ctx.enter_context(self.nc.semaphore(name))
        return self.sems[name]

    def phase(self):
        for g in self.engines:
            for s, n in g.made.items():
                self.base[s] = self.base.get(s, 0) + n
            g.made, g.took, g.latest = {}, {}, None


def program(nc, A, out, plan, vat, cat):
    ctx = ExitStack()
    with ctx:
        book = Book(nc, ctx)
        PE, AC, VE, GP, SP = book.engines
        sem = book.sem

        def fixed(name, shape, dt=F32):
            return ctx.enter_context(nc.sbuf_tensor(name, shape, dt))

        wraw = fixed("wraw", [P, RAW, BLK])
        whi, wlo = fixed("whi", [P, SPL, BLK], F32R), fixed("wlo", [P, SPL, BLK], F32R)
        vec = fixed("vec_sb", [P, A["vec"].shape[1]])
        con = fixed("con_sb", [P, A["con"].shape[1]])
        started = fixed("started", [P, len(LAGGED)])
        cact = fixed("cact", [P, KT])
        cact3 = fixed("cact3", [P, KT, 3])
        mod = [fixed(f"mod{i}", [P, 48]) for i in range(2)]
        kvm = fixed("kvm", [P, 16])
        ada0 = fixed("ada0", [P, 2, 24])
        ada1 = fixed("ada1", [P, 24])
        coef = fixed("coef", [P, 8, KT])
        NT = nc.sbuf_bytes_remaining // 2048
        fence = nc.sbuf_base
        fixed("arena", [P, NT, T])
        off0 = (fence + 31) // 32 * 32
        named = {}

        def tiles(name, at, n=None, dt=F32, shape=None):
            shape = shape or [P, n, T]
            words = int(np.prod(shape[1:]))
            assert at * T + words <= NT * T, (name, at, words, NT)
            if name not in named:
                named[name] = nc.alloc_sbuf_tensor_at(name, shape, dt, offset=off0 + at * 2048)
            return named[name]

        ps = ctx.enter_context(nc.psum_tensor("ps", [P, 8, 512], F32))

        def V(name, i=None, n=1):
            at, width = vat[name]
            return vec[:, at:at + width] if i is None else vec[:, at + i:at + i + n]

        def C(name):
            at, width = cat[name]
            return con[:, at:at + width]

        ident, ones, head = C("ident"), C("ones"), C("head")

        raws = [kind for kind, _, n in plan for _ in range(n)]
        seqno, firsts, n_split, n_raw = [], {}, 0, 0
        for kind, name, n in plan:
            firsts[name] = (len(seqno), n_split if kind == "split" else n_raw)
            for _ in range(n):
                if kind == "split":
                    seqno.append(n_split)
                    n_split += 1
                else:
                    seqno.append(n_raw)
                    n_raw += 1
        split_at = [r for r, k in enumerate(raws) if k == "split"]
        firsts_raw = {m: f[0] for m, f in firsts.items()}
        w_full = [sem(f"w_loaded{s}") for s in range(RAW)]
        w_split, w_used, w_cond = sem("w_split"), sem("w_used"), sem("w_cond_used")
        sent = {"dma": 0, "pool": 0, "q": 0}

        def settle(e):
            e.nop(nofuse=True)

        def load_weights(sp, upto):
            upto = min(upto, len(raws))
            while sent["dma"] < upto:
                r = sent["dma"]
                if r < RAW:
                    sp.dma_start(wraw[:, r], A["wst"][r]).then_inc(w_full[r], 16)
                    sent["dma"] += 1
                    continue
                n = 1
                while r + n < upto and raws[r + n - RAW] == raws[r - RAW]:
                    n += 1
                free = w_split if raws[r - RAW] == "split" else w_cond
                turns, c0 = n // 2, seqno[r - RAW] + 1

                def one(k, i):
                    sp.wait_ge(free, c0 + k + 2 * i)
                    sp.dma_start(wraw[:, (r + k) % RAW], A["wst"][ds(r + k + 2 * i, 1)].rearrange(
                        "a p c -> (a p) c")).then_inc(w_full[(r + k) % RAW], 16)
                if turns > 1:
                    with sp.Fori(0, turns) as i:
                        one(0, i)
                        one(1, i)
                    rest = range(2 * turns, n)
                else:
                    rest = range(n)
                for k in rest:
                    one(k, 0)
                sent["dma"] += n

        def split_weights(pool, upto):
            upto = min(upto, n_split)
            while sent["pool"] < upto:
                q = sent["pool"]
                r = split_at[q]
                n = 1
                while q + n < upto and split_at[q + n] == r + n:
                    n += 1
                if q < SPL:
                    n = 1

                def one(k, i):
                    s, f = (q + k) % SPL, (r + k) % RAW
                    if q >= SPL:
                        pool.wait_ge(w_used, q + k + 2 * i)
                    pool.wait_ge(w_full[f], ((r + k) // 2 + 1 + i) * 16)
                    pool.tensor_tensor(whi[:, s], wraw[:, f], C("zero").broadcast_to([P, BLK]), ALU.add).then_inc(sem("w_high"), 1)
                    pool.wait_ge(sem("w_high"), q + k + 1 + 2 * i)
                    pool.tensor_tensor(wlo[:, s], wraw[:, f], whi[:, s].bitcast(F32),
                                       ALU.subtract).then_inc(w_split, 1)
                turns = n // 2
                if turns > 1:
                    with pool.Fori(0, turns) as i:
                        one(0, i)
                        one(1, i)
                    rest = range(2 * turns, n)
                else:
                    rest = range(n)
                for k in rest:
                    one(k, 0)
                sent["pool"] += n

        def ahead(*names):
            raw_end = max(firsts_raw[m] + c for _, m, c in plan if m in names)
            q_end = sum(1 for r in split_at if r < raw_end)
            if q_end < n_split and split_at[q_end] == raw_end:
                return raw_end + 3, q_end + 1
            return raw_end + 2, q_end

        acc_ready = sem("acc_ready")
        acc_free = [sem(f"acc_free{b}") for b in range(NACC)]
        turn = {"acc": 0}

        def block_of(e, q, i, xhi, xlo, nk, width, tokens=((0, T),), k0=0, first=True, final=True, m0=0, mn=None,
                     open_bank=None, tell=True, bank_free=None):
            s = q % SPL
            wh = whi[:, s, :nk * width].rearrange("p (k c) -> p k c", k=nk)
            wl = wlo[:, s, :nk * width].rearrange("p (k c) -> p k c", k=nk)
            e.wait_ge(w_split, q + i + 1)
            told = not tell
            for m in range(width // P if mn is None else mn):
                for a, (t0, nt) in enumerate(tokens):
                    if open_bank is None or first:
                        b = turn["acc"] % NACC
                        turn["acc"] += 1
                        for w in (bank_free() if bank_free else PE.again(acc_free[b])):
                            e.wait_ge(*w)
                        if open_bank is not None:
                            open_bank[m] = b
                    else:
                        b = open_bank[m]
                    mc = slice((m0 + m) * P, (m0 + m + 1) * P)
                    for k in range(nk):
                        passes = ((wh, xhi), (wh, xlo), (wl, xhi))
                        for j, (w, x) in enumerate(passes):
                            o = e.matmul(ps[:, b, :nt], w[:, k, mc], x[:, k0 + k, t0:t0 + nt],
                                         start=first and k == 0 and j == 0,
                                         stop=final and k == nk - 1 and j == 2)
                            if not told:
                                o.then_inc(w_used, 1)
                                told = True
                    if final:
                        o.then_inc(*PE.up(acc_ready))

        def tokens_of(e, q, i, xhi, xlo, nk=8, width=256):
            s = q % SPL
            wh = whi[:, s, :nk * width].rearrange("p (k c) -> p k c", k=nk)
            wl = wlo[:, s, :nk * width].rearrange("p (k c) -> p k c", k=nk)
            e.wait_ge(w_split, q + i + 1)
            for t in range(T // P):
                b = turn["acc"] % NACC
                turn["acc"] += 1
                for w in PE.again(acc_free[b]):
                    e.wait_ge(*w)
                tc = slice(t * P, (t + 1) * P)
                for k in range(nk):
                    for j, (w, x) in enumerate(((wh, xhi), (wl, xhi), (wh, xlo))):
                        o = e.matmul(ps[:, b, :width], x[:, k, tc], w[:, k, :], start=k == 0 and j == 0,
                                     stop=k == nk - 1 and j == 2)
                        if t == 0 and k == 0 and j == 0:
                            o.then_inc(w_used, 1)
                o.then_inc(*PE.up(acc_ready))

        def phase_start():
            book.phase()
            turn["acc"] = 0
            turn["evac"] = 0

        def bank():
            b = turn["evac"] % NACC
            turn["evac"] += 1
            return b

        sq, rms, nt = (tiles(n, 24 + 2 * j, 2) for j, n in enumerate(("sq", "rms", "nt")))
        hh, hl = tiles("hh", 8, KT, F32R), tiles("hl", 16, KT, F32R)

        def norm_pe(e, bank_no, n=T):
            e.wait_ge(*PE.need(sem("square_added"), KT - 1))
            e.matmul(ps[:, bank_no, :n], ones, rms[:, 1, :n], start=True, stop=True).then_inc(*PE.up(sem("square_sum")))

        def norm_act(e, src, bank_no, shift=None, n=T, hi=None):
            for k in range(KT):
                if k == 2 or k > 3:
                    e.wait_ge(*AC.need(sem("square_added")))
                e.activation(sq[:, k % 2, :n], src(k), ACT.Square).then_inc(*AC.up(sem("square")))
            e.wait_ge(*AC.need(sem("square_sum")))
            e.activation(rms[:, 0, :n], ps[:, bank_no, :n], ACT.Sqrt, bias=C("epsn"),
                         scale=1.0 / D).then_inc(*AC.up(sem("rms")))
            if hi is not None:
                for k in range(KT):
                    e.wait_ge(*AC.need(sem("scaled")))
                    e.activation(hi(k), nt[:, k % 2, :n], ACT.Identity,
                                 bias=shift(k)).then_inc(*AC.up(sem("rounded")))

        def norm_dve(e, src, gain, shift=None, n=T, hi=None, lo=None, plain=None):
            total = rms[:, 1, :n]
            e.wait_ge(*VE.need(sem("square")))
            for k in range(1, KT):
                e.wait_ge(*VE.need(sem("square")))
                e.tensor_tensor(total, sq[:, 0, :n] if k == 1 else total, sq[:, k % 2, :n],
                                ALU.add).then_inc(*VE.up(sem("square_added")))
                if k < KT - 1:
                    e.wait_ge(*VE.last())
            e.wait_ge(*VE.need(sem("rms")))
            e.reciprocal(rms[:, 1, :n], rms[:, 0, :n]).then_inc(*VE.up(sem("dve")))
            e.wait_ge(*VE.last())

            def low(k):
                e.wait_ge(*VE.need(sem("rounded")))
                e.scalar_tensor_tensor(lo(k), nt[:, k % 2, :n], shift(k), hi(k).bitcast(F32), ALU.add,
                                       ALU.subtract).then_inc(*VE.up(sem("x_ready")))
            for k in range(KT):
                if k >= 2 and not plain:
                    e.wait_ge(*VE.last())
                to = plain(k) if plain and shift is None else nt[:, k % 2, :n]
                o = e.scalar_tensor_tensor(to, src(k), gain(k), rms[:, 1, :n], ALU.mult, ALU.mult)
                if not plain:
                    o.then_inc(*VE.up(sem("scaled")))
                    if k:
                        low(k - 1)
                elif shift is None:
                    o.then_inc(*VE.up(sem("x_ready")))
                else:
                    o.then_inc(*VE.up(sem("dve")))
                    e.wait_ge(*VE.last())
                    e.tensor_scalar(plain(k), nt[:, k % 2, :n], shift(k), None,
                                    ALU.add).then_inc(*VE.up(sem("x_ready")))
                    e.wait_ge(*VE.last())
            if not plain:
                low(KT - 1)

        def cond_blocks(e, name, rhs, w, dst):
            r0, c0 = firsts[name]
            n = [c for _, m, c in plan if m == name][0]

            def two(i):
                for k in range(2):
                    e.wait_ge(w_full[(r0 + k) % RAW], ((r0 + k) // 2 + 1 + i) * 16)
                    slot = wraw[:, (r0 + k) % RAW].rearrange("p (k c) -> p k c", k=KT)
                    for m in range(2):
                        for t in range(KT):
                            o = e.matmul(dst[:, ds(i * 4 * w + (2 * k + m) * w, w)],
                                         slot[:, t, m * P:(m + 1) * P], rhs[:, t, :],
                                         start=t == 0, stop=t == KT - 1)
                    o.then_inc(w_cond, 1)
            with e.Fori(0, n // 2) as i:
                two(i)

        def gains(e, j, g, scale):
            e.scalar_tensor_tensor(coef[:, j], scale, 1.0, g, ALU.add, ALU.mult).then_inc(*VE.up(sem("dve")))

        x_sb = tiles("x", 0, KT)
        phase_start()
        with nc.Block() as block:
            @block.sync
            def _(sp):
                sp.dma_start(vec[:], A["vec"]).then_inc(*SP.up16(sem("vec_loaded")))
                sp.dma_start(con[:], A["con"]).then_inc(*SP.up16(sem("con_loaded")))
                sp.dma_start(x_sb[:], A["xT"]).then_inc(*SP.up16(sem("x_loaded")))
                load_weights(sp, ahead("mod0")[0])
                sp.wait_ge(sem("vec_loaded"), 16)
                sp.wait_ge(sem("con_loaded"), 16)
                sp.wait_ge(sem("x_loaded"), 16)

            @block.gpsimd
            def _(pool):
                for k, name in enumerate(LAGGED):
                    pool.memset(started[:, k:k + 1], 0.0).then_inc(*GP.up(sem(name)))
                split_weights(pool, ahead("mod0")[1])

            @block.scalar
            def _(act):
                act.wait_ge(*AC.need(sem("vec_loaded"), 16))
                act.activation(cact[:], V("c"), ACT.Silu).then_inc(*AC.up(sem("cond")))
                act.activation(cact3[:].rearrange("p k c -> p (k c)"), V("c3"),
                               ACT.Silu).then_inc(*AC.up(sem("cond")))

            @block.tensor
            def _(pe):
                pe.wait_ge(*PE.need(sem("cond"), 2))
                cond_blocks(pe, "mod0", cact[:].rearrange("p (k c) -> p k c", c=1), 1, ps[:, 7, :])

            @block.vector
            def _(dve):
                dve.wait_ge(w_cond, firsts["mod0"][1] + 8)
                dve.wait_ge(*VE.need(sem("vec_loaded"), 16))
                dve.tensor_tensor(mod[0][:, :16], ps[:, 7, :16], V("modb0", 0, 16), ALU.add).then_inc(*VE.up(sem("dve")))
        hpad = tiles("hpad", 8, shape=[P, KT, T + 1])
        phase_start()
        with nc.Block() as block:
            @block.vector
            def _(dve):
                dve.memset(hpad[:, :, 0:1], 0.0).then_inc(*VE.up(sem("dve")))
                gains(dve, 0, V("nmix0"), mod[0][:, 8:16])
                norm_dve(dve, lambda k: x_sb[:, k], lambda k: coef[:, 0, k:k + 1], lambda k: mod[0][:, k:k + 1],
                         plain=lambda k: hpad[:, k, 1:])

            @block.scalar
            def _(act):
                norm_act(act, lambda k: x_sb[:, k], 7)

            @block.tensor
            def _(pe):
                norm_pe(pe, 7)

        mixh, mixl = tiles("mixh", 17, KT, F32R), tiles("mixl", 25, KT, F32R)
        dif, mix = tiles("dif", 0, 2), tiles("mix", 2, 2)
        sgh, sgl = tiles("sgh", 4, 2, F32R), tiles("sgl", 6, 2, F32R)
        w_sb, a_sb, r_sb, k_sb, v_sb = (tiles(n, 33 + 8 * j, KT) for j, n in enumerate(
            ("w_sb", "a_sb", "r_sb", "k_sb", "v_sb")))
        hidh, hidl = tiles("hidh", 49, 2, F32R), tiles("hidl", 51, 2, F32R)
        hid = tiles("hid", 53, 2)
        phase_start()
        with nc.Block() as block:
            names = ("w1", "a1", "w2a2", "g1", "wr", "wk", "wv")

            @block.sync
            def _(sp):
                load_weights(sp, ahead(*names)[0])

            @block.gpsimd
            def _(pool):
                split_weights(pool, ahead(*names)[1])

            @block.tensor
            def _(pe):
                def full(name, n, width, **kw):
                    for j in range(n):
                        block_of(pe, firsts[name][1] + j, 0, mixh, mixl, KT, width, **kw)
                pe.wait_ge(*PE.need(sem("mix_ready"), KT))
                full("w1", 1, P)
                pe.wait_ge(*PE.need(sem("mix_ready"), KT))
                full("a1", 1, P)
                for j in range(2):
                    pe.wait_ge(*PE.need(sem("hid_ready")))
                q = firsts["w2a2"][1]
                block_of(pe, q, 0, hidh, hidl, 1, BLK, mn=8)
                block_of(pe, q, 0, hidh, hidl, 1, BLK, mn=8, m0=8, k0=1, tell=False)
                pe.wait_ge(*PE.need(sem("mix_ready"), KT))
                full("g1", 1, 256)
                for name in ("wr", "wk", "wv"):
                    pe.wait_ge(*PE.need(sem("mix_ready"), KT))
                    full(name, 4, 256)

            @block.vector
            def _(dve):
                def mixing(j, done):
                    if done:
                        dve.wait_ge(*VE.need(acc_ready, done))
                    for k in range(KT + 1):
                        if k < KT:
                            dve.tensor_tensor(dif[:, k % 2], hpad[:, k, :T], hpad[:, k, 1:],
                                              ALU.subtract).then_inc(*VE.up(sem("dve")))
                            dve.wait_ge(*VE.last())
                            dve.scalar_tensor_tensor(mix[:, k % 2], dif[:, k % 2], V(f"mu{j}", k), hpad[:, k, 1:],
                                                     ALU.mult, ALU.add).then_inc(*VE.up(sem("mixed")))
                        if k:
                            dve.wait_ge(*VE.need(sem("mix_high")))
                            dve.tensor_tensor(mixl[:, k - 1], mix[:, (k - 1) % 2], mixh[:, k - 1].bitcast(F32),
                                              ALU.subtract).then_inc(*VE.up(sem("mix_ready")))

                def hidden_low(n, lo, hi):
                    dve.wait_ge(*VE.need(sem("hid_high")))
                    dve.tensor_tensor(lo, hid[:, n], hi.bitcast(F32), ALU.subtract).then_inc(*VE.up(sem("hid_ready")))
                mixing(1, 0)
                hidden_low(0, hidl[:, 0], hidh[:, 0])
                mixing(4, 1)
                hidden_low(1, hidl[:, 1], hidh[:, 1])
                mixing(5, 1)
                for n in range(2):
                    hidden_low(n, sgl[:, n], sgh[:, n])
                mixing(0, 16 + 2)
                mixing(2, 8)
                mixing(3, 8)

            @block.scalar
            def _(act):
                def high():
                    for k in range(KT):
                        act.wait_ge(*AC.need(sem("mixed")))
                        act.activation(mixh[:, k], mix[:, k % 2], ACT.Copy).then_inc(*AC.up(sem("mix_high")))

                def read_out(dst, func, bias=0.0):
                    b = bank()
                    act.wait_ge(*AC.need(acc_ready))
                    act.activation(dst, ps[:, b], func, bias=bias).then_inc(*AC.up(acc_free[b]))

                def hidden(n, func, hi):
                    read_out(hid[:, n], func)
                    act.wait_ge(*AC.last())
                    act.activation(hi, hid[:, n], ACT.Copy).then_inc(*AC.up(sem("hid_high")))
                high()
                hidden(0, ACT.Tanh, hidh[:, 0])
                high()
                hidden(1, ACT.Copy, hidh[:, 1])
                high()
                for k in range(KT):
                    read_out(w_sb[:, k], ACT.Sigmoid, V("w0", k))
                for k in range(KT):
                    read_out(a_sb[:, k], ACT.Sigmoid, V("a0", k))
                for n in range(2):
                    act.wait_ge(*AC.need(sem("hid_ready")))
                    hidden(n, ACT.Sigmoid, sgh[:, n])
                for to in (r_sb, k_sb, v_sb):
                    high()
                    for k in range(KT):
                        read_out(to[:, k], ACT.Copy)

        w = iter([0, 1, 2, 3] + list(range(8, 33)))

        def work(name, n=1, shape=None):
            at = [next(w) for _ in range(n)]
            assert at[-1] - at[0] == n - 1
            return tiles(name, at[0], n, shape=shape or [P, 4, P])
        t1, t2, t3, t4 = (work(f"t{j}", shape=[P, T]) for j in range(1, 5))
        ar = work("ar", 2, [P, 4, 2, P])
        abrb = work("abrb", 2, [P, 4, 2, P])
        akrk = work("akrk", 2, [P, 4, 2, P])
        xav = work("xav", 2, [P, 4, 2, P])
        fg = work("fg", 2, [P, 4, 2, P])
        bb, kb, bt, kt, vt, ad, adt, aot, pt, a2, a2t = (work(n) for n in (
            "bb", "kb", "bt", "kt", "vt", "ad", "adt", "aot", "pt", "a2", "a2t"))
        kkn, wc, yt = (work(n, shape=[P, T]) for n in ("kkn", "wc", "yt"))
        st = work("st", shape=[P, 2, P])
        pv = fixed("pv", [P, 5])
        to_act, to_dve, ev_a, ev_v = sem("mat_for_act"), sem("mat_for_dve"), sem("mat_by_act"), sem("mat_by_dve")
        vs = tiles("vs", 73, shape=[P, 4, 2, CH])
        WKV_STEPS = ("GB", "GA", "BT", "GK", "AT", "KT", "VT", "A2", "A2T", "AV", "P2", "A4", "A4T", "P3", "A8", "P4",
                     "TD", "M", "MT", "Q", "M2", "T", "FG", "PHI", "E")
        WKV_DVE_STEPS = ("GB", "GA", "GK", "VT", "P2", "P3", "P4", "Q", "T", "PHI", "E")
        WKV_ACT = 2 * (2 * (len(WKV_STEPS) - len(WKV_DVE_STEPS)) + 1) + 2
        WKV_DVE = 2 * (2 * len(WKV_DVE_STEPS) + 4) + 2
        wkv_order = ["norm", "bonus"]
        for half in range(2):
            wkv_order += [(n, half, g) for n in WKV_STEPS for g in range(2)] + [("Y", half)]
            wkv_order += [("S", half, c) for c in range(4)]
        wkv_order += ["mean", "var"]
        wkv_bank = {n: j % 7 for j, n in enumerate(wkv_order)}
        phase_start()

        def tile_of(buf, i):
            return buf[:, ds(i, 1)].rearrange("p a t -> p (a t)")

        def chunks(ap):
            return ap.rearrange("p (c t) -> p c t", t=CH)

        with nc.Block() as block:
            @block.sync
            def _(sp):
                load_weights(sp, ahead("ada1")[0])

            @block.gpsimd
            def _(pool):
                split_weights(pool, ahead("ada1")[1])

            @block.tensor
            def _(pe):
                n_act, n_dve = WKV_ACT, WKV_DVE

                def turn_of(e, i, conditions=10):
                    ready, last, made = {}, {}, {"a": 0, "v": 0}
                    seen, wanted = {"a": 0, "v": 0}, []

                    def wait_for_wanted():
                        for to, s, tot in (("a", ev_a, n_act), ("v", ev_v, n_dve)):
                            latest = max([n for t, n in wanted if t == to] + [0])
                            if latest > seen[to]:
                                e.wait_ge(s, book.base.get(s, 0) + i * tot + latest)
                                seen[to] = latest
                        wanted.clear()

                    if not isinstance(i, int) or i:
                        e.wait_ge(ev_a, book.base.get(ev_a, 0) + i * n_act)
                        e.wait_ge(ev_v, book.base.get(ev_v, 0) + i * n_dve)

                    def unit(name, to, products, n=256, transpose=False):
                        b = wkv_bank[name]
                        if b in last:
                            wanted.append(last[b])
                        wait_for_wanted()
                        o = products(b)
                        made[to] += 1
                        ready[name] = last[b] = (to, made[to])
                        o.then_inc(*PE.up(to_act if to == "a" else to_dve))

                    def mats(name, to, g, out, *terms, after=()):
                        for a in after:
                            wanted.append(ready[a, half, g])

                        def go(b):
                            for c in range(2):
                                for j, (l, r) in enumerate(terms):
                                    rhs = r(2 * g + c)
                                    cw = out // 2
                                    o = e.matmul(ps[:, b, c * cw:(c + 1) * cw], l(2 * g + c), rhs,
                                                 start=j == 0, stop=j == len(terms) - 1)
                            return o
                        unit((name, half, g), to, go)

                    def turned(name, to, g, src, after=()):
                        for a in after:
                            wanted.append(ready[a, half, g])

                        def go(b):
                            for c in range(2):
                                o = e.transpose(ps[:, b, c * P:(c + 1) * P], src(2 * g + c), ident)
                            return o
                        unit((name, half, g), to, go)

                    taken = [0]

                    def cond_block():
                        if taken[0] == conditions:
                            return
                        k, r0 = taken[0], firsts_raw["mod0b"]
                        taken[0] += 1
                        e.wait_ge(w_full[(r0 + k) % RAW], ((r0 + k) // 2 + 1 + 5 * i) * 16)
                        slot = wraw[:, (r0 + k) % RAW].rearrange("p (k c) -> p k c", k=KT)
                        for j in range(2):
                            for t in range(KT):
                                o = e.matmul(ps[:, 7, ds(i * 60 + (2 * k + j) * 3, 3)],
                                             slot[:, t, j * P:(j + 1) * P], cact3[:, t],
                                             start=t == 0, stop=t == KT - 1)
                        o.then_inc(w_cond, 1)

                    def headsum(name, to, src):
                        unit(name, to, lambda b: e.matmul(ps[:, b], head, src[:], start=True, stop=True))

                    e.wait_ge(*PE.need(sem("kk_squared")))
                    headsum("norm", "a", t1)
                    e.wait_ge(*PE.need(sem("rk_ready")))
                    headsum("bonus", "v", t2)

                    def m(buf, part=None):
                        return (lambda c: buf[:, c]) if part is None else (lambda c: buf[:, c, part])
                    for half in range(2):
                        e.wait_ge(*PE.need(sem("bd_ready")))

                        def arw(c):
                            return ar[:, c].rearrange("p a t -> p (a t)")

                        def vdup(c):
                            return vs[:, c].rearrange("p a t -> p (a t)")
                        G = range(2)
                        for g in G:
                            mats("GB", "v", g, 512, (m(bb), arw))
                        for g in G:
                            mats("GA", "v", g, 256, (m(ar, 0), m(bb)))
                        for g in G:
                            turned("BT", "a", g, m(bb))
                        for g in G:
                            mats("GK", "v", g, 512, (m(kb), arw))
                        for g in G:
                            turned("AT", "a", g, m(ar, 0))
                        for g in G:
                            turned("KT", "a", g, m(kb))
                        e.wait_ge(*PE.need(sem("v_twice")))
                        for g in G:
                            turned("VT", "v", g, vdup)
                        for g in G:
                            mats("A2", "a", g, 256, (m(adt), m(ad)), after=("GB", "GA"))
                        for g in G:
                            mats("A2T", "a", g, 256, (m(ad), m(adt)))
                        for g in G:
                            mats("AV", "a", g, 256, (m(akrk, 0), m(vt)), after=("GK", "VT"))
                        cond_block()
                        for g in G:
                            mats("P2", "v", g, 256, (m(a2), m(pt)), after=("A2",))
                        for g in G:
                            mats("A4", "a", g, 256, (m(a2t), m(a2)), after=("A2T",))
                        for g in G:
                            mats("A4T", "a", g, 256, (m(a2), m(a2t)))
                        cond_block()
                        for g in G:
                            mats("P3", "v", g, 256, (m(ad), m(pt)), after=("A4", "P2"))
                        for g in G:
                            mats("A8", "a", g, 256, (m(adt), m(ad)), after=("A4T",))
                        for g in G:
                            mats("P4", "v", g, 256, (m(a2), m(pt)), after=("A8", "P3"))
                        cond_block()
                        for g in G:
                            turned("TD", "a", g, m(pt), after=("P4",))
                        for g in G:
                            mats("M", "a", g, 256, (m(aot), m(a2t)), after=("TD",))
                        for g in G:
                            mats("MT", "a", g, 256, (m(a2t), m(aot)))
                        cond_block()
                        for g in G:
                            mats("Q", "v", g, 256, (m(ad), m(pt)), after=("M",))
                        for g in G:
                            mats("M2", "a", g, 256, (m(adt), m(ad)), after=("MT",))
                        for g in G:
                            mats("T", "v", g, 256, (m(a2), m(pt)), after=("M2", "Q"))
                        cond_block()
                        for g in G:
                            mats("FG", "a", g, 512, (m(pt), lambda c: xav[:, c].rearrange("p a t -> p (a t)")),
                                 after=("T", "AV", "AT"))
                        for g in G:
                            mats("PHI", "v", g, 256, (m(fg, 0), m(bt)), after=("FG", "BT"))
                        for g in G:
                            mats("E", "v", g, 256, (m(fg, 0), m(abrb, 1)))
                        yb = wkv_bank["Y", half]
                        if yb in last:
                            wanted.append(last[yb])
                        for g in G:
                            for name in ("KT", "PHI", "E"):
                                wanted.append(ready[name, half, g])
                        for c in range(4):
                            old = st[:, c % 2]
                            if c or half:
                                wanted.append(ready["S", half if c else half - 1, c - 1 if c else 3])

                            def state(b):
                                e.matmul(ps[:, b, :P], bt[:, c], fg[:, c, 1], start=True, stop=False)
                                e.matmul(ps[:, b, :P], kt[:, c], vt[:, c], start=False, stop=False)
                                return e.matmul(ps[:, b, :P], ad[:, c], old, start=False, stop=True)
                            unit(("S", half, c), "v", state)
                            yc = ps[:, yb, c * P:(c + 1) * P]
                            e.matmul(yc, fg[:, c, 1], abrb[:, c, 1], start=True, stop=False)
                            e.matmul(yc, vt[:, c], akrk[:, c, 1], start=False, stop=False)
                            o = e.matmul(yc, old, adt[:, c], start=False, stop=True)
                        o.then_inc(*PE.up(to_act))
                        made["a"] += 1
                        last[yb] = ("a", made["a"])
                    wanted.append(last[yb])
                    headsum("mean", "v", yt)
                    e.wait_ge(*PE.need(sem("y_squared")))
                    headsum("var", "a", t1)
                    assert made == {"a": n_act, "v": n_dve}, made

                PE.loop(pe, KT - 1, turn_of)
                turn_of(pe, KT - 1, conditions=2)

            @block.scalar
            def _(act):
                def copy(e, to, bank_no, n=256, func=ACT.Copy, own=ev_a, **kw):
                    e.wait_ge(*AC.need(to_act))
                    e.activation(to, ps[:, bank_no, :n], func, **kw).then_inc(*AC.up(own))

                def turn_of(e, i):
                    b = wkv_bank
                    e.wait_ge(*AC.need(sem("kr_ready")))
                    e.activation(t1[:], kkn[:], ACT.Square).then_inc(*AC.up(sem("kk_squared")))
                    copy(e, t1[:], b["norm"], T, ACT.Sqrt)
                    e.wait_ge(*AC.need(sem("cum_ready")))
                    e.activation(wc[:], t4[:], ACT.Exp).then_inc(*AC.up(sem("exp")))
                    e.activation(t4[:], t4[:], ACT.Exp, scale=-1.0).then_inc(*AC.up(sem("exp")))
                    e.activation(t3[:], t3[:], ACT.Exp).then_inc(*AC.up(sem("exp")))
                    for half in range(2):
                        for a in range(2):
                            o = e.activation(vs[:, :, a], chunks(v_sb[:, ds(i, 1), half * 256:half * 256 + 256].rearrange(
                                "p a t -> p (a t)")), ACT.Copy)
                        o.then_inc(*AC.up(sem("v_twice")))
                        for name, to in (("BT", bt), ("AT", xav), ("KT", kt), ("A2", a2), ("A2T", a2t), ("AV", xav),
                                         ("A4", ad), ("A4T", adt), ("A8", a2), ("TD", a2t), ("M", ad), ("MT", adt),
                                         ("M2", a2), ("FG", fg)):
                            for g in range(2):
                                cc = slice(2 * g, 2 * g + 2)
                                n = 512 if name == "FG" else 256
                                if name == "FG":
                                    dst = to[:, cc].rearrange("p c a t -> p (c a t)")
                                elif name == "AT":
                                    dst = to[:, cc, 0]
                                elif name == "AV":
                                    dst = to[:, cc, 1]
                                else:
                                    dst = to[:, cc].rearrange("p c t -> p (c t)")
                                src = ps[:, b[name, half, g], :n]
                                if name in ("AT", "AV"):
                                    src = src.rearrange("p (c t) -> p c t", c=2)
                                e.wait_ge(*AC.need(to_act))
                                e.activation(dst, src, ACT.Copy).then_inc(*AC.up(ev_a))
                        e.wait_ge(*AC.need(to_act))
                        for h in range(2):
                            o = e.activation(chunks(yt[64 * h:64 * h + 64, half * 256:(half + 1) * 256]),
                                             ps[64 * h:64 * h + 64, b["Y", half]].rearrange(
                                                 "p (c t) -> p c t", c=4)[:, :, 64 * h:64 * h + 64], ACT.Copy)
                        o.then_inc(*AC.up(ev_a))
                    e.wait_ge(ev_v, book.base.get(ev_v, 0) + i * WKV_DVE + WKV_DVE)
                    e.activation(t1[:], yt[:], ACT.Square).then_inc(*AC.up(sem("y_squared")))
                    copy(e, t2[:], b["var"], T, ACT.Sqrt, bias=C("epsg"), scale=1.0 / 64)
                AC.loop(act, KT, turn_of)

            @block.vector
            def _(dve):
                chain = sem("dve")
                for buf in (ar[:], bb[:], kb[:]):
                    dve.memset(buf, 0.0).then_inc(*VE.up(chain))

                def turn_of(e, i):
                    b = wkv_bank
                    kx, rx, vx, wx, ax = (tile_of(z, i) for z in (k_sb, r_sb, v_sb, w_sb, a_sb))

                    def step(o, s=chain):
                        o.then_inc(*VE.up(s))
                        e.wait_ge(*VE.last())

                    def taken(o):
                        o.then_inc(*VE.up(ev_v))
                    at = vat["pair"][0]
                    step(e.tensor_copy(pv[:], vec[:, ds(i * 5 + at, 5)]))
                    e.memset(st[:, 0], 0.0).then_inc(*VE.up(chain))
                    e.tensor_scalar(kkn[:], kx, pv[:, 0:1], None, ALU.mult).then_inc(*VE.up(sem("kr_ready")))
                    e.tensor_scalar(t3[:], wx, -HALF, None, ALU.mult).then_inc(*VE.up(chain))
                    step(e.tensor_scalar(t2[:], ax, -1.0, pv[:, 1:2], ALU.add, ALU.mult))
                    e.tensor_tensor_scan(t4[:], C("keep"), t3[:], 0.0, ALU.mult, ALU.add).then_inc(*VE.up(chain))
                    step(e.scalar_tensor_tensor(kx, t2[:], 1.0, kx, ALU.add, ALU.mult))
                    e.tensor_tensor(t3[:], t4[:], t3[:], ALU.subtract).then_inc(*VE.up(sem("cum_ready")))
                    e.scalar_tensor_tensor(t2[:], rx, pv[:, 2:3], kx, ALU.mult,
                                           ALU.mult).then_inc(*VE.up(sem("rk_ready")))
                    e.wait_ge(ev_a, book.base.get(ev_a, 0) + i * WKV_ACT + 1)
                    step(e.tensor_scalar(t1[:], t1[:], 1e-12, None, ALU.max))
                    step(e.reciprocal(t1[:], t1[:]))
                    step(e.tensor_tensor(kkn[:], kkn[:], t1[:], ALU.mult))
                    step(e.tensor_tensor(ax, kkn[:], ax, ALU.mult))
                    e.wait_ge(*VE.need(to_dve))
                    taken(e.tensor_tensor(wx, ps[:, b["bonus"]], vx, ALU.mult))
                    e.wait_ge(*VE.need(sem("exp"), 3))
                    for half in range(2):
                        for h in range(2):
                            rr, tc = slice(64 * h, 64 * h + 64), slice(256 * half, 256 * half + 256)

                            def part(z):
                                return chunks(z[rr, tc])
                            e.scalar_tensor_tensor(ar[rr, :, 0, rr], part(kkn[:]), -1.0, part(t3[:]), ALU.mult,
                                                   ALU.mult)
                            e.tensor_tensor(ar[rr, :, 1, rr], part(rx), part(wc[:]), ALU.mult)
                            e.tensor_tensor(bb[rr, :, rr], part(ax), part(t4[:]), ALU.mult)
                            o = e.tensor_tensor(kb[rr, :, rr], part(kx), part(t4[:]), ALU.mult)
                        o.then_inc(*VE.up(sem("bd_ready")))

                        def cc(g):
                            return slice(2 * g, 2 * g + 2)

                        def src(name, g, n=256):
                            return ps[:, b[name, half, g], :n]

                        def bc(z, k, n):
                            return z.rearrange("p (a n) -> p a n", a=1).broadcast_to([P, k, n])

                        def add(name, g, to, other):
                            e.wait_ge(*VE.need(to_dve))
                            taken(e.tensor_tensor(to[:, cc(g)], src(name, g).rearrange("p (c t) -> p c t", c=2),
                                                  other, ALU.add))

                        def masked(name, g, to, mask):
                            e.wait_ge(*VE.need(to_dve))
                            return e.tensor_tensor(to, src(name, g).rearrange("p (c t) -> p c t", c=2), mask, ALU.mult)
                        for g in range(2):
                            e.wait_ge(*VE.need(to_dve))
                            step(e.tensor_tensor(abrb[:, cc(g)].rearrange("p c a t -> p c (a t)"),
                                                 src("GB", g, 512).rearrange("p (c t) -> p c t", c=2),
                                                 bc(C("mrec"), 2, 256), ALU.mult))
                            step(e.tensor_tensor(adt[:, cc(g)], abrb[:, cc(g), 0], bc(C("m16"), 2, P), ALU.mult))
                            e.tensor_tensor(aot[:, cc(g)], abrb[:, cc(g), 0], adt[:, cc(g)], ALU.subtract)
                            taken(e.tensor_tensor(pt[:, cc(g)], adt[:, cc(g)], bc(ident, 2, P), ALU.add))
                        for g in range(2):
                            taken(masked("GA", g, ad[:, cc(g)], bc(C("mlow16"), 2, P)))
                        for g in range(2):
                            e.wait_ge(*VE.need(to_dve))
                            taken(e.tensor_tensor(akrk[:, cc(g)].rearrange("p c a t -> p c (a t)"),
                                                  src("GK", g, 512).rearrange("p (c t) -> p c t", c=2),
                                                  bc(C("mrec"), 2, 256), ALU.mult))
                        for g in range(2):
                            taken(masked("VT", g, vt[:, cc(g)], bc(head, 2, P)))
                        for name in ("P2", "P3", "P4", "Q", "T"):
                            for g in range(2):
                                add(name, g, pt, pt[:, cc(g)])
                        for g in range(2):
                            add("PHI", g, ad, bc(ident, 2, P))
                        for g in range(2):
                            add("E", g, adt, ar[:, cc(g), 1])
                        for c in range(4):
                            e.wait_ge(*VE.need(to_dve))
                            tl = (4 * half + c) * CH + CH - 1
                            taken(e.tensor_scalar(st[:, (c + 1) % 2], ps[:, b["S", half, c], :P], wc[:, tl:tl + 1],
                                                  None, ALU.mult))
                    e.wait_ge(*VE.need(to_dve))
                    e.scalar_tensor_tensor(yt[:], ps[:, b["mean"]], -1.0 / 64, yt[:], ALU.mult,
                                           ALU.add).then_inc(*VE.up(ev_v))
                    e.wait_ge(*VE.last())
                    e.wait_ge(ev_a, book.base.get(ev_a, 0) + i * WKV_ACT + WKV_ACT)
                    step(e.reciprocal(t2[:], t2[:]))
                    step(e.tensor_tensor(yt[:], yt[:], t2[:], ALU.mult))
                    step(e.tensor_scalar(yt[:], yt[:], pv[:, 3:4], pv[:, 4:5], ALU.mult, ALU.add))
                    step(e.tensor_tensor(rx, yt[:], wx, ALU.add))
                VE.loop(dve, KT, turn_of)

        def linear(e, name, xhi, xlo, part=(0, None), nk=8, width=256, **kw):
            n = [c for _, m, c in plan if m == name][0]
            lo, hi = part[0], part[1] or n
            q = firsts[name][1] + lo
            if hi - lo <= 2:
                for j in range(hi - lo):
                    block_of(e, q + j, 0, xhi, xlo, nk, width, **kw)
                return

            def two(f, i):
                for j in range(2):
                    block_of(f, q + j, 2 * i, xhi, xlo, nk, width, **kw)
            PE.loop(e, (hi - lo) // 2, two)

        def one_of(buf, i):
            return buf[:, ds(i, 1)].rearrange("p a t -> p (a t)")

        def add_to_x(e, gate, n=KT):
            def four(f, i):
                for j in range(4):
                    b = bank()
                    f.wait_ge(*VE.need(acc_ready))
                    xt = one_of(x_sb, 4 * i + j)
                    f.scalar_tensor_tensor(xt, ps[:, b], gate(4 * i + j), xt, ALU.mult,
                                           ALU.add).then_inc(*VE.up(acc_free[b]))
            VE.loop(e, n // 4, four)

        phase_start()
        yg = tiles("yg", 24, 2)
        with nc.Block() as block:
            names = ("g2", "wo")

            @block.sync
            def _(sp):
                load_weights(sp, ahead(*names)[0])

            @block.gpsimd
            def _(pool):
                split_weights(pool, ahead(*names)[1])

            @block.tensor
            def _(pe):
                block_of(pe, firsts["g2"][1], 0, sgh, sgl, 2, D)
                pe.wait_ge(*PE.need(sem("x_ready"), KT))
                linear(pe, "wo", hh, hl)

            @block.scalar
            def _(act):
                for k in range(KT):
                    act.wait_ge(*AC.need(acc_free[k % NACC]))
                    act.activation(hh[:, k], yg[:, k % 2], ACT.Copy).then_inc(*AC.up(sem("rounded")))
                act.dma_start(x_sb[:], A["xT"]).then_inc(*AC.up16(sem("x_again")))

            @block.vector
            def _(dve):
                for k in range(KT + 1):
                    if k < KT:
                        b = bank()
                        if k >= 2:
                            dve.wait_ge(*VE.last())
                        dve.wait_ge(*VE.need(acc_ready))
                        dve.tensor_tensor(yg[:, k % 2], ps[:, b], r_sb[:, k], ALU.mult).then_inc(*VE.up(acc_free[b]))
                    if k:
                        dve.wait_ge(*VE.need(sem("rounded")))
                        dve.tensor_tensor(hl[:, k - 1], yg[:, (k - 1) % 2], hh[:, k - 1].bitcast(F32),
                                          ALU.subtract).then_inc(*VE.up(sem("x_ready")))
                chain = sem("dve")
                cp = ps[:, 7, :432].rearrange("p (j c) -> p c j", c=3)
                for to, src, bias in ((mod[0][:, 16:], cp[:, 0, 0:32], V("modb0", 16, 32)),
                                      (mod[1][:], cp[:, 0, 32:80], V("modb1")), (kvm[:], cp[:, 0, 80:96], V("kvmb")),
                                      (ada0[:, 0], cp[:, 1, 96:120], V("adab0")), (ada0[:, 1], cp[:, 2, 96:120], V("adab0")),
                                      (ada1[:], cp[:, 1, 120:144], V("adab1"))):
                    dve.tensor_tensor(to, src, bias, ALU.add).then_inc(*VE.up(chain))
                dve.wait_ge(*VE.last())
                for i in range(2):
                    for c in (16, 40):
                        dve.tensor_scalar(mod[i][:, c:c + 8], mod[i][:, c:c + 8], 1.0, None,
                                          ALU.add).then_inc(*VE.up(chain))
                for j, g, sc in ((1, "nmlp0", mod[0][:, 32:40]), (2, "nmix1", mod[1][:, 8:16]),
                                 (3, "nmlp1", mod[1][:, 32:40]), (4, "kvn", kvm[:, 8:16]), (5, "n20", ada0[:, 0, 8:16]),
                                 (6, "n20", ada0[:, 1, 8:16]), (7, "n21", ada1[:, 8:16])):
                    gains(dve, j, V(g), sc)
                dve.wait_ge(*VE.last())
                dve.wait_ge(*VE.need(sem("x_again"), 16))
                add_to_x(dve, lambda m: mod[0][:, ds(16 + m, 1)])

        def norm_phase(gain_no, shift, names=()):
            phase_start()
            with nc.Block() as block:
                @block.vector
                def _(dve):
                    norm_dve(dve, lambda k: x_sb[:, k], lambda k: coef[:, gain_no, k:k + 1],
                             lambda k: shift[:, k:k + 1], hi=lambda k: hh[:, k], lo=lambda k: hl[:, k])

                @block.scalar
                def _(act):
                    norm_act(act, lambda k: x_sb[:, k], 7, lambda k: shift[:, k:k + 1], hi=lambda k: hh[:, k])

                @block.tensor
                def _(pe):
                    norm_pe(pe, 7)

        midh = [tiles(f"midh{b}", 32 + 16 * b, KT, F32R) for b in range(2)]
        midl = [tiles(f"midl{b}", 40 + 16 * b, KT, F32R) for b in range(2)]
        relu, rsq = tiles("relu", 64, 4), tiles("rsq", 68, 4)

        def mlp_phase(layer):
            order = [("up", 0), ("up", 1), ("down", 0), ("up", 2), ("down", 1), ("up", 3), ("down", 2), ("down", 3)]
            names = [f"mlp{layer}_{j}" for j in range(8)]
            phase_start()
            with nc.Block() as block:
                @block.sync
                def _(sp):
                    load_weights(sp, ahead(*names)[0])

                @block.gpsimd
                def _(pool):
                    split_weights(pool, ahead(*names)[1])

                @block.tensor
                def _(pe):
                    for name, (what, q) in zip(names, order):
                        if what == "up":
                            linear(pe, name, hh, hl)
                        else:
                            pe.wait_ge(*PE.need(sem("mid_ready"), KT))
                            linear(pe, name, midh[q % 2], midl[q % 2])

                @block.scalar
                def _(act):
                    for what, q in order:
                        if what == "down":
                            AC.skip(acc_ready, KT)
                            for b in range(NACC):
                                AC.skip(acc_free[b], KT // NACC)
                            turn["evac"] += KT
                            continue

                        def four(e, i):
                            for j in range(4):
                                b = bank()
                                e.wait_ge(*AC.need(acc_ready))
                                e.activation(relu[:, j], ps[:, b], ACT.Relu).then_inc(*AC.up(acc_free[b]))
                                e.wait_ge(*AC.need(acc_free[b]))
                                for w in AC.again(sem("mid_ready")):
                                    e.wait_ge(*w)
                                e.activation(rsq[:, j], relu[:, j], ACT.Square).then_inc(*AC.up(sem("squared")))
                                e.wait_ge(*AC.last())
                                settle(e)
                                e.activation(one_of(midh[q % 2], 4 * i + j), rsq[:, j],
                                             ACT.Copy).then_inc(*AC.up(sem("mid_high")))
                        AC.loop(act, 2, four)

                @block.vector
                def _(dve):
                    for what, q in order:
                        if what == "down":
                            add_to_x(dve, lambda m: mod[layer][:, ds(40 + m, 1)])
                            continue
                        VE.skip(acc_ready, KT)
                        turn["evac"] += KT

                        def four(e, i):
                            for j in range(4):
                                e.wait_ge(*VE.need(sem("mid_high")))
                                e.tensor_tensor(one_of(midl[q % 2], 4 * i + j), rsq[:, j],
                                                one_of(midh[q % 2], 4 * i + j).bitcast(F32),
                                                ALU.subtract).then_inc(*VE.up(sem("mid_ready")))
                        VE.loop(dve, 2, four)

        norm_phase(1, mod[0][:, 24:32])
        mlp_phase(0)

        kk_sb, q_sb, g_sb = tiles("kk_sb", 32, KT), tiles("q_sb", 48, KT), tiles("g_sb", 56, KT)
        vtok = tiles("vtok", 40, shape=[P, 4, D])
        f16 = tiles("f16", 64, shape=[16, 4, T])
        fneg = tiles("fneg", 68, shape=[16, T])
        ftok = fixed("ftok", [P, 4, 16])
        norm_phase(4, kvm[:, 0:8])
        phase_start()
        with nc.Block() as block:
            names = ("kvk", "kvf", "kvv")

            @block.sync
            def _(sp):
                load_weights(sp, ahead(*names)[0])

            @block.gpsimd
            def _(pool):
                split_weights(pool, ahead(*names)[1])

            @block.tensor
            def _(pe):
                linear(pe, "kvk", hh, hl)
                block_of(pe, firsts["kvf"][1], 0, hh, hl, KT, P)
                for j in range(4):
                    tokens_of(pe, firsts["kvv"][1] + j, 0, hh, hl)

            @block.scalar
            def _(act):
                for k in range(KT):
                    b = bank()
                    act.wait_ge(*AC.need(acc_ready))
                    act.activation(kk_sb[:, k], ps[:, b], ACT.Copy).then_inc(*AC.up(acc_free[b]))
                b = bank()
                act.wait_ge(*AC.need(acc_ready))
                act.activation(f16[:, 0], ps[:16, b], ACT.Identity, bias=V("fb")[:16]).then_inc(*AC.up(acc_free[b]))
                act.wait_ge(*AC.last())
                act.activation(f16[:, 1], f16[:, 0], ACT.Abs).then_inc(*AC.up(sem("f_z")))
                act.wait_ge(*AC.last())
                act.activation(f16[:, 1], f16[:, 1], ACT.Exp, scale=-1.0).then_inc(*AC.up(sem("f_z")))
                act.wait_ge(*AC.last())
                act.activation(f16[:, 1], f16[:, 1], ACT.Ln, bias=1.0).then_inc(*AC.up(sem("f_z")))

            @block.vector
            def _(dve):
                VE.skip(acc_ready, KT + 1)
                chain = sem("dve")
                dve.memset(f16[:, 3], 1.0).then_inc(*VE.up(chain))
                dve.wait_ge(*VE.need(sem("f_z"), 3))
                dve.tensor_scalar(f16[:, 2], f16[:, 0], 0.0, None, ALU.min).then_inc(*VE.up(chain))
                dve.wait_ge(*VE.last())
                dve.tensor_tensor(f16[:, 2], f16[:, 2], f16[:, 1], ALU.subtract).then_inc(*VE.up(chain))
                dve.wait_ge(*VE.last())
                dve.tensor_tensor_scan(f16[:, 0], f16[:, 3], f16[:, 2], 0.0, ALU.mult, ALU.add).then_inc(*VE.up(chain))
                dve.wait_ge(*VE.last())
                dve.tensor_scalar(fneg[:], f16[:, 0], -1.0, None, ALU.mult).then_inc(*VE.up(chain))
                turn["evac"] = KT + 1
                for j in range(4):
                    for t in range(4):
                        b = bank()
                        dve.wait_ge(*VE.need(acc_ready))
                        dve.tensor_copy(vtok[:, t, 256 * j:256 * j + 256],
                                        ps[:, b, :256]).then_inc(*VE.up(acc_free[b]))

        norm_phase(2, mod[1][:, 0:8])
        phase_start()
        with nc.Block() as block:
            @block.sync
            def _(sp):
                load_weights(sp, ahead("fq")[0])

            @block.gpsimd
            def _(pool):
                split_weights(pool, ahead("fq")[1])

            @block.tensor
            def _(pe):
                linear(pe, "fq", hh, hl)

            @block.scalar
            def _(act):
                for to, func in ((q_sb, ACT.Copy), (g_sb, ACT.Sigmoid)):
                    def four(e, i):
                        for j in range(4):
                            b = bank()
                            e.wait_ge(*AC.need(acc_ready))
                            settle(e)
                            e.activation(one_of(to, 4 * i + j), ps[:, b], func).then_inc(*AC.up(acc_free[b]))
                    AC.loop(act, 2, four)

        fall = tiles("fall", 8, 16)
        qk_sq = tiles("qk_sq", 72, 2)
        qk_rms = tiles("qk_rms", 30, shape=[P, 2, 64])
        rows = tiles("rows", 26, shape=[16, 2, T])
        phase_start()
        with nc.Block() as block:
            @block.tensor
            def _(pe):
                for t in range(4):
                    o = pe.transpose(ps[:, 7, 16 * t:16 * t + 16], f16[:, 0, P * t:P * t + P], ident[:16, :16])
                o.then_inc(*PE.up(sem("f_turned")))

                def two_heads(e, i):
                    for j in range(2):
                        e.wait_ge(*PE.need(sem("qk_squared")))
                        for t in range(4):
                            o = e.matmul(ps[:, 5 + j, ds(2 * i + 16 * t, 2)], qk_sq[:, j, P * t:P * t + P],
                                         head[:, 0:P:64], start=True, stop=True)
                        o.then_inc(*PE.up(sem("qk_sum")))
                PE.loop(pe, KT, two_heads)
                for h in range(16):
                    for w in PE.again(acc_free[h % 4]):
                        pe.wait_ge(*w)
                    pe.matmul(ps[:, h % 4], ident[:16, h:h + 1].broadcast_to([16, P]), fneg[:], start=True,
                              stop=True).then_inc(*PE.up(acc_ready))
                pe.wait_ge(*PE.need(sem("qk_inverse")))
                for j in range(2):
                    for t in range(4):
                        o = pe.transpose(ps[:16, 5 + j, P * t:P * t + P], qk_rms[:, j, 16 * t:16 * t + 16], ident)
                    o.then_inc(*PE.up(sem("qk_rows")))

            @block.scalar
            def _(act):
                def two_heads(e, i):
                    for j, src in enumerate((q_sb, kk_sb)):
                        e.wait_ge(sem("qk_sum"), book.base[sem("qk_sum")] + 2 * i + j - 1)
                        settle(e)
                        e.activation(qk_sq[:, j], one_of(src, i), ACT.Square).then_inc(*AC.up(sem("qk_squared")))
                AC.loop(act, KT, two_heads)
                act.wait_ge(sem("qk_sum"), book.base[sem("qk_sum")] + 2 * KT)
                act.activation(qk_rms[:], ps[:, 5:7, :64], ACT.Sqrt, bias=C("epsn"),
                               scale=1.0 / 64).then_inc(*AC.up(sem("qk_rms")))
                for h in range(16):
                    act.wait_ge(*AC.need(acc_ready))
                    act.activation(fall[:, h], ps[:, h % 4], ACT.Copy).then_inc(*AC.up(acc_free[h % 4]))
                act.wait_ge(*AC.need(sem("qk_rows"), 2))
                act.activation(rows[:], ps[:16, 5:7], ACT.Copy).then_inc(*AC.up(sem("rows_ready")))

            @block.vector
            def _(dve):
                dve.wait_ge(*VE.need(sem("f_turned")))
                dve.tensor_copy(ftok[:], ps[:, 7, :64].rearrange("p (t h) -> p t h", h=16)).then_inc(*VE.up(sem("dve")))
                dve.wait_ge(*VE.need(sem("qk_rms")))
                dve.reciprocal(qk_rms[:], qk_rms[:]).then_inc(*VE.up(sem("qk_inverse")))

        qn, kn = tiles("qn", 24, shape=[P, T]), tiles("kn", 25, shape=[P, T])
        vp = tiles("vp", 28, shape=[P, 4, P])
        otile = tiles("otile", 29, shape=[P, T])
        sc, pr = tiles("sc", 64, 4), tiles("pr", 68, 2)
        ptr = tiles("ptr", 70, 4)
        oh, ol = tiles("oh", 48, KT, F32R), tiles("ol", 32, KT, F32R)
        sm = fixed("sm", [P, 4, 3])
        qgs = fixed("qgs", [P, 1])
        ftp = fixed("ftp", [P, 4, 2])
        pair_sel = fixed("pair_sel", [16, P])
        items = [(h, t) for h in range(2) for t in range(4)]
        NI = len(items)
        score_bank = [0, 1, 2, 0, 1, 2, 0, 1]
        phase_start()
        scored, read, turned_read = sem("scores"), sem("scores_read"), sem("turned_read")
        with nc.Block() as block:
            @block.tensor
            def _(pe):
                def prepare(e):
                    e.wait_ge(*PE.need(sem("pair_ready")))
                    for j, b in enumerate((3, 7)):
                        o = e.matmul(ps[:, b], pair_sel[:], rows[:, j], start=True, stop=True)
                    o.then_inc(*PE.up(sem("scale_ready")))
                    e.wait_ge(*PE.need(sem("qk_normed")))

                def scores(e, i, n, free=None):
                    h, t = items[n]
                    rr = slice(64 * h, 64 * h + 64)
                    if free is not None:
                        e.wait_ge(read, book.base.get(read, 0) + NI * i + free + 1)
                    e.matmul(ps[:, score_bank[n], :P * (t + 1)], qn[rr, P * t:P * t + P], kn[rr, :P * (t + 1)],
                             start=True, stop=True).then_inc(*PE.up(scored))

                def turned(e, i, n):
                    h, t = items[n]
                    e.wait_ge(*PE.need(sem("p_ready")))
                    if n >= 2:
                        e.wait_ge(turned_read, book.base.get(turned_read, 0) + NI * i + n - 1)
                    for s in range(t + 1):
                        o = e.transpose(ps[:, 4 + n % 2, P * s:P * s + P], pr[:, n % 2, P * s:P * s + P], ident)
                    o.then_inc(*PE.up(sem("p_turned")))

                def values(e, i, h):
                    rr = slice(64 * h, 64 * h + 64)
                    if h == 0:
                        e.wait_ge(*PE.need(sem("v_copied")))
                        e.wait_ge(sem("o_gated"), book.base.get(sem("o_gated"), 0) + 2 * i)
                    e.wait_ge(turned_read, book.base.get(turned_read, 0) + NI * i + 4 * h + 4)
                    for s in range(4):
                        o = e.matmul(ps[rr, 6, P * s:], vp[:, s, rr], ptr[:, s, P * s:], start=s == 0, stop=s == 3)
                    o.then_inc(*PE.up(sem("o_done")))

                def turn_of(e, i, more=True):
                    scores(e, i, 2)
                    for n in range(NI):
                        if n + 3 < NI:
                            scores(e, i, n + 3, n)
                        elif more and n == 5:
                            prepare(e)
                        elif more:
                            scores(e, i, n - 6, n)
                        if n == 4:
                            values(e, i, 0)
                        turned(e, i, n)
                    values(e, i, 1)
                prepare(pe)
                scores(pe, 0, 0)
                scores(pe, 0, 1)
                PE.loop(pe, KT - 1, turn_of)
                turn_of(pe, KT - 1, more=False)

            @block.scalar
            def _(act):
                def select(e, i):
                    for h in range(2):
                        src = ident[:16, ds(2 * i + h, 1)] if not isinstance(i, int) else ident[:16, 2 * i + h:2 * i + h + 1]
                        o = e.activation(pair_sel[:, 64 * h:64 * h + 64], src.broadcast_to([16, 64]), ACT.Copy)
                    o.then_inc(*AC.up(sem("pair_ready")))

                def exp(e, n):
                    h, t = items[n]
                    w = P * (t + 1)
                    e.wait_ge(*AC.need(sem("max_ready")))
                    e.activation(pr[:, n % 2, :w], sc[:, n % 4, :w], ACT.Exp, bias=sm[:, n % 4, 0:1],
                                 accum_out=sm[:, n % 4, 1:2]).then_inc(*AC.up(sem("exp_done")))

                def turn_of(e, i, more=True):
                    for n, (h, t) in enumerate(items):
                        if n + 1 < NI:
                            exp(e, n + 1)
                        elif more:
                            exp(e, 0)
                        e.wait_ge(*AC.need(sem("p_turned")))
                        e.activation(ptr[:, 0:t + 1, P * t:P * t + P], ps[:, 4 + n % 2, :P * (t + 1)].rearrange(
                            "p (s t) -> p s t", t=P), ACT.Copy).then_inc(*AC.up(turned_read))
                        if n == 0:
                            e.activation(vp[:], vtok[:, :, ds(i * P, P)], ACT.Copy).then_inc(*AC.up(sem("v_copied")))
                        if n == 1 and more:
                            select(e, i + 1)
                select(act, 0)
                exp(act, 0)
                AC.loop(act, KT - 1, turn_of)
                turn_of(act, KT - 1, more=False)

            @block.vector
            def _(dve):
                chain = sem("dve")
                dve.tensor_scalar(qgs[:], V("qg", 0), 0.125, None, ALU.mult).then_inc(*VE.up(chain))
                dve.wait_ge(*VE.last())

                def step(e, o, s=chain):
                    o.then_inc(*VE.up(s))
                    e.wait_ge(*VE.last())

                def prepare(e, i):
                    e.tensor_copy(ftp[:], ftok[:, :, ds(2 * i, 2)]).then_inc(*VE.up(chain))
                    e.wait_ge(*VE.need(sem("scale_ready")))
                    e.scalar_tensor_tensor(qn[:], one_of(q_sb, i), qgs[:, 0:1], ps[:, 3], ALU.mult,
                                           ALU.mult).then_inc(*VE.up(chain))
                    step(e, e.scalar_tensor_tensor(kn[:], one_of(kk_sb, i), V("kg", 0), ps[:, 7], ALU.mult,
                                                   ALU.mult), sem("qk_normed"))

                def softmax(e, i, n):
                    h, t = items[n]
                    k, w = n % 4, P * (t + 1)
                    e.wait_ge(*VE.need(scored))
                    step(e, e.scalar_tensor_tensor(sc[:, k, :w], ps[:, score_bank[n], :w], ftp[:, t, h:h + 1],
                                                   one_of(fall, 2 * i + h)[:, :w], ALU.add, ALU.add), read)
                    step(e, e.tensor_tensor(sc[:, k, P * t:w], sc[:, k, P * t:w], C("causal"), ALU.add))
                    e.tensor_reduce(sm[:, k, 0:1], sc[:, k, :w], AX.X, ALU.max,
                                    negate=True).then_inc(*VE.up(sem("max_ready")))

                def divide(e, n):
                    h, t = items[n]
                    k, w = n % 4, P * (t + 1)
                    e.wait_ge(*VE.need(sem("exp_done")))
                    step(e, e.reciprocal(sm[:, k, 2:3], sm[:, k, 1:2]))
                    e.tensor_scalar(pr[:, n % 2, :w], pr[:, n % 2, :w], sm[:, k, 2:3], None,
                                    ALU.mult).then_inc(*VE.up(sem("p_ready")))

                def gate(e, i, h):
                    rr = slice(64 * h, 64 * h + 64)
                    e.wait_ge(*VE.need(sem("o_done")))
                    step(e, e.tensor_tensor(otile[rr], ps[rr, 6], one_of(g_sb, i)[rr], ALU.mult), sem("o_gated"))

                def turn_of(e, i, more=True):
                    for n in range(NI):
                        divide(e, n)
                        if n + 2 < NI:
                            softmax(e, i, n + 2)
                        elif more:
                            softmax(e, i + 1, n - 6)
                        if n == 5 and more:
                            prepare(e, i + 1)
                        if n == 5:
                            gate(e, i, 0)
                    gate(e, i, 1)
                    step(e, e.tensor_copy(one_of(oh, i), otile[:]))
                    step(e, e.tensor_tensor(one_of(ol, i), otile[:], one_of(oh, i).bitcast(F32), ALU.subtract))
                prepare(dve, 0)
                softmax(dve, 0, 0)
                softmax(dve, 0, 1)
                VE.loop(dve, KT - 1, turn_of)
                turn_of(dve, KT - 1, more=False)

        phase_start()
        with nc.Block() as block:
            @block.sync
            def _(sp):
                load_weights(sp, ahead("fo")[0])

            @block.gpsimd
            def _(pool):
                split_weights(pool, ahead("fo")[1])

            @block.tensor
            def _(pe):
                linear(pe, "fo", oh, ol)

            @block.vector
            def _(dve):
                add_to_x(dve, lambda m: mod[1][:, ds(16 + m, 1)])
        norm_phase(3, mod[1][:, 24:32])
        mlp_phase(1)

        def plain_norm(x, g, out_tiles):
            phase_start()
            with nc.Block() as block:
                @block.vector
                def _(dve):
                    norm_dve(dve, lambda k: x[:, k], lambda k: g[:, k:k + 1],
                             plain=lambda k: out_tiles[:, k])

                @block.scalar
                def _(act):
                    norm_act(act, lambda k: x[:, k], 7)

                @block.tensor
                def _(pe):
                    norm_pe(pe, 7)
        plain_norm(x_sb, V("final"), x_sb)

        h2h, h2l = (tiles(n, a, dt=F32R, shape=[P, KT, TA]) for n, a in (("h2h", 8), ("h2l", 20)))
        sq, rms, nt = (tiles(n, 60 + 2 * j, 2) for j, n in enumerate(("sq2", "rms2", "nt2")))
        ctx_sb = tiles("ctx_sb", 56, shape=[P, KT, TX])
        LAT = slice(TX, TA)
        for src, gain_no, shift, part, n in ((x_sb, 5, ada0[:, 0, 0:8], LAT, T), (ctx_sb, 6, ada0[:, 1, 0:8],
                                                                                   slice(0, TX), TX)):
            phase_start()
            with nc.Block() as block:
                @block.vector
                def _(dve):
                    norm_dve(dve, lambda k: src[:, k], lambda k: coef[:, gain_no, k:k + 1],
                             lambda k: shift[:, k:k + 1], n=n, hi=lambda k: h2h[:, k, part],
                             lo=lambda k: h2l[:, k, part])

                @block.scalar
                def _(act):
                    norm_act(act, lambda k: src[:, k], 7, lambda k: shift[:, k:k + 1], n=n, hi=lambda k: h2h[:, k, part])
                    if n == T:
                        act.dma_start(ctx_sb[:], A["cT"]).then_inc(*AC.up16(sem("ctx_loaded")))
                        act.wait_ge(*AC.last())

                @block.tensor
                def _(pe):
                    norm_pe(pe, 7, n=n)

        xm, qx, kx2 = (tiles(n, a, shape=[P, 4, TA]) for n, a in (("xm", 32), ("qx", 55), ("kx2", 61)))
        xch, xcl = tiles("xch", 38, dt=F32R, shape=[P, 4, TA]), tiles("xcl", 44, dt=F32R, shape=[P, 4, TA])
        xc = tiles("xc", 50, shape=[P, 2, TA])
        gacc = tiles("gacc", 53, shape=[P, TA])
        rowt = fixed("rowt", [P, NACC])
        ssb = tiles("ssb", 67, 6)
        vsb = tiles("vsb", 38, 6)
        d_s = nc.dram_tensor("d_s", (4, P, 6, T), F32, kind="Internal").ap()
        d_v = nc.dram_tensor("d_v", (4, P, 6, T), F32, kind="Internal").ap()
        d_x = nc.dram_tensor("d_x", (4, P, 4, T), F32, kind="Internal").ap()
        d_h = nc.dram_tensor("d_h", (4, P, 4, T), F32, kind="Internal").ap()
        spans = ((0, TX), (TX, T))
        KS = 512 ** -0.5
        phase_start()
        with nc.Block() as block:
            names = [f"{n}{h}" for n in ("xm", "q", "k", "gate") for h in range(4)]

            @block.sync
            def _(sp):
                load_weights(sp, ahead(*names)[0])

            @block.gpsimd
            def _(pool):
                split_weights(pool, ahead(*names)[1])

            acc_taken, per_head = sem("acc_taken"), 36

            def taken(i, h, n):
                return acc_taken, book.base.get(acc_taken, 0) + NACC + per_head * (2 * i + h) + n + 1

            @block.tensor
            def _(pe):
                def two_heads(e, i):
                    for h in range(2):
                        q0 = firsts["xm0"][1] + 4 * h
                        r0 = firsts["xm0"][0] + 5 * h
                        n = [0]

                        def bank_free():
                            n[0] += 1
                            s_, v = taken(i, h, n[0] - 1)
                            return [(s_, v - NACC)]

                        def tile_bank():
                            b = turn["acc"] % NACC
                            turn["acc"] += 1
                            for w in bank_free():
                                e.wait_ge(*w)
                            return b
                        for j in range(2):
                            block_of(e, q0 + j, 8 * i, h2h, h2l, KT, 256, tokens=spans, bank_free=bank_free)
                        e.wait_ge(*PE.need(sem("xc_ready"), 4))
                        for j in (2, 3):
                            block_of(e, q0 + j, 8 * i, xch, xcl, 4, 512, tokens=spans, bank_free=bank_free)
                        for s in range(6):
                            b = tile_bank()
                            for m in range(4):
                                o = e.transpose(ps[:, b, P * m:P * m + P], xm[:, m, P * s:P * s + P], ident)
                            o.then_inc(*PE.up(acc_ready))
                        e.wait_ge(*taken(i, h, 23))
                        r = r0 + 4
                        e.wait_ge(w_full[r % RAW], (r // 2 + 1 + 5 * i) * 16)
                        for w in PE.again(sem("gates_read")):
                            e.wait_ge(*w)
                        wg = wraw[:, r % RAW, :12 * P].rearrange("p (k c) -> p k c", k=12)
                        for b, (t0, nt_) in zip((4, 5), spans):
                            for j, src in enumerate((qx, kx2, xm)):
                                for m in range(4):
                                    o = e.matmul(ps[:, b, :nt_], wg[:, 4 * j + m], src[:, m, t0:t0 + nt_],
                                                 start=j == 0 and m == 0, stop=j == 2 and m == 3)
                        o.then_inc(w_cond, 1)
                        for s in range(6):
                            b = tile_bank()
                            for m in range(4):
                                o = e.matmul(ps[:, b], kx2[:, m, P * s:P * s + P], qx[:, m, LAT], start=m == 0,
                                             stop=m == 3)
                            o.then_inc(*PE.up(acc_ready))
                PE.loop(pe, 2, two_heads)

            @block.scalar
            def _(act):
                for j in range(NACC):
                    act.activation(rowt[:, j:j + 1], con[:, 0:1], ACT.Copy).then_inc(*AC.up(acc_taken))

                def two_heads(e, i):
                    for h in range(2):
                        def read_out(dst, n, **kw):
                            b = bank()
                            e.wait_ge(*AC.need(acc_ready))
                            e.activation(dst, ps[:, b, :n], ACT.Copy, **kw).then_inc(*AC.up(acc_taken))

                        def silu(m):
                            e.wait_ge(*AC.need(sem("conv_done")))
                            bias = vec[:, ds(vat["convb"][0] + 4 * (2 * i + h) + m, 1)]
                            settle(e)
                            e.activation(xc[:, m % 2], xc[:, m % 2], ACT.Silu, bias=bias).then_inc(*AC.up(sem("silu")))
                            e.wait_ge(sem("silu"), book.base.get(sem("silu"), 0) + 4 * (2 * i + h) + m + 1)
                            e.dma_start(d_x[ds(2 * i + h, 1), :, m].rearrange("a p t -> (a p) t"),
                                        xc[:, m % 2, LAT]).then_inc(*AC.up16(sem(f"skip_sent{m % 2}")))
                            e.activation(xch[:, m], xc[:, m % 2], ACT.Copy).then_inc(*AC.up(sem("xc_high")))
                        for m in range(4):
                            for t0, n in spans:
                                read_out(xm[:, m, t0:t0 + n], n)
                            if m == 1 and (h or not isinstance(i, int)):
                                e.wait_ge(sem("v_sent"), book.base.get(sem("v_sent"), 0) + 16 * (2 * i + h))
                            if m:
                                silu(m - 1)
                        silu(3)
                        for to, f in ((qx, 1.0), (kx2, KS)):
                            for m in range(4):
                                for t0, n in spans:
                                    read_out(to[:, m, t0:t0 + n], n, scale=f)
                        for s in range(6):
                            read_out(vsb[:, s], T)
                        e.wait_ge(*taken(i, h, 29))
                        e.dma_start(d_v[ds(2 * i + h, 1)].rearrange("a p s t -> (a p) s t"),
                                    vsb[:]).then_inc(*AC.up16(sem("v_sent")))
                        if h or not isinstance(i, int):
                            e.wait_ge(sem("s_sent"), book.base.get(sem("s_sent"), 0) + 16 * (2 * i + h))
                        for s in range(6):
                            read_out(ssb[:, s], T)
                        e.wait_ge(*taken(i, h, 35))
                        e.dma_start(d_s[ds(2 * i + h, 1)].rearrange("a p s t -> (a p) s t"),
                                    ssb[:]).then_inc(*AC.up16(sem("s_sent")))
                AC.loop(act, 2, two_heads)
                act.wait_ge(sem("v_sent"), book.base[sem("v_sent")] + 64)
                act.wait_ge(sem("s_sent"), book.base[sem("s_sent")] + 64)
                act.wait_ge(sem("skip_sent0"), book.base[sem("skip_sent0")] + 128)
                act.wait_ge(sem("skip_sent1"), book.base[sem("skip_sent1")] + 128)

            @block.vector
            def _(dve):
                chain = sem("dve")
                dve.memset(gacc[:], 0.0).then_inc(*VE.up(chain))
                dve.wait_ge(*VE.last())

                def two_heads(e, i):
                    for h in range(2):
                        def conv(m):
                            at = vat["convw"][0] + 9 * (4 * (2 * i + h) + m)
                            e.wait_ge(*taken(i, h, 2 * m + 1))
                            if m >= 2 or h or not isinstance(i, int):
                                s_ = sem(f"skip_sent{m % 2}")
                                e.wait_ge(s_, book.base.get(s_, 0) + 16 * (2 * (2 * i + h) + m // 2))
                            first = [True]

                            def tap(kh, kw, dst, src, center=False):
                                w = vec[:, ds(at + 3 * kh + kw, 1)]
                                if not first[0]:
                                    e.wait_ge(*VE.last())
                                if center:
                                    o = e.tensor_scalar(dst, src, w, None, ALU.mult)
                                else:
                                    o = e.scalar_tensor_tensor(dst, src, w, dst, ALU.mult, ALU.add)
                                first[0] = False
                                return o
                            y, z = xc[:, m % 2], xm[:, m]
                            tap(1, 1, y, z, True).then_inc(*VE.up(chain))
                            tap(1, 0, y[:, 1:TX], z[:, 0:TX - 1]).then_inc(*VE.up(chain))
                            tap(1, 2, y[:, 0:TX - 1], z[:, 1:TX]).then_inc(*VE.up(chain))
                            yg_ = y[:, LAT].rearrange("p (r c) -> p r c", c=64)
                            zg = z[:, LAT].rearrange("p (r c) -> p r c", c=64)
                            taps = [(a, b) for a in range(3) for b in range(3) if (a, b) != (1, 1)]
                            for kh, kw in taps:
                                r0, r1 = max(0, 1 - kh), 8 - max(0, kh - 1)
                                c0, c1 = max(0, 1 - kw), 64 - max(0, kw - 1)
                                o = tap(kh, kw, yg_[:, r0:r1, c0:c1],
                                        zg[:, r0 + kh - 1:r1 + kh - 1, c0 + kw - 1:c1 + kw - 1])
                                o.then_inc(*VE.up(sem("conv_done") if (kh, kw) == (2, 2) else chain))

                        def low(m):
                            e.wait_ge(*VE.need(sem("xc_high")))
                            e.tensor_tensor(xcl[:, m], xc[:, m % 2], xch[:, m].bitcast(F32),
                                            ALU.subtract).then_inc(*VE.up(sem("xc_ready")))
                            e.wait_ge(*VE.last())
                        conv(0)
                        conv(1)
                        low(0)
                        conv(2)
                        low(1)
                        conv(3)
                        low(2)
                        low(3)
                        e.wait_ge(w_cond, firsts["gate0"][1] + 2 * i + h + 1)
                        e.tensor_tensor(gacc[:, :TX], gacc[:, :TX], ps[:, 4, :TX], ALU.add).then_inc(*VE.up(chain))
                        e.tensor_tensor(gacc[:, LAT], gacc[:, LAT], ps[:, 5],
                                        ALU.add).then_inc(*VE.up(sem("gates_read")))
                        e.wait_ge(*VE.last())
                VE.loop(dve, 2, two_heads)

        gz, gl = tiles("gz", 55, shape=[P, TA]), tiles("gl", 57, shape=[P, TA])
        li, lf, bcum, gdir, mrun = (tiles(n, 59 + 3 * j, shape=[4, 2, TA]) for j, n in enumerate(
            ("li", "lf", "bcum", "gdir", "mrun")))
        one4 = tiles("one4", 50, shape=[4, TA])
        gnat = tiles("gnat", 32, shape=[4, 2, TA])
        nmax, nm = tiles("nmax", 35, shape=[4, 2, T]), tiles("nm", 37, shape=[4, 2, T])
        gcol = fixed("gcol", [P, 2, 6, 4])
        phase_start()
        with nc.Block() as block:
            @block.scalar
            def _(act):
                act.wait_ge(*AC.need(sem("gz_ready")))
                act.activation(gl[:], gz[:], ACT.Abs).then_inc(*AC.up(sem("gl")))
                act.wait_ge(*AC.last())
                act.activation(gl[:], gl[:], ACT.Exp, scale=-1.0).then_inc(*AC.up(sem("gl")))
                act.wait_ge(*AC.last())
                act.activation(gl[:], gl[:], ACT.Ln, bias=1.0).then_inc(*AC.up(sem("gl")))

            @block.vector
            def _(dve):
                def step(o, s=None):
                    o.then_inc(*VE.up(s or sem("dve")))
                    dve.wait_ge(*VE.last())
                step(dve.tensor_scalar(gz[:], gacc[:], V("bif", 0), None, ALU.add), sem("gz_ready"))
                dve.memset(one4[:], 1.0).then_inc(*VE.up(sem("dve")))
                dve.wait_ge(*VE.need(sem("gl"), 3))
                step(dve.tensor_scalar(gacc[:], gz[:], 0.0, None, ALU.min))
                step(dve.tensor_tensor(gl[:], gacc[:], gl[:], ALU.subtract))

                def ordered(dst, src, d, parts=((0, TX), (TX, TA))):
                    for a, b in parts:
                        view = src[:, a:b]
                        step(dve.tensor_copy(dst[:, a:b], view[:, ::-1] if d else view))
                for d in range(2):
                    ordered(li[:, d], gz[64 * d:64 * d + 4], d)
                    ordered(lf[:, d], gl[64 * d + 32:64 * d + 36], d)
                    step(dve.tensor_tensor_scan(bcum[:, d], one4[:], lf[:, d], 0.0, ALU.mult, ALU.add))
                    step(dve.tensor_tensor(gdir[:, d], li[:, d], bcum[:, d], ALU.subtract))
                    step(dve.tensor_tensor_scan(mrun[:, d], gdir[:, d], gdir[:, d], 0.0, ALU.max, ALU.max))
                    step(dve.tensor_tensor(li[:, d], bcum[:, d], mrun[:, d], ALU.add))
                    ordered(gnat[:, d], gdir[:, d], d)
                    for dst, src in ((nmax, mrun), (nm, li)):
                        view = src[:, d, LAT]
                        step(dve.tensor_scalar(dst[:, d], view[:, ::-1] if d else view, -1.0, None, ALU.mult),
                             sem("gate_rows"))
                dve.wait_ge(*VE.need(sem("g_turned")))
                dve.tensor_copy(gcol[:].rearrange("p d s h -> p (d s h)"), ps[:, 7, :48]).then_inc(*VE.up(sem("dve")))

            @block.tensor
            def _(pe):
                pe.wait_ge(*PE.need(sem("gate_rows"), 4))
                for d in range(2):
                    for s in range(6):
                        o = pe.transpose(ps[:, 7, 24 * d + 4 * s:24 * d + 4 * s + 4], gnat[:, d, P * s:P * s + P],
                                         ident[:4, :4])
                o.then_inc(*PE.up(sem("g_turned")))

        sld, vld = tiles("sld", 40, 6), tiles("vld", 46, 6)
        swf, swr = tiles("swf", 52, 6), tiles("swr", 58, 6)
        mb = tiles("mb", 64, 2)
        em = tiles("em", 66, 2)
        wt = tiles("wt", 68, 2)
        hb = tiles("hb", 70, 4)
        sel = tiles("sel", 39, shape=[4, T])
        sw = (swf, swr)

        def region(d, s):
            if s < 2:
                return 0, T
            return (P * (s - 2), T) if d == 0 else (0, P * (s - 1))
        parts = [(s, d) for s in range(6) for d in range(2)]
        phase_start()
        with nc.Block() as block:
            @block.sync
            def _(sp):
                def turn_of(e, i):
                    if not isinstance(i, int) or i:
                        e.wait_ge(sem("s_used"), book.base.get(sem("s_used"), 0) + i)
                    e.dma_start(sld[:], d_s[ds(i, 1)].rearrange("a p s t -> (a p) s t")).then_inc(*SP.up16(sem("s_in")))
                    if not isinstance(i, int) or i:
                        e.wait_ge(sem("v_used"), book.base.get(sem("v_used"), 0) + i)
                    e.dma_start(vld[:], d_v[ds(i, 1)].rearrange("a p s t -> (a p) s t")).then_inc(*SP.up16(sem("v_in")))
                SP.loop(sp, 4, turn_of)

            @block.tensor
            def _(pe):
                def turn_of(e, i):
                    for n in range(4):
                        e.wait_ge(*PE.need(sem("sel_ready")))
                        e.matmul(ps[:, n], ones[:4], sel[:], start=True, stop=True).then_inc(*PE.up(sem("spread")))
                    for s, d in parts:
                        t0, t1_ = region(d, s)
                        e.wait_ge(*PE.need(sem("sw_ready")))
                        o = e.matmul(ps[:, 4 + d, t0:t1_], ones, sw[d][:, s, t0:t1_], start=s == 0, stop=s == 5)
                        if s == 5:
                            o.then_inc(*PE.up(sem("den")))
                    e.wait_ge(*PE.need(sem("p_ready2"), 6))
                    e.wait_ge(*PE.need(sem("v_in"), 16))
                    for m in range(4):
                        for s in range(6):
                            t1_ = region(1, s)[1]
                            o = e.matmul(ps[:, m, :t1_], vld[:, s, P * m:P * m + P], swr[:, s, :t1_], start=s == 0,
                                         stop=s == 5)
                            if t1_ < T:
                                e.matmul(ps[:, m, t1_:], vld[:, s, P * m:P * m + P], swf[:, s, t1_:], start=False,
                                         stop=False)
                        o.then_inc(*PE.up(sem("v_used") if m == 3 else sem("h_done")))
                    for m in range(4):
                        e.wait_ge(*PE.need(sem("h_taken")))
                        o = e.matmul(ps[:, 6], ones, hb[:, m], start=m == 0, stop=m == 3)
                    o.then_inc(*PE.up(sem("h_sum")))
                    for m in range(4):
                        e.wait_ge(*PE.need(sem("h_squared")))
                        e.matmul(ps[:, 7], ones, wt[:, m % 2], start=m == 0,
                                 stop=m == 3).then_inc(*PE.up(sem("h_square_used")))
                PE.loop(pe, 4, turn_of)

            @block.scalar
            def _(act):
                def turn_of(e, i):
                    for n in range(4):
                        e.wait_ge(*AC.need(sem("spread")))
                        if n < 2:
                            e.activation(mb[:, n], ps[:, n], ACT.Copy).then_inc(*AC.up(sem("spread_taken")))
                        else:
                            e.activation(em[:, n - 2], ps[:, n], ACT.Exp).then_inc(*AC.up(sem("spread_taken")))
                    for n, (s, d) in enumerate(parts):
                        t0, t1_ = region(d, s)
                        e.wait_ge(*AC.need(sem("w_log")))
                        e.activation(wt[:, n % 2, t0:t1_], wt[:, n % 2, t0:t1_],
                                     ACT.Exp).then_inc(*AC.up(sem("w_exp")))
                    for d in range(2):
                        e.wait_ge(*AC.need(sem("den")))
                        e.activation(mb[:, d], ps[:, 4 + d], ACT.Abs).then_inc(*AC.up(sem("den_abs")))
                    for m in range(4):
                        e.wait_ge(*AC.need(sem("v_used") if m == 3 else sem("h_done")))
                        e.activation(hb[:, m], ps[:, m], ACT.Copy).then_inc(*AC.up(sem("h_taken")))
                    for m in range(4):
                        e.wait_ge(*AC.need(sem("h_centred")))
                        if m >= 2:
                            e.wait_ge(*AC.need(sem("h_square_used")))
                        e.activation(wt[:, m % 2], hb[:, m], ACT.Square).then_inc(*AC.up(sem("h_squared")))
                    e.wait_ge(*AC.need(sem("h_square_used"), 2))
                    e.activation(mb[:, 0], ps[:, 7], ACT.Sqrt, bias=C("epsn"),
                                 scale=1.0 / 512).then_inc(*AC.up(sem("h_dev")))
                    e.wait_ge(*AC.need(sem("h_normed")))
                    e.dma_start(d_h[ds(i, 1)].rearrange("a p m t -> (a p) m t"), hb[:]).then_inc(*AC.up16(sem("h_sent")))
                    e.wait_ge(*AC.need(sem("h_sent"), 16))
                AC.loop(act, 4, turn_of)

            @block.vector
            def _(dve):
                def turn_of(e, i):
                    def step(o, s=None):
                        o.then_inc(*VE.up(s or sem("dve")))
                        e.wait_ge(*VE.last())
                    for n in range(4):
                        src = (nmax, nm)[n // 2][:, n % 2]
                        step(e.tensor_scalar(sel[:], src, ident[:4, ds(i, 1)], None, ALU.mult), sem("sel_ready"))
                        e.wait_ge(*VE.need(sem("spread_taken")))
                    e.wait_ge(*VE.need(sem("s_in"), 16))

                    def log_weight(n):
                        s, d = parts[n]
                        t0, t1_ = region(d, s)
                        e.tensor_scalar(wt[:, n % 2, t0:t1_], mb[:, d, t0:t1_], gcol[:, d, s, ds(i, 1)], 0.0, ALU.add,
                                        ALU.min).then_inc(*VE.up(sem("w_log")))
                    log_weight(0)
                    for n, (s, d) in enumerate(parts):
                        t0, t1_ = region(d, s)
                        if n + 1 < len(parts):
                            log_weight(n + 1)
                        e.wait_ge(*VE.need(sem("w_exp")))
                        if s >= 2:
                            diag = slice(P * (s - 2), P * (s - 1))
                            step(e.tensor_tensor(wt[:, n % 2, diag], wt[:, n % 2, diag], C(("fwd", "rev")[d]), ALU.mult))
                        step(e.tensor_tensor(sw[d][:, s, t0:t1_], wt[:, n % 2, t0:t1_], sld[:, s, t0:t1_], ALU.mult),
                             sem("sw_ready"))
                    for d in range(2):
                        e.wait_ge(*VE.need(sem("den_abs")))
                        step(e.tensor_tensor(em[:, d], em[:, d], mb[:, d], ALU.max))
                        step(e.reciprocal(em[:, d], em[:, d]), sem("s_used") if d else None)
                    for s in range(6):
                        for d in range(2):
                            t0, t1_ = region(d, s)
                            e.tensor_tensor(sw[d][:, s, t0:t1_], sw[d][:, s, t0:t1_], em[:, d, t0:t1_],
                                            ALU.mult).then_inc(*VE.up(sem("dve")))
                        e.wait_ge(*VE.last())
                        both = slice(0, T) if s < 2 else slice(P * (s - 2), P * (s - 1))
                        e.tensor_tensor(swr[:, s, both], swr[:, s, both], swf[:, s, both],
                                        ALU.add).then_inc(*VE.up(sem("p_ready2")))
                    e.wait_ge(*VE.need(sem("h_sum")))
                    for m in range(4):
                        e.scalar_tensor_tensor(hb[:, m], ps[:, 6], -1.0 / 512, hb[:, m], ALU.mult,
                                               ALU.add).then_inc(*VE.up(sem("h_centred")))
                    e.wait_ge(*VE.need(sem("h_dev")))
                    step(e.reciprocal(mb[:, 1], mb[:, 0]))
                    for m in range(4):
                        o = e.scalar_tensor_tensor(hb[:, m], hb[:, m], vec[:, ds(vat["lnw2"][0] + 4 * i + m, 1)],
                                                   mb[:, 1], ALU.mult, ALU.mult)
                        if m == 3:
                            o.then_inc(*VE.up(sem("h_normed")))
                    e.wait_ge(*VE.last())
                VE.loop(dve, 4, turn_of)

        y_sb = tiles("y_sb", 32, 16)
        skip_sb = tiles("skip_sb", 48, 16)
        yh, yl = tiles("yh", 48, 16, F32R), tiles("yl", 32, 16, F32R)
        gt_, yz = tiles("gt_", 64, 4), tiles("yz", 68, 4)

        def gated(e, func, free=None):
            for j in range(4):
                b = bank()
                for w in free(j) if free else ():
                    e.wait_ge(*w)
                e.wait_ge(*AC.need(acc_ready))
                e.activation(gt_[:, j], ps[:, b], func).then_inc(*AC.up(acc_free[b]))

        phase_start()
        with nc.Block() as block:
            names = ("o",)

            @block.sync
            def _(sp):
                for h in range(4):
                    sp.dma_start(y_sb[:, 4 * h:4 * h + 4], d_h[h]).then_inc(*SP.up16(sem(f"y_in{h}")))
                    sp.dma_start(skip_sb[:, 4 * h:4 * h + 4], d_x[h]).then_inc(*SP.up16(sem(f"skip_in{h}")))
                load_weights(sp, ahead("o")[0])
                for h in range(4):
                    sp.wait_ge(*SP.need(sem(f"y_in{h}"), 16))
                    sp.wait_ge(*SP.need(sem(f"skip_in{h}"), 16))

            @block.gpsimd
            def _(pool):
                split_weights(pool, ahead("o")[1])

            @block.tensor
            def _(pe):
                linear(pe, "o", h2h, h2l, tokens=((TX, T),))

            @block.scalar
            def _(act):
                AC.loop(act, 4, lambda e, i: gated(e, ACT.Sigmoid, lambda j: AC.again(sem(f"gt_used{j}"))))

            @block.vector
            def _(dve):
                for h in range(4):
                    dve.wait_ge(*VE.need(sem(f"y_in{h}"), 16))
                    dve.wait_ge(*VE.need(sem(f"skip_in{h}"), 16))

                def four(e, i):
                    for j in range(4):
                        y = one_of(y_sb, 4 * i + j)
                        e.wait_ge(*VE.need(acc_free[j]))
                        e.tensor_tensor(y, y, gt_[:, j], ALU.mult).then_inc(*VE.up(sem(f"gt_used{j}")))
                        e.wait_ge(*VE.last())
                        e.scalar_tensor_tensor(y, one_of(skip_sb, 4 * i + j), vec[:, ds(vat["skip"][0] + 4 * i + j, 1)],
                                               y, ALU.mult, ALU.add).then_inc(*VE.up(sem("dve")))
                VE.loop(dve, 4, four)

        def silu_phase(name, xhi, xlo, **kw):
            phase_start()
            with nc.Block() as block:
                @block.sync
                def _(sp):
                    load_weights(sp, ahead(name)[0])

                @block.gpsimd
                def _(pool):
                    split_weights(pool, ahead(name)[1])

                @block.tensor
                def _(pe):
                    linear(pe, name, xhi, xlo, **kw)

                @block.scalar
                def _(act):
                    def four(e, i):
                        gated(e, ACT.Silu)
                        for j in range(4):
                            e.wait_ge(*AC.need(sem(f"gated{j}")))
                            settle(e)
                            e.activation(one_of(yh, 4 * i + j), yz[:, j], ACT.Copy).then_inc(*AC.up(sem("y_high")))
                    AC.loop(act, 4, four)

                @block.vector
                def _(dve):
                    def four(e, i):
                        for j in range(4):
                            e.wait_ge(*VE.need(acc_free[j]))
                            e.tensor_tensor(yz[:, j], one_of(y_sb, 4 * i + j), gt_[:, j],
                                            ALU.mult).then_inc(*VE.up(sem(f"gated{j}")))
                        for j in range(4):
                            e.wait_ge(*VE.need(sem("y_high")))
                            e.tensor_tensor(one_of(yl, 4 * i + j), yz[:, j], one_of(yh, 4 * i + j).bitcast(F32),
                                            ALU.subtract).then_inc(*VE.up(sem("dve")))
                        e.wait_ge(*VE.last())
                    VE.loop(dve, 4, four)

        def wide_out(name, gate):
            phase_start()
            with nc.Block() as block:
                @block.sync
                def _(sp):
                    load_weights(sp, ahead(name)[0])

                @block.gpsimd
                def _(pool):
                    split_weights(pool, ahead(name)[1])

                @block.tensor
                def _(pe):
                    q = firsts[name][1]

                    def pair(e, i):
                        for j in range(2):
                            open_bank = {}
                            for k in range(2):
                                block_of(e, q + 2 * j + k, 4 * i, yh, yl, KT, 256, k0=KT * k, first=k == 0,
                                         final=k == 1, open_bank=open_bank)
                    PE.loop(pe, 2, pair)

                @block.vector
                def _(dve):
                    add_to_x(dve, gate)
        silu_phase("z", h2h, h2l, tokens=((TX, T),))
        wide_out("mo", lambda m: ada0[:, 0, ds(16 + m, 1)])

        dch, dtok = tiles("dch", 24, shape=[P, 2, 512]), tiles("dtok", 64, shape=[P, 2, 4, T])
        u_sb, ucs = tiles("u_sb", 26, 4), tiles("ucs", 48, 8)
        sq, rms, nt = (tiles(n, 24 + 2 * j, 2) for j, n in enumerate(("sq", "rms", "nt")))
        norm_phase(7, ada1[:, 0:8])
        phase_start()
        with nc.Block() as block:
            f_taken, per_turn = sem("f_taken"), 16

            def ftaken(i, n):
                return f_taken, book.base.get(f_taken, 0) + NACC + per_turn * i + n + 1

            @block.sync
            def _(sp):
                sp.dma_start(dch[:].rearrange("p a c -> p (a c)"), A["dch"]).then_inc(*SP.up16(sem("dch_in")))
                sp.dma_start(dtok[:].rearrange("p a b c -> p (a b c)"), A["dtok"]).then_inc(*SP.up16(sem("dtok_in")))
                load_weights(sp, ahead("fu")[0])

            @block.gpsimd
            def _(pool):
                split_weights(pool, ahead("fu")[1])

            @block.tensor
            def _(pe):
                pe.wait_ge(*PE.need(sem("dch_in"), 16))
                pe.wait_ge(*PE.need(sem("dtok_in"), 16))

                def two_groups(e, i):
                    made, seen = [0], [-NACC - 1]

                    def wait_taken(n):
                        if n > seen[0]:
                            e.wait_ge(*ftaken(i, n))
                            seen[0] = n

                    def bank_free():
                        made[0] += 1
                        seen[0] = made[0] - 1 - NACC
                        return [ftaken(i, seen[0])]

                    def tile_bank(operand):
                        b = turn["acc"] % NACC
                        turn["acc"] += 1
                        made[0] += 1
                        wait_taken(max(made[0] - 1 - NACC, operand))
                        return b
                    for h in range(2):
                        block_of(e, firsts["fu"][1] + h, 2 * i, hh, hl, KT, 256, bank_free=bank_free)
                    for h in range(2):
                        for t in range(4):
                            b = tile_bank(2 * h + 1)
                            for k in range(2):
                                o = e.matmul(ps[:, b], u_sb[:, 2 * h + k, P * t:P * t + P], dch[:, k], start=k == 0,
                                             stop=k == 1)
                            o.then_inc(*PE.up(acc_ready))
                    for h in range(2):
                        for m in range(2):
                            b = tile_bank(4 + 4 * h)
                            for t in range(4):
                                wait_taken(4 + 4 * h + t)
                                for c in range(2):
                                    o = e.matmul(ps[:, b], ucs[:, 4 * h + t, 256 * c + P * m:256 * c + P * m + P],
                                                 dtok[:, c, t], start=t == 0 and c == 0, stop=t == 3 and c == 1)
                            o.then_inc(*PE.up(acc_ready))
                PE.loop(pe, 4, two_groups)

            @block.scalar
            def _(act):
                for j in range(NACC):
                    act.activation(rowt[:, j:j + 1], con[:, 0:1], ACT.Copy).then_inc(*AC.up(f_taken))

                def two_groups(e, i):
                    for n in range(per_turn):
                        b = bank()
                        e.wait_ge(*AC.need(acc_ready))
                        if n < 4:
                            to = u_sb[:, n]
                        elif n < 12:
                            to = ucs[:, n - 4]
                        else:
                            to = one_of(y_sb, 4 * i + n - 12)
                            settle(e)
                        e.activation(to, ps[:, b], ACT.Copy).then_inc(*AC.up(f_taken))
                AC.loop(act, 4, two_groups)
        silu_phase("fz", hh, hl)
        wide_out("fo2", lambda m: ada1[:, ds(16 + m, 1)])
        res = tiles("res", 32, KT)
        plain_norm(x_sb, V("normf"), res)

        phase_start()
        with nc.Block() as block:
            @block.sync
            def _(sp):
                sp.dma_start(out, res[:]).then_inc(*SP.up16(sem("out_written")))
                sp.wait_ge(*SP.need(sem("out_written"), 16))


def kernel(**inputs):
    import concourse.bacc as bacc
    from concourse.bass_utils import run_bass_kernel_spmd

    x = {k: np.asarray(v) for k, v in inputs.items()}
    arrays, plan, vat, cat = layout(x)
    nc = bacc.Bacc("TRN2", target_bir_lowering=False, num_devices=1)
    A = {n: nc.dram_tensor(n, a.shape, F32, kind="ExternalInput").ap() for n, a in arrays.items()}
    out = nc.dram_tensor("out", (P, KT, T), F32, kind="ExternalOutput").ap()
    program(nc, A, out, plan, vat, cat)
    r = run_bass_kernel_spmd(nc, [arrays], core_ids=[0])
    got = np.asarray(r.results[0]["out"])
    return np.ascontiguousarray(got.transpose(2, 1, 0).reshape(1, T, D))
```

```python
from contextlib import ExitStack

import numpy as np

import concourse.bass as bass
from concourse import mybir

F32 = mybir.dt.float32
F32R = mybir.dt.float32r
ACT = mybir.ActivationFunctionType
ALU = mybir.AluOpType
AX = mybir.AxisListType
ds = bass.ds

P = 128
T = 512
D = 1024
KT = D // P
TX = 256
TA = TX + T
NF = 4 * D // P
E2 = 2048
ET = E2 // P
CH = 64
NC = T // CH
BLK = 2048
RAW, SPL = 2, 2
COND_TURN = 12
NACC = 4
LAGGED = (*(f"acc_free{b}" for b in range(NACC)), "mat_by_act", "mat_by_dve", "mid_ready", "qk_sum", "qk_sum",
          "o_gated", "gates_read", "v_sent", "s_sent", "skip_sent0",
          "skip_sent1", "gt_used0", "gt_used1", "gt_used2", "gt_used3")
HALF = 0.6065306597126334
NORM_EPS, GN_EPS = 1e-6, 64e-5


def cols(v):
    return np.ascontiguousarray(np.asarray(v).reshape(-1, P).T)


def blocks(w, width=256, kt=8):
    w = np.asarray(w)
    rows, n = w.shape
    b = w.reshape(rows // (P * kt), kt, P, n // width, width).transpose(3, 0, 2, 1, 4)
    b = b.reshape(-1, P, kt * width)
    out = np.zeros((b.shape[0], P, BLK), w.dtype)
    out[:, :, :kt * width] = b
    return out


def padded(w, rows, n):
    out = np.zeros((rows, n), np.asarray(w).dtype)
    out[:w.shape[0], :w.shape[1]] = w
    return out


def stream(x):
    def mlp(i):
        up, down = x["mlp_up"][i], x["mlp_down"][i]
        u = [blocks(up[:, D * q:D * (q + 1)]) for q in range(4)]
        d = [blocks(down[D * q:D * (q + 1)]) for q in range(4)]
        return [u[0], u[1], d[0], u[2], d[1], u[3], d[2], d[3]]
    lora_w = np.zeros((1, P, BLK), np.float32)
    lora_w[0, :64, :D] = x["rw_w2"][0]
    lora_w[0, 64:, D:] = x["rw_a2"][0]
    a1 = np.zeros((D, P), np.float32)
    a1[:, 64:] = x["rw_a1"][0]
    seq = [("raw", "mod0", blocks(x["mod_w"][0][:, :2 * D])),
           ("split", "wr", blocks(x["rw_wr"][0])),
           ("split", "w1", blocks(padded(x["rw_w1"][0], D, P), P)),
           ("split", "a1", blocks(a1, P)),
           ("split", "wk", blocks(x["rw_wk"][0])),
           ("split", "wv", blocks(x["rw_wv"][0])),
           ("split", "w2a2", lora_w),
           ("split", "g1", blocks(padded(x["rw_g1"][0], D, 256))),
           ("raw", "mod0b", blocks(x["mod_w"][0][:, 2 * D:])),
           ("raw", "mod1", blocks(x["mod_w"][1])),
           ("raw", "kvm", blocks(x["kv_mod_w"])),
           ("raw", "ada0", blocks(x["w_ada_2"][0])),
           ("raw", "ada1", blocks(x["w_ada_2"][1])),
           ("raw", "ada0c", blocks(x["w_ada_2"][0])),
           ("split", "g2", blocks(padded(x["rw_g2"][0], 256, D), D, 2)),
           ("split", "wo", blocks(x["rw_wo"][0]))]
    seq += [("split", f"mlp0_{j}", b) for j, b in enumerate(mlp(0))]
    kv = x["kv_w"]
    wqg = x["fx_wqg"][0]
    seq += [("split", "kvk", blocks(kv[:, :D])),
            ("split", "kvf", blocks(padded(kv[:, 2 * D:], D, P), P)),
            ("split", "kvv", blocks(kv[:, D:2 * D])),
            ("split", "fq", blocks(wqg)),
            ("split", "fo", blocks(x["fx_wo"][0]))]
    seq += [("split", f"mlp1_{j}", b) for j, b in enumerate(mlp(1))]
    w_in = x["m_w_in_2"][0]
    wif = np.asarray(x["m_w_if_2"][0])
    for h in range(4):
        c = slice(512 * h, 512 * (h + 1))
        gate = np.zeros((1, P, 12, P), wif.dtype)
        for t in range(3):
            for d in range(2):
                part = wif[d, t, c].reshape(4, P, 8).transpose(1, 0, 2)
                gate[0, :, 4 * t:4 * t + 4, 64 * d:64 * d + 4] = part[:, :, :4]
                gate[0, :, 4 * t:4 * t + 4, 64 * d + 32:64 * d + 36] = part[:, :, 4:]
        g = np.zeros((1, P, BLK), wif.dtype)
        g[:, :, :12 * P] = gate.reshape(1, P, -1)
        seq += [("split", f"xm{h}", blocks(w_in[:, c])),
                ("split", f"q{h}", blocks(x["m_w_q_2"][0, h], 512, 4)),
                ("split", f"k{h}", blocks(x["m_w_k_2"][0, h], 512, 4)),
                ("raw", f"gate{h}", g)]
    f_in = x["f_w_in_2"][0]
    seq += [("split", "o", blocks(w_in[:, E2:2 * E2])),
            ("split", "z", blocks(w_in[:, 2 * E2:])),
            ("split", "mo", blocks(x["m_w_out_2"][0])),
            ("split", "fu", blocks(f_in[:, :E2])),
            ("split", "fz", blocks(f_in[:, E2:])),
            ("split", "fo2", blocks(x["f_w_out_2"][0]))]
    return seq


def vectors(x):
    v = {}
    for i in range(2):
        v[f"nmix{i}"] = cols(x["norm_mix_g"][i])
        v[f"nmlp{i}"] = cols(x["norm_mlp_g"][i])
        v[f"modb{i}"] = cols(x["mod_b"][i])
        v[f"adab{i}"] = cols(x["b_ada_2"][i])
        v[f"n2{i}"] = cols(x["norm_g_2"][i])
    v["c"] = cols(x["c"])
    v["c3"] = np.stack([cols(x["c"]), cols(x["c_2"]), cols(x["c_ctx_2"])], 1).reshape(P, -1)
    for j in range(6):
        v[f"mu{j}"] = cols(x["rw_mu"][0, j])
    v["w0"], v["a0"] = cols(x["rw_w0"][0]), cols(x["rw_a0"][0])
    pair = [cols(x[n][0]) for n in ("rw_kk", "rw_ka", "rw_rk", "rw_lnw", "rw_lnb")]
    v["pair"] = np.stack(pair, 2).reshape(P, -1)
    v["kvn"], v["kvmb"] = cols(x["kv_norm_g"]), cols(x["kv_mod_b"])
    v["kg"], v["qg"] = cols(np.tile(x["kv_kg"], 2)), cols(np.tile(x["fx_qg"][0], 2))
    v["fb"] = padded(np.asarray(x["kv_fb"])[:, None], P, 1)
    v["final"] = cols(x["final_g"])
    v["convw"] = np.asarray(x["m_conv_w_2"][0]).reshape(9, ET, P).transpose(2, 1, 0).reshape(P, -1)
    v["convb"] = cols(x["m_conv_b_2"][0])
    bias = np.zeros((P, 1), np.float32)
    for d in range(2):
        bias[64 * d:64 * d + 4, 0] = x["m_b_i_2"][0, d]
        bias[64 * d + 32:64 * d + 36, 0] = x["m_b_f_2"][0, d]
    v["bif"] = bias
    v["lnw2"], v["skip"] = cols(x["m_ln_w_2"][0]), cols(x["m_skip_2"][0])
    v["normf"] = cols(x["norm_f_2"])
    return v


def constants():
    c = {}
    i = np.arange(P)
    same = i[:, None] // 64 == i[None] // 64
    c["ident"] = np.eye(P)
    c["ones"] = np.ones((P, P))
    c["head"] = same * 1.0
    up, upi = same * (i[:, None] < i[None]), same * (i[:, None] <= i[None])
    c["mrec"] = np.concatenate([up, upi], 1)
    c["m16"] = i[:, None] // 16 == i[None] // 16
    c["mlow16"] = c["m16"] * (i[:, None] > i[None])
    c["keep"] = np.tile(np.arange(T) % CH != 0, (P, 1))
    c["causal"] = np.where(i[None] <= i[:, None], 0.0, -1e30)
    c["fwd"] = (i[:, None] <= i[None]) * 1.0
    c["rev"] = (i[:, None] >= i[None]) * 1.0
    c["epsn"] = np.full((P, 1), NORM_EPS)
    c["zero"] = np.zeros((P, 1))
    c["epsg"] = np.full((P, 1), GN_EPS)
    return {k: np.asarray(v, np.float32) for k, v in c.items()}


def dft_tables():
    a = 2 * np.pi * (np.arange(256)[:, None] * np.arange(256)[None] % 256) / 256
    ch = np.concatenate([np.cos(a), np.sin(a)], 1).reshape(2, P, 512).transpose(1, 0, 2)
    b = 2 * np.pi * (np.arange(T)[:, None] * np.arange(T)[None] % T) / T
    f = (T * 256) ** -0.5
    tok = np.stack([np.cos(b) * f, -np.sin(b) * f]).reshape(2, 4, P, T).transpose(2, 0, 1, 3)
    return ch.reshape(P, -1).astype(np.float32), tok.reshape(P, -1).astype(np.float32)


def layout(x):
    seq = stream(x)
    vec, con = vectors(x), constants()
    ch, tok = dft_tables()
    arrays = {
        "wst": np.concatenate([b for _, _, b in seq]),
        "vec": np.concatenate(list(vec.values()), 1),
        "con": np.concatenate(list(con.values()), 1),
        "xT": np.ascontiguousarray(np.asarray(x["x"])[0].T.reshape(KT, P, T).transpose(1, 0, 2)),
        "cT": np.ascontiguousarray(np.asarray(x["ctx_2"])[0].T.reshape(KT, P, TX).transpose(1, 0, 2)),
        "dch": ch, "dtok": tok,
    }
    plan = [(kind, name, b.shape[0]) for kind, name, b in seq]
    vat, cat = {}, {}
    for table, parts in ((vat, vec), (cat, con)):
        at = 0
        for k, a in parts.items():
            table[k] = (at, a.shape[1])
            at += a.shape[1]
    return arrays, plan, vat, cat


class Dry:

    def _same(self, *args, **kwargs):
        return self

    matmul = transpose = activation = tensor_tensor = tensor_scalar = scalar_tensor_tensor = _same
    tensor_copy = tensor_reduce = reciprocal = memset = dma_start = then_inc = wait_ge = nop = _same
    tensor_tensor_scan = affine_select = _same


class Engine:

    def __init__(self, book, name):
        self.book, self.name, self.latest = book, name, None
        self.made, self.took = {}, {}

    def up(self, sem):
        self.made[sem] = self.made.get(sem, 0) + 1
        self.latest = sem
        return sem, 1

    def up16(self, sem):
        self.made[sem] = self.made.get(sem, 0) + 16
        self.latest = sem
        return sem, 16

    def used(self, sem):
        return sem, self.book.base.get(sem, 0) + self.took[sem]

    def skip(self, sem, k):
        self.took[sem] = self.took.get(sem, 0) + k

    def last(self):
        return self.latest, self.book.base.get(self.latest, 0) + self.made[self.latest]

    def need(self, sem, k=1):
        self.took[sem] = self.took.get(sem, 0) + k
        return sem, self.book.base.get(sem, 0) + self.took[sem]

    def again(self, sem):
        n = self.took.get(sem, 0)
        self.took[sem] = n + 1
        if isinstance(n, int) and n == 0:
            return []
        return [(sem, self.book.base.get(sem, 0) + n)]

    def loop(self, e, n, body):
        made, took, latest = dict(self.made), dict(self.took), self.latest
        body(Dry(), 0)
        dm = {s: v - made.get(s, 0) for s, v in self.made.items()}
        dt = {s: v - took.get(s, 0) for s, v in self.took.items()}

        def at(start, step, i):
            return {s: start.get(s, 0) + (i * step[s] if step[s] else 0) for s in step}
        self.latest = latest
        with e.Fori(0, n) as i:
            self.made, self.took = at(made, dm, i), at(took, dt, i)
            body(e, i)
        self.made, self.took = at(made, dm, n), at(took, dt, n)


class Book:

    def __init__(self, nc, ctx):
        self.nc, self.ctx, self.base, self.sems = nc, ctx, {}, {}
        self.engines = [Engine(self, n) for n in ("pe", "act", "dve", "pool", "sp")]

    def sem(self, name):
        if name not in self.sems:
            self.sems[name] = self.ctx.enter_context(self.nc.semaphore(name))
        return self.sems[name]

    def phase(self):
        for g in self.engines:
            for s, n in g.made.items():
                self.base[s] = self.base.get(s, 0) + n
            g.made, g.took, g.latest = {}, {}, None


def program(nc, A, out, plan, vat, cat):
    ctx = ExitStack()
    with ctx:
        book = Book(nc, ctx)
        PE, AC, VE, GP, SP = book.engines
        sem = book.sem

        def fixed(name, shape, dt=F32):
            return ctx.enter_context(nc.sbuf_tensor(name, shape, dt))

        wraw = fixed("wraw", [P, RAW, BLK])
        ring_at = (nc.sbuf_base + 31) // 32 * 32
        fixed("split_ring", [P, 2 * SPL * BLK])
        whi, wlo = (nc.alloc_sbuf_tensor_at(n, [P, SPL, BLK], F32R, offset=ring_at + 4 * j * SPL * BLK)
                    for j, n in enumerate(("whi", "wlo")))
        scaled = nc.alloc_sbuf_tensor_at("scaled", [P, KT, 256], F32, offset=ring_at)
        csum = nc.alloc_sbuf_tensor_at("csum", [P, COND_TURN, 256], F32, offset=ring_at + 4 * SPL * BLK)
        vec = fixed("vec_sb", [P, A["vec"].shape[1]])
        con = fixed("con_sb", [P, A["con"].shape[1]])
        started = fixed("started", [P, len(LAGGED)])
        cact = fixed("cact", [P, KT])
        cact3 = fixed("cact3", [P, 3, KT])
        mod = [fixed(f"mod{i}", [P, 48]) for i in range(2)]
        kvm = fixed("kvm", [P, 16])
        ada0 = fixed("ada0", [P, 2, 24])
        ada1 = fixed("ada1", [P, 24])
        coef = fixed("coef", [P, 8, KT])
        NT = nc.sbuf_bytes_remaining // 2048
        fence = nc.sbuf_base
        fixed("arena", [P, NT, T])
        off0 = (fence + 31) // 32 * 32
        named = {}

        def tiles(name, at, n=None, dt=F32, shape=None):
            shape = shape or [P, n, T]
            words = int(np.prod(shape[1:]))
            assert at * T + words <= NT * T, (name, at, words, NT)
            if name not in named:
                named[name] = nc.alloc_sbuf_tensor_at(name, shape, dt, offset=off0 + at * 2048)
            return named[name]

        ps = ctx.enter_context(nc.psum_tensor("ps", [P, 8, 512], F32))

        def V(name, i=None, n=1):
            at, width = vat[name]
            return vec[:, at:at + width] if i is None else vec[:, at + i:at + i + n]

        def C(name):
            at, width = cat[name]
            return con[:, at:at + width]

        ident, ones, head = C("ident"), C("ones"), C("head")

        raws = [kind for kind, _, n in plan for _ in range(n)]
        seqno, firsts, n_split, n_raw = [], {}, 0, 0
        for kind, name, n in plan:
            firsts[name] = (len(seqno), n_split if kind == "split" else n_raw)
            for _ in range(n):
                if kind == "split":
                    seqno.append(n_split)
                    n_split += 1
                else:
                    seqno.append(n_raw)
                    n_raw += 1
        split_at = [r for r, k in enumerate(raws) if k == "split"]
        firsts_raw = {m: f[0] for m, f in firsts.items()}
        w_full = [sem(f"w_loaded{s}") for s in range(RAW)]
        w_split, w_used, w_cond = sem("w_split"), sem("w_used"), sem("w_cond_used")
        sent = {"dma": 0, "pool": 0, "q": 0}

        def settle(e):
            e.nop(nofuse=True)

        def load_weights(sp, upto):
            upto = min(upto, len(raws))
            while sent["dma"] < upto:
                r = sent["dma"]
                if r < RAW:
                    sp.dma_start(wraw[:, r], A["wst"][r]).then_inc(w_full[r], 16)
                    sent["dma"] += 1
                    continue
                n = 1
                while r + n < upto and raws[r + n - RAW] == raws[r - RAW]:
                    n += 1
                free = w_split if raws[r - RAW] == "split" else w_cond
                turns, c0 = n // 2, seqno[r - RAW] + 1

                def one(k, i):
                    sp.wait_ge(free, c0 + k + 2 * i)
                    sp.dma_start(wraw[:, (r + k) % RAW], A["wst"][ds(r + k + 2 * i, 1)].rearrange(
                        "a p c -> (a p) c")).then_inc(w_full[(r + k) % RAW], 16)
                if turns > 1:
                    with sp.Fori(0, turns) as i:
                        one(0, i)
                        one(1, i)
                    rest = range(2 * turns, n)
                else:
                    rest = range(n)
                for k in rest:
                    one(k, 0)
                sent["dma"] += n

        def split_weights(pool, upto):
            upto = min(upto, n_split)
            while sent["pool"] < upto:
                q = sent["pool"]
                r = split_at[q]
                n = 1
                while q + n < upto and split_at[q + n] == r + n:
                    n += 1
                if q < SPL:
                    n = 1

                def one(k, i):
                    s, f = (q + k) % SPL, (r + k) % RAW
                    if q >= SPL:
                        pool.wait_ge(w_used, q + k + 2 * i)
                    pool.wait_ge(w_full[f], ((r + k) // 2 + 1 + i) * 16)
                    pool.tensor_tensor(whi[:, s], wraw[:, f], C("zero").broadcast_to([P, BLK]), ALU.add).then_inc(sem("w_high"), 1)
                    pool.wait_ge(sem("w_high"), q + k + 1 + 2 * i)
                    pool.tensor_tensor(wlo[:, s], wraw[:, f], whi[:, s].bitcast(F32),
                                       ALU.subtract).then_inc(w_split, 1)
                turns = n // 2
                if turns > 1:
                    with pool.Fori(0, turns) as i:
                        one(0, i)
                        one(1, i)
                    rest = range(2 * turns, n)
                else:
                    rest = range(n)
                for k in rest:
                    one(k, 0)
                sent["pool"] += n

        def ahead(*names):
            raw_end = max(firsts_raw[m] + c for _, m, c in plan if m in names)
            q_end = sum(1 for r in split_at if r < raw_end)
            if q_end < n_split and split_at[q_end] == raw_end:
                return raw_end + 3, q_end + 1
            return raw_end + 2, q_end

        acc_ready = sem("acc_ready")
        acc_free = [sem(f"acc_free{b}") for b in range(NACC)]
        turn = {"acc": 0}

        def block_of(e, q, i, xhi, xlo, nk, width, tokens=((0, T),), k0=0, first=True, final=True, m0=0, mn=None,
                     open_bank=None, tell=True, bank_free=None):
            s = q % SPL
            wh = whi[:, s, :nk * width].rearrange("p (k c) -> p k c", k=nk)
            wl = wlo[:, s, :nk * width].rearrange("p (k c) -> p k c", k=nk)
            e.wait_ge(w_split, q + i + 1)
            told = not tell
            for m in range(width // P if mn is None else mn):
                for a, (t0, nt) in enumerate(tokens):
                    if open_bank is None or first:
                        b = turn["acc"] % NACC
                        turn["acc"] += 1
                        for w in (bank_free() if bank_free else PE.again(acc_free[b])):
                            e.wait_ge(*w)
                        if open_bank is not None:
                            open_bank[m] = b
                    else:
                        b = open_bank[m]
                    mc = slice((m0 + m) * P, (m0 + m + 1) * P)
                    for k in range(nk):
                        passes = ((wh, xhi), (wh, xlo), (wl, xhi))
                        for j, (w, x) in enumerate(passes):
                            o = e.matmul(ps[:, b, :nt], w[:, k, mc], x[:, k0 + k, t0:t0 + nt],
                                         start=first and k == 0 and j == 0,
                                         stop=final and k == nk - 1 and j == 2)
                            if not told:
                                o.then_inc(w_used, 1)
                                told = True
                    if final:
                        o.then_inc(*PE.up(acc_ready))

        def tokens_of(e, q, i, xhi, xlo, nk=8, width=256):
            s = q % SPL
            wh = whi[:, s, :nk * width].rearrange("p (k c) -> p k c", k=nk)
            wl = wlo[:, s, :nk * width].rearrange("p (k c) -> p k c", k=nk)
            e.wait_ge(w_split, q + i + 1)
            for t in range(T // P):
                b = turn["acc"] % NACC
                turn["acc"] += 1
                for w in PE.again(acc_free[b]):
                    e.wait_ge(*w)
                tc = slice(t * P, (t + 1) * P)
                for k in range(nk):
                    for j, (w, x) in enumerate(((wh, xhi), (wl, xhi), (wh, xlo))):
                        o = e.matmul(ps[:, b, :width], x[:, k, tc], w[:, k, :], start=k == 0 and j == 0,
                                     stop=k == nk - 1 and j == 2)
                        if t == 0 and k == 0 and j == 0:
                            o.then_inc(w_used, 1)
                o.then_inc(*PE.up(acc_ready))

        def phase_start():
            book.phase()
            turn["acc"] = 0
            turn["evac"] = 0

        def bank():
            b = turn["evac"] % NACC
            turn["evac"] += 1
            return b

        sq, rms, nt = (tiles(n, 24 + 2 * j, 2) for j, n in enumerate(("sq", "rms", "nt")))
        hh, hl = tiles("hh", 8, KT, F32R), tiles("hl", 16, KT, F32R)

        def norm_pe(e, bank_no, n=T):
            e.wait_ge(*PE.need(sem("square_added"), KT - 1))
            e.matmul(ps[:, bank_no, :n], ones, rms[:, 1, :n], start=True, stop=True).then_inc(*PE.up(sem("square_sum")))

        def norm_act(e, src, bank_no, shift=None, n=T, hi=None):
            for k in range(KT):
                if k == 2 or k > 3:
                    e.wait_ge(*AC.need(sem("square_added")))
                e.activation(sq[:, k % 2, :n], src(k), ACT.Square).then_inc(*AC.up(sem("square")))
            e.wait_ge(*AC.need(sem("square_sum")))
            e.activation(rms[:, 0, :n], ps[:, bank_no, :n], ACT.Sqrt, bias=C("epsn"),
                         scale=1.0 / D).then_inc(*AC.up(sem("rms")))
            if hi is not None:
                for k in range(KT):
                    e.wait_ge(*AC.need(sem("scaled")))
                    e.activation(hi(k), nt[:, k % 2, :n], ACT.Identity,
                                 bias=shift(k)).then_inc(*AC.up(sem("rounded")))

        def norm_dve(e, src, gain, shift=None, n=T, hi=None, lo=None, plain=None):
            total = rms[:, 1, :n]
            e.wait_ge(*VE.need(sem("square")))
            for k in range(1, KT):
                e.wait_ge(*VE.need(sem("square")))
                e.tensor_tensor(total, sq[:, 0, :n] if k == 1 else total, sq[:, k % 2, :n],
                                ALU.add).then_inc(*VE.up(sem("square_added")))
                if k < KT - 1:
                    e.wait_ge(*VE.last())
            e.wait_ge(*VE.need(sem("rms")))
            e.reciprocal(rms[:, 1, :n], rms[:, 0, :n]).then_inc(*VE.up(sem("dve")))
            e.wait_ge(*VE.last())

            def low(k):
                e.wait_ge(*VE.need(sem("rounded")))
                e.scalar_tensor_tensor(lo(k), nt[:, k % 2, :n], shift(k), hi(k).bitcast(F32), ALU.add,
                                       ALU.subtract).then_inc(*VE.up(sem("x_ready")))
            for k in range(KT):
                if k >= 2 and not plain:
                    e.wait_ge(*VE.last())
                to = plain(k) if plain and shift is None else nt[:, k % 2, :n]
                o = e.scalar_tensor_tensor(to, src(k), gain(k), rms[:, 1, :n], ALU.mult, ALU.mult)
                if not plain:
                    o.then_inc(*VE.up(sem("scaled")))
                    if k:
                        low(k - 1)
                elif shift is None:
                    o.then_inc(*VE.up(sem("x_ready")))
                else:
                    o.then_inc(*VE.up(sem("dve")))
                    e.wait_ge(*VE.last())
                    e.tensor_scalar(plain(k), nt[:, k % 2, :n], shift(k), None,
                                    ALU.add).then_inc(*VE.up(sem("x_ready")))
                    e.wait_ge(*VE.last())
            if not plain:
                low(KT - 1)

        def cond_blocks(e, name, rhs, w, dst):
            r0, c0 = firsts[name]
            n = [c for _, m, c in plan if m == name][0]

            def two(i):
                for k in range(2):
                    e.wait_ge(w_full[(r0 + k) % RAW], ((r0 + k) // 2 + 1 + i) * 16)
                    slot = wraw[:, (r0 + k) % RAW].rearrange("p (k c) -> p k c", k=KT)
                    for m in range(2):
                        for t in range(KT):
                            o = e.matmul(dst[:, ds(i * 4 * w + (2 * k + m) * w, w)],
                                         slot[:, t, m * P:(m + 1) * P], rhs[:, t, :],
                                         start=t == 0, stop=t == KT - 1)
                    o.then_inc(w_cond, 1)
            with e.Fori(0, n // 2) as i:
                two(i)

        def gains(e, j, g, scale):
            e.scalar_tensor_tensor(coef[:, j], scale, 1.0, g, ALU.add, ALU.mult).then_inc(*VE.up(sem("dve")))

        x_sb = tiles("x", 0, KT)
        phase_start()
        with nc.Block() as block:
            @block.sync
            def _(sp):
                sp.dma_start(vec[:], A["vec"]).then_inc(*SP.up16(sem("vec_loaded")))
                sp.dma_start(con[:], A["con"]).then_inc(*SP.up16(sem("con_loaded")))
                sp.dma_start(x_sb[:], A["xT"]).then_inc(*SP.up16(sem("x_loaded")))
                load_weights(sp, ahead("mod0")[0])
                sp.wait_ge(sem("vec_loaded"), 16)
                sp.wait_ge(sem("con_loaded"), 16)
                sp.wait_ge(sem("x_loaded"), 16)

            @block.gpsimd
            def _(pool):
                for k, name in enumerate(LAGGED):
                    pool.memset(started[:, k:k + 1], 0.0).then_inc(*GP.up(sem(name)))
                split_weights(pool, ahead("mod0")[1])

            @block.scalar
            def _(act):
                act.wait_ge(*AC.need(sem("vec_loaded"), 16))
                act.activation(cact[:], V("c"), ACT.Silu).then_inc(*AC.up(sem("cond")))
                act.activation(cact3[:].rearrange("p c k -> p (c k)"), V("c3"),
                               ACT.Silu).then_inc(*AC.up(sem("cond")))

            @block.tensor
            def _(pe):
                pe.wait_ge(*PE.need(sem("cond"), 2))
                cond_blocks(pe, "mod0", cact[:].rearrange("p (k c) -> p k c", c=1), 1, ps[:, 7, :])

            @block.vector
            def _(dve):
                dve.wait_ge(w_cond, firsts["mod0"][1] + 8)
                dve.wait_ge(*VE.need(sem("vec_loaded"), 16))
                dve.tensor_tensor(mod[0][:, :16], ps[:, 7, :16], V("modb0", 0, 16), ALU.add).then_inc(*VE.up(sem("dve")))
        hpad = tiles("hpad", 8, shape=[P, KT, T + 1])
        phase_start()
        with nc.Block() as block:
            @block.vector
            def _(dve):
                dve.memset(hpad[:, :, 0:1], 0.0).then_inc(*VE.up(sem("dve")))
                gains(dve, 0, V("nmix0"), mod[0][:, 8:16])
                norm_dve(dve, lambda k: x_sb[:, k], lambda k: coef[:, 0, k:k + 1], lambda k: mod[0][:, k:k + 1],
                         plain=lambda k: hpad[:, k, 1:])

            @block.scalar
            def _(act):
                norm_act(act, lambda k: x_sb[:, k], 7)

            @block.tensor
            def _(pe):
                norm_pe(pe, 7)

        dif, mix = tiles("dif", 0, 2), tiles("mix", 2, 2)
        hid, hidh, hidl = tiles("hid", 4, 1), tiles("hidh", 5, 1, F32R), tiles("hidl", 6, 1, F32R)
        hidg = tiles("hidg", 0, 2)
        sgh, sgl = tiles("sgh", 4, 2, F32R), tiles("sgl", 6, 2, F32R)
        w_sb, a_sb, r_sb, k_sb, v_sb = (tiles(n, 33 + 8 * j, KT) for j, n in enumerate(
            ("w_sb", "a_sb", "r_sb", "k_sb", "v_sb")))
        A_, B_, C_ = ((tiles(f"mixh{n}", at, KT, F32R), tiles(f"mixl{n}", at + 8, KT, F32R))
                      for n, at in (("a", 17), ("b", 33), ("c", 57)))
        phase_start()
        with nc.Block() as block:
            names = ("wr", "w1", "a1", "wk", "wv", "w2a2", "g1")

            @block.sync
            def _(sp):
                load_weights(sp, ahead(*names)[0])

            @block.gpsimd
            def _(pool):
                split_weights(pool, ahead(*names)[1])

            @block.tensor
            def _(pe):
                def full(name, n, width, buf):
                    pe.wait_ge(*PE.need(sem("mix_ready"), KT))
                    for j in range(n):
                        block_of(pe, firsts[name][1] + j, 0, buf[0], buf[1], KT, width)
                full("wr", 4, 256, A_)
                full("w1", 1, P, B_)
                full("a1", 1, P, C_)
                full("wk", 4, 256, A_)
                full("wv", 4, 256, B_)
                pe.wait_ge(*PE.need(sem("hid_ready"), 2))
                q = firsts["w2a2"][1]
                block_of(pe, q, 0, hidh, hidl, 1, BLK, mn=8)
                block_of(pe, q, 0, hidh, hidl, 1, BLK, mn=8, m0=8, tell=False)
                full("g1", 1, 256, A_)

            @block.vector
            def _(dve):
                def mixing(j, buf, done):
                    if done:
                        dve.wait_ge(*VE.need(acc_ready, done))
                    for k in range(KT + 1):
                        if k < KT:
                            dve.tensor_tensor(dif[:, k % 2], hpad[:, k, :T], hpad[:, k, 1:],
                                              ALU.subtract).then_inc(*VE.up(sem("dve")))
                            dve.wait_ge(*VE.last())
                            dve.scalar_tensor_tensor(mix[:, k % 2], dif[:, k % 2], V(f"mu{j}", k), hpad[:, k, 1:],
                                                     ALU.mult, ALU.add).then_inc(*VE.up(sem("mixed")))
                        if k:
                            dve.wait_ge(*VE.need(sem("mix_high")))
                            dve.tensor_tensor(buf[1][:, k - 1], mix[:, (k - 1) % 2], buf[0][:, k - 1].bitcast(F32),
                                              ALU.subtract).then_inc(*VE.up(sem("mix_ready")))

                def hidden_low(x, lo, hi):
                    dve.wait_ge(*VE.need(sem("hid_high")))
                    dve.tensor_tensor(lo, x, hi.bitcast(F32), ALU.subtract).then_inc(*VE.up(sem("hid_ready")))
                mixing(0, A_, 0)
                mixing(1, B_, 0)
                mixing(4, C_, 0)
                mixing(2, A_, 8)
                for n in range(2):
                    rr = slice(64 * n, 64 * n + 64)
                    hidden_low(hid[rr, 0], hidl[rr, 0], hidh[rr, 0])
                mixing(3, B_, 1)
                mixing(5, A_, 1 + 8)
                for n in range(2):
                    hidden_low(hidg[:, n], sgl[:, n], sgh[:, n])

            @block.scalar
            def _(act):
                def high(buf, tiles_=range(KT)):
                    for k in tiles_:
                        act.wait_ge(*AC.need(sem("mixed")))
                        act.activation(buf[0][:, k], mix[:, k % 2], ACT.Copy).then_inc(*AC.up(sem("mix_high")))

                def read_out(dst, func, bias=0.0, rows=slice(0, P)):
                    b = bank()
                    act.wait_ge(*AC.need(acc_ready))
                    act.activation(dst, ps[rows, b], func, bias=bias).then_inc(*AC.up(acc_free[b]))

                def hidden(x, func, hi, rows=slice(0, P)):
                    read_out(x, func, rows=rows)
                    act.wait_ge(*AC.last())
                    act.activation(hi, x, ACT.Copy).then_inc(*AC.up(sem("hid_high")))
                high(A_)
                for k in range(KT):
                    high(B_ if k < 4 else C_, (2 * (k % 4), 2 * (k % 4) + 1))
                    read_out(r_sb[:, k], ACT.Copy)
                for n, func in enumerate((ACT.Tanh, ACT.Copy)):
                    rr = slice(64 * n, 64 * n + 64)
                    hidden(hid[rr, 0], func, hidh[rr, 0], rr)
                high(A_)
                for to, buf in ((k_sb, B_), (v_sb, A_)):
                    for k in range(KT):
                        if to is k_sb:
                            high(buf, (k,))
                            read_out(to[:, k], ACT.Copy)
                        else:
                            read_out(to[:, k], ACT.Copy)
                            high(buf, (k,))
                for k in range(KT):
                    read_out(w_sb[:, k], ACT.Sigmoid, V("w0", k))
                for k in range(KT):
                    read_out(a_sb[:, k], ACT.Sigmoid, V("a0", k))
                for n in range(2):
                    hidden(hidg[:, n], ACT.Sigmoid, sgh[:, n])

        w = iter([0, 1, 2, 3] + list(range(8, 33)))

        def work(name, n=1, shape=None):
            at = [next(w) for _ in range(n)]
            assert at[-1] - at[0] == n - 1
            return tiles(name, at[0], n, shape=shape or [P, 4, P])
        t1, t2, t3, t4 = (work(f"t{j}", shape=[P, T]) for j in range(1, 5))
        ar = work("ar", 2, [P, 4, 2, P])
        abrb = work("abrb", 2, [P, 4, 2, P])
        akrk = work("akrk", 2, [P, 4, 2, P])
        xav = work("xav", 2, [P, 4, 2, P])
        fg = work("fg", 2, [P, 4, 2, P])
        bb, kb, bt, kt, vt, ad, adt, aot, pt, a2, a2t = (work(n) for n in (
            "bb", "kb", "bt", "kt", "vt", "ad", "adt", "aot", "pt", "a2", "a2t"))
        kkn, wc, yt = (work(n, shape=[P, T]) for n in ("kkn", "wc", "yt"))
        st = work("st", shape=[P, 2, P])
        pv = fixed("pv", [P, 5])
        to_act, to_dve, ev_a, ev_v = sem("mat_for_act"), sem("mat_for_dve"), sem("mat_by_act"), sem("mat_by_dve")
        vs = tiles("vs", 73, shape=[P, 4, 2, CH])
        WKV_STEPS = ("GB", "GA", "BT", "GK", "AT", "KT", "VT", "A2", "A2T", "AV", "P2", "A4", "A4T", "P3", "A8", "P4",
                     "TD", "M", "MT", "Q", "M2", "T", "FG", "PHI", "E")
        WKV_DVE_STEPS = ("GB", "GA", "GK", "VT", "P2", "P3", "P4", "Q", "T", "PHI", "E")
        WKV_ACT = 2 * (2 * (len(WKV_STEPS) - len(WKV_DVE_STEPS)) + 1) + 2
        WKV_DVE = 2 * (2 * len(WKV_DVE_STEPS) + 4) + 2
        wkv_order = ["norm", "bonus"]
        for half in range(2):
            wkv_order += [(n, half, g) for n in WKV_STEPS for g in range(2)] + [("Y", half)]
            wkv_order += [("S", half, c) for c in range(4)]
        wkv_order += ["mean", "var"]
        wkv_bank = {n: j % 7 for j, n in enumerate(wkv_order)}
        phase_start()

        def tile_of(buf, i):
            return buf[:, ds(i, 1)].rearrange("p a t -> p (a t)")

        def chunks(ap):
            return ap.rearrange("p (c t) -> p c t", t=CH)

        with nc.Block() as block:
            @block.sync
            def _(sp):
                load_weights(sp, ahead("ada0c")[0])

            @block.gpsimd
            def _(pool):
                r0, c0 = firsts["mod0b"]

                def turn_blocks(e, i, cond, first):
                    for k in range(COND_TURN):
                        r = r0 + k
                        e.wait_ge(w_full[r % RAW], (r // 2 + 1) * 16 + COND_TURN * 8 * (first + i))
                        w = wraw[:, r % RAW].rearrange("p (k c) -> p k c", k=KT)
                        c = cact3[:, cond].rearrange("p (k a) -> p k a", a=1).broadcast_to([P, KT, 256])
                        e.tensor_tensor(scaled[:], w, c, ALU.mult).then_inc(w_cond, 1)
                        e.wait_ge(w_cond, c0 + k + 1 + COND_TURN * (first + i))
                        e.tensor_tensor(scaled[:, 0:4], scaled[:, 0:4], scaled[:, 4:8],
                                        ALU.add).then_inc(*GP.up(sem("cond_added")))
                        e.wait_ge(*GP.last())
                        e.tensor_tensor(scaled[:, 0:2], scaled[:, 0:2], scaled[:, 2:4],
                                        ALU.add).then_inc(*GP.up(sem("cond_added")))
                        e.wait_ge(*GP.last())
                        if not isinstance(i, int) or first or i:
                            e.wait_ge(sem("cond_taken"), COND_TURN * (first + i - 1) + k + 1)
                        e.tensor_tensor(csum[:, k], scaled[:, 0], scaled[:, 1],
                                        ALU.add).then_inc(*GP.up(sem("cond_summed")))
                        e.wait_ge(*GP.last())
                turn_blocks(pool, 0, 0, 0)
                GP.loop(pool, 3, lambda e, i: turn_blocks(e, i, 0, 1))
                GP.loop(pool, 2, lambda e, i: turn_blocks(e, i, 1, 4))
                turn_blocks(pool, 0, 2, 6)
                pool.wait_ge(sem("cond_taken"), 7 * COND_TURN)
                split_weights(pool, ahead("ada0c")[1])

            @block.tensor
            def _(pe):
                n_act, n_dve = WKV_ACT, WKV_DVE

                def turn_of(e, i, conditions=COND_TURN):
                    ready, last, made = {}, {}, {"a": 0, "v": 0}
                    seen, wanted = {"a": 0, "v": 0}, []

                    def wait_for_wanted():
                        for to, s, tot in (("a", ev_a, n_act), ("v", ev_v, n_dve)):
                            latest = max([n for t, n in wanted if t == to] + [0])
                            if latest > seen[to]:
                                e.wait_ge(s, book.base.get(s, 0) + i * tot + latest)
                                seen[to] = latest
                        wanted.clear()

                    if not isinstance(i, int) or i:
                        e.wait_ge(ev_a, book.base.get(ev_a, 0) + i * n_act)
                        e.wait_ge(ev_v, book.base.get(ev_v, 0) + i * n_dve)

                    def unit(name, to, products, n=256, transpose=False):
                        b = wkv_bank[name]
                        if b in last:
                            wanted.append(last[b])
                        wait_for_wanted()
                        o = products(b)
                        made[to] += 1
                        ready[name] = last[b] = (to, made[to])
                        o.then_inc(*PE.up(to_act if to == "a" else to_dve))

                    def mats(name, to, g, out, *terms, after=()):
                        for a in after:
                            wanted.append(ready[a, half, g])

                        def go(b):
                            for c in range(2):
                                for j, (l, r) in enumerate(terms):
                                    rhs = r(2 * g + c)
                                    cw = out // 2
                                    o = e.matmul(ps[:, b, c * cw:(c + 1) * cw], l(2 * g + c), rhs,
                                                 start=j == 0, stop=j == len(terms) - 1)
                            return o
                        unit((name, half, g), to, go)

                    def turned(name, to, g, src, after=()):
                        for a in after:
                            wanted.append(ready[a, half, g])

                        def go(b):
                            for c in range(2):
                                o = e.transpose(ps[:, b, c * P:(c + 1) * P], src(2 * g + c), ident)
                            return o
                        unit((name, half, g), to, go)

                    taken = [0]

                    def cond_block():
                        if taken[0] == conditions:
                            return
                        k = taken[0]
                        taken[0] += 1
                        e.wait_ge(*PE.need(sem("cond_summed")))
                        for j in range(2):
                            o = e.matmul(ps[:, 7, ds(i * 2 * COND_TURN + 2 * k + j, 1)], csum[:, k, j * P:(j + 1) * P],
                                         ones[:, 0:1], start=True, stop=True)
                        o.then_inc(*PE.up(sem("cond_taken")))

                    def headsum(name, to, src):
                        unit(name, to, lambda b: e.matmul(ps[:, b], head, src[:], start=True, stop=True))

                    e.wait_ge(*PE.need(sem("kk_squared")))
                    headsum("norm", "a", t1)
                    e.wait_ge(*PE.need(sem("rk_ready")))
                    headsum("bonus", "v", t2)

                    def m(buf, part=None):
                        return (lambda c: buf[:, c]) if part is None else (lambda c: buf[:, c, part])
                    for half in range(2):
                        e.wait_ge(*PE.need(sem("bd_ready")))

                        def arw(c):
                            return ar[:, c].rearrange("p a t -> p (a t)")

                        def vdup(c):
                            return vs[:, c].rearrange("p a t -> p (a t)")
                        G = range(2)
                        for g in G:
                            mats("GB", "v", g, 512, (m(bb), arw))
                        for g in G:
                            mats("GA", "v", g, 256, (m(ar, 0), m(bb)))
                        for g in G:
                            turned("BT", "a", g, m(bb))
                        for g in G:
                            mats("GK", "v", g, 512, (m(kb), arw))
                        cond_block()
                        for g in G:
                            turned("AT", "a", g, m(ar, 0))
                        for g in G:
                            turned("KT", "a", g, m(kb))
                        e.wait_ge(*PE.need(sem("v_twice")))
                        for g in G:
                            turned("VT", "v", g, vdup)
                        for g in G:
                            mats("A2", "a", g, 256, (m(adt), m(ad)), after=("GB", "GA"))
                        for g in G:
                            mats("A2T", "a", g, 256, (m(ad), m(adt)))
                        for g in G:
                            mats("AV", "a", g, 256, (m(akrk, 0), m(vt)), after=("GK", "VT"))
                        cond_block()
                        for g in G:
                            mats("P2", "v", g, 256, (m(a2), m(pt)), after=("A2",))
                        for g in G:
                            mats("A4", "a", g, 256, (m(a2t), m(a2)), after=("A2T",))
                        for g in G:
                            mats("A4T", "a", g, 256, (m(a2), m(a2t)))
                        cond_block()
                        for g in G:
                            mats("P3", "v", g, 256, (m(ad), m(pt)), after=("A4", "P2"))
                        for g in G:
                            mats("A8", "a", g, 256, (m(adt), m(ad)), after=("A4T",))
                        for g in G:
                            mats("P4", "v", g, 256, (m(a2), m(pt)), after=("A8", "P3"))
                        cond_block()
                        for g in G:
                            turned("TD", "a", g, m(pt), after=("P4",))
                        for g in G:
                            mats("M", "a", g, 256, (m(aot), m(a2t)), after=("TD",))
                        for g in G:
                            mats("MT", "a", g, 256, (m(a2t), m(aot)))
                        cond_block()
                        for g in G:
                            mats("Q", "v", g, 256, (m(ad), m(pt)), after=("M",))
                        for g in G:
                            mats("M2", "a", g, 256, (m(adt), m(ad)), after=("MT",))
                        for g in G:
                            mats("T", "v", g, 256, (m(a2), m(pt)), after=("M2", "Q"))
                        cond_block()
                        for g in G:
                            mats("FG", "a", g, 512, (m(pt), lambda c: xav[:, c].rearrange("p a t -> p (a t)")),
                                 after=("T", "AV", "AT"))
                        for g in G:
                            mats("PHI", "v", g, 256, (m(fg, 0), m(bt)), after=("FG", "BT"))
                        for g in G:
                            mats("E", "v", g, 256, (m(fg, 0), m(abrb, 1)))
                        yb = wkv_bank["Y", half]
                        if yb in last:
                            wanted.append(last[yb])
                        for g in G:
                            for name in ("KT", "PHI", "E"):
                                wanted.append(ready[name, half, g])
                        for c in range(4):
                            old = st[:, c % 2]
                            if c or half:
                                wanted.append(ready["S", half if c else half - 1, c - 1 if c else 3])

                            def state(b):
                                e.matmul(ps[:, b, :P], bt[:, c], fg[:, c, 1], start=True, stop=False)
                                e.matmul(ps[:, b, :P], kt[:, c], vt[:, c], start=False, stop=False)
                                return e.matmul(ps[:, b, :P], ad[:, c], old, start=False, stop=True)
                            unit(("S", half, c), "v", state)
                            yc = ps[:, yb, c * P:(c + 1) * P]
                            e.matmul(yc, fg[:, c, 1], abrb[:, c, 1], start=True, stop=False)
                            e.matmul(yc, vt[:, c], akrk[:, c, 1], start=False, stop=False)
                            o = e.matmul(yc, old, adt[:, c], start=False, stop=True)
                        o.then_inc(*PE.up(to_act))
                        made["a"] += 1
                        last[yb] = ("a", made["a"])
                    wanted.append(last[yb])
                    headsum("mean", "v", yt)
                    e.wait_ge(*PE.need(sem("y_squared")))
                    headsum("var", "a", t1)
                    assert made == {"a": n_act, "v": n_dve}, made

                PE.loop(pe, KT - 1, turn_of)
                turn_of(pe, KT - 1, conditions=0)

            @block.scalar
            def _(act):
                def copy(e, to, bank_no, n=256, func=ACT.Copy, own=ev_a, **kw):
                    e.wait_ge(*AC.need(to_act))
                    e.activation(to, ps[:, bank_no, :n], func, **kw).then_inc(*AC.up(own))

                def turn_of(e, i):
                    b = wkv_bank
                    e.wait_ge(*AC.need(sem("kr_ready")))
                    e.activation(t1[:], kkn[:], ACT.Square).then_inc(*AC.up(sem("kk_squared")))
                    copy(e, t1[:], b["norm"], T, ACT.Sqrt)
                    e.wait_ge(*AC.need(sem("cum_ready")))
                    e.activation(wc[:], t4[:], ACT.Exp).then_inc(*AC.up(sem("exp")))
                    e.activation(t4[:], t4[:], ACT.Exp, scale=-1.0).then_inc(*AC.up(sem("exp")))
                    e.activation(t3[:], t3[:], ACT.Exp).then_inc(*AC.up(sem("exp")))
                    for half in range(2):
                        for a in range(2):
                            o = e.activation(vs[:, :, a], chunks(v_sb[:, ds(i, 1), half * 256:half * 256 + 256].rearrange(
                                "p a t -> p (a t)")), ACT.Copy)
                        o.then_inc(*AC.up(sem("v_twice")))
                        for name, to in (("BT", bt), ("AT", xav), ("KT", kt), ("A2", a2), ("A2T", a2t), ("AV", xav),
                                         ("A4", ad), ("A4T", adt), ("A8", a2), ("TD", a2t), ("M", ad), ("MT", adt),
                                         ("M2", a2), ("FG", fg)):
                            for g in range(2):
                                cc = slice(2 * g, 2 * g + 2)
                                n = 512 if name == "FG" else 256
                                if name == "FG":
                                    dst = to[:, cc].rearrange("p c a t -> p (c a t)")
                                elif name == "AT":
                                    dst = to[:, cc, 0]
                                elif name == "AV":
                                    dst = to[:, cc, 1]
                                else:
                                    dst = to[:, cc].rearrange("p c t -> p (c t)")
                                src = ps[:, b[name, half, g], :n]
                                if name in ("AT", "AV"):
                                    src = src.rearrange("p (c t) -> p c t", c=2)
                                e.wait_ge(*AC.need(to_act))
                                e.activation(dst, src, ACT.Copy).then_inc(*AC.up(ev_a))
                        e.wait_ge(*AC.need(to_act))
                        for h in range(2):
                            o = e.activation(chunks(yt[64 * h:64 * h + 64, half * 256:(half + 1) * 256]),
                                             ps[64 * h:64 * h + 64, b["Y", half]].rearrange(
                                                 "p (c t) -> p c t", c=4)[:, :, 64 * h:64 * h + 64], ACT.Copy)
                        o.then_inc(*AC.up(ev_a))
                    e.wait_ge(ev_v, book.base.get(ev_v, 0) + i * WKV_DVE + WKV_DVE)
                    e.activation(t1[:], yt[:], ACT.Square).then_inc(*AC.up(sem("y_squared")))
                    copy(e, t2[:], b["var"], T, ACT.Sqrt, bias=C("epsg"), scale=1.0 / 64)
                AC.loop(act, KT, turn_of)

            @block.vector
            def _(dve):
                chain = sem("dve")
                for buf in (ar[:], bb[:], kb[:]):
                    dve.memset(buf, 0.0).then_inc(*VE.up(chain))

                def turn_of(e, i):
                    b = wkv_bank
                    kx, rx, vx, wx, ax = (tile_of(z, i) for z in (k_sb, r_sb, v_sb, w_sb, a_sb))

                    def step(o, s=chain):
                        o.then_inc(*VE.up(s))
                        e.wait_ge(*VE.last())

                    def taken(o):
                        o.then_inc(*VE.up(ev_v))
                    at = vat["pair"][0]
                    step(e.tensor_copy(pv[:], vec[:, ds(i * 5 + at, 5)]))
                    e.memset(st[:, 0], 0.0).then_inc(*VE.up(chain))
                    e.tensor_scalar(kkn[:], kx, pv[:, 0:1], None, ALU.mult).then_inc(*VE.up(sem("kr_ready")))
                    e.tensor_scalar(t3[:], wx, -HALF, None, ALU.mult).then_inc(*VE.up(chain))
                    step(e.tensor_scalar(t2[:], ax, -1.0, pv[:, 1:2], ALU.add, ALU.mult))
                    e.tensor_tensor_scan(t4[:], C("keep"), t3[:], 0.0, ALU.mult, ALU.add).then_inc(*VE.up(chain))
                    step(e.scalar_tensor_tensor(kx, t2[:], 1.0, kx, ALU.add, ALU.mult))
                    e.tensor_tensor(t3[:], t4[:], t3[:], ALU.subtract).then_inc(*VE.up(sem("cum_ready")))
                    e.scalar_tensor_tensor(t2[:], rx, pv[:, 2:3], kx, ALU.mult,
                                           ALU.mult).then_inc(*VE.up(sem("rk_ready")))
                    e.wait_ge(ev_a, book.base.get(ev_a, 0) + i * WKV_ACT + 1)
                    step(e.tensor_scalar(t1[:], t1[:], 1e-12, None, ALU.max))
                    step(e.reciprocal(t1[:], t1[:]))
                    step(e.tensor_tensor(kkn[:], kkn[:], t1[:], ALU.mult))
                    step(e.tensor_tensor(ax, kkn[:], ax, ALU.mult))
                    e.wait_ge(*VE.need(to_dve))
                    taken(e.tensor_tensor(wx, ps[:, b["bonus"]], vx, ALU.mult))
                    e.wait_ge(*VE.need(sem("exp"), 3))
                    for half in range(2):
                        for h in range(2):
                            rr, tc = slice(64 * h, 64 * h + 64), slice(256 * half, 256 * half + 256)

                            def part(z):
                                return chunks(z[rr, tc])
                            e.scalar_tensor_tensor(ar[rr, :, 0, rr], part(kkn[:]), -1.0, part(t3[:]), ALU.mult,
                                                   ALU.mult)
                            e.tensor_tensor(ar[rr, :, 1, rr], part(rx), part(wc[:]), ALU.mult)
                            e.tensor_tensor(bb[rr, :, rr], part(ax), part(t4[:]), ALU.mult)
                            o = e.tensor_tensor(kb[rr, :, rr], part(kx), part(t4[:]), ALU.mult)
                        o.then_inc(*VE.up(sem("bd_ready")))

                        def cc(g):
                            return slice(2 * g, 2 * g + 2)

                        def src(name, g, n=256):
                            return ps[:, b[name, half, g], :n]

                        def bc(z, k, n):
                            return z.rearrange("p (a n) -> p a n", a=1).broadcast_to([P, k, n])

                        def add(name, g, to, other):
                            e.wait_ge(*VE.need(to_dve))
                            taken(e.tensor_tensor(to[:, cc(g)], src(name, g).rearrange("p (c t) -> p c t", c=2),
                                                  other, ALU.add))

                        def masked(name, g, to, mask):
                            e.wait_ge(*VE.need(to_dve))
                            return e.tensor_tensor(to, src(name, g).rearrange("p (c t) -> p c t", c=2), mask, ALU.mult)
                        for g in range(2):
                            e.wait_ge(*VE.need(to_dve))
                            step(e.tensor_tensor(abrb[:, cc(g)].rearrange("p c a t -> p c (a t)"),
                                                 src("GB", g, 512).rearrange("p (c t) -> p c t", c=2),
                                                 bc(C("mrec"), 2, 256), ALU.mult))
                            step(e.tensor_tensor(adt[:, cc(g)], abrb[:, cc(g), 0], bc(C("m16"), 2, P), ALU.mult))
                            e.tensor_tensor(aot[:, cc(g)], abrb[:, cc(g), 0], adt[:, cc(g)], ALU.subtract)
                            taken(e.tensor_tensor(pt[:, cc(g)], adt[:, cc(g)], bc(ident, 2, P), ALU.add))
                        for g in range(2):
                            taken(masked("GA", g, ad[:, cc(g)], bc(C("mlow16"), 2, P)))
                        for g in range(2):
                            e.wait_ge(*VE.need(to_dve))
                            taken(e.tensor_tensor(akrk[:, cc(g)].rearrange("p c a t -> p c (a t)"),
                                                  src("GK", g, 512).rearrange("p (c t) -> p c t", c=2),
                                                  bc(C("mrec"), 2, 256), ALU.mult))
                        for g in range(2):
                            taken(masked("VT", g, vt[:, cc(g)], bc(head, 2, P)))
                        for name in ("P2", "P3", "P4", "Q", "T"):
                            for g in range(2):
                                add(name, g, pt, pt[:, cc(g)])
                        for g in range(2):
                            add("PHI", g, ad, bc(ident, 2, P))
                        for g in range(2):
                            add("E", g, adt, ar[:, cc(g), 1])
                        for c in range(4):
                            e.wait_ge(*VE.need(to_dve))
                            tl = (4 * half + c) * CH + CH - 1
                            taken(e.tensor_scalar(st[:, (c + 1) % 2], ps[:, b["S", half, c], :P], wc[:, tl:tl + 1],
                                                  None, ALU.mult))
                    e.wait_ge(*VE.need(to_dve))
                    e.scalar_tensor_tensor(yt[:], ps[:, b["mean"]], -1.0 / 64, yt[:], ALU.mult,
                                           ALU.add).then_inc(*VE.up(ev_v))
                    e.wait_ge(*VE.last())
                    e.wait_ge(ev_a, book.base.get(ev_a, 0) + i * WKV_ACT + WKV_ACT)
                    step(e.reciprocal(t2[:], t2[:]))
                    step(e.tensor_tensor(yt[:], yt[:], t2[:], ALU.mult))
                    step(e.tensor_scalar(yt[:], yt[:], pv[:, 3:4], pv[:, 4:5], ALU.mult, ALU.add))
                    step(e.tensor_tensor(rx, yt[:], wx, ALU.add))
                VE.loop(dve, KT, turn_of)

        def linear(e, name, xhi, xlo, part=(0, None), nk=8, width=256, **kw):
            n = [c for _, m, c in plan if m == name][0]
            lo, hi = part[0], part[1] or n
            q = firsts[name][1] + lo
            if hi - lo <= 2:
                for j in range(hi - lo):
                    block_of(e, q + j, 0, xhi, xlo, nk, width, **kw)
                return

            def two(f, i):
                for j in range(2):
                    block_of(f, q + j, 2 * i, xhi, xlo, nk, width, **kw)
            PE.loop(e, (hi - lo) // 2, two)

        def one_of(buf, i):
            return buf[:, ds(i, 1)].rearrange("p a t -> p (a t)")

        def add_to_x(e, gate, n=KT):
            def four(f, i):
                for j in range(4):
                    b = bank()
                    f.wait_ge(*VE.need(acc_ready))
                    xt = one_of(x_sb, 4 * i + j)
                    f.scalar_tensor_tensor(xt, ps[:, b], gate(4 * i + j), xt, ALU.mult,
                                           ALU.add).then_inc(*VE.up(acc_free[b]))
            VE.loop(e, n // 4, four)

        phase_start()
        yg = tiles("yg", 24, 2)
        with nc.Block() as block:
            names = ("g2", "wo")

            @block.sync
            def _(sp):
                load_weights(sp, ahead(*names)[0])

            @block.gpsimd
            def _(pool):
                split_weights(pool, ahead(*names)[1])

            @block.tensor
            def _(pe):
                block_of(pe, firsts["g2"][1], 0, sgh, sgl, 2, D)
                pe.wait_ge(*PE.need(sem("x_ready"), KT))
                linear(pe, "wo", hh, hl)

            @block.scalar
            def _(act):
                for k in range(KT):
                    act.wait_ge(*AC.need(acc_free[k % NACC]))
                    act.activation(hh[:, k], yg[:, k % 2], ACT.Copy).then_inc(*AC.up(sem("rounded")))
                act.dma_start(x_sb[:], A["xT"]).then_inc(*AC.up16(sem("x_again")))

            @block.vector
            def _(dve):
                for k in range(KT + 1):
                    if k < KT:
                        b = bank()
                        if k >= 2:
                            dve.wait_ge(*VE.last())
                        dve.wait_ge(*VE.need(acc_ready))
                        dve.tensor_tensor(yg[:, k % 2], ps[:, b], r_sb[:, k], ALU.mult).then_inc(*VE.up(acc_free[b]))
                    if k:
                        dve.wait_ge(*VE.need(sem("rounded")))
                        dve.tensor_tensor(hl[:, k - 1], yg[:, (k - 1) % 2], hh[:, k - 1].bitcast(F32),
                                          ALU.subtract).then_inc(*VE.up(sem("x_ready")))
                chain = sem("dve")
                cp = ps[:, 7]
                for to, src, bias in ((mod[0][:, 16:], cp[:, 0:32], V("modb0", 16, 32)),
                                      (mod[1][:], cp[:, 32:80], V("modb1")), (kvm[:], cp[:, 80:96], V("kvmb")),
                                      (ada0[:, 0], cp[:, 96:120], V("adab0")), (ada0[:, 1], cp[:, 144:168], V("adab0")),
                                      (ada1[:], cp[:, 120:144], V("adab1"))):
                    dve.tensor_tensor(to, src, bias, ALU.add).then_inc(*VE.up(chain))
                dve.wait_ge(*VE.last())
                for i in range(2):
                    for c in (16, 40):
                        dve.tensor_scalar(mod[i][:, c:c + 8], mod[i][:, c:c + 8], 1.0, None,
                                          ALU.add).then_inc(*VE.up(chain))
                for j, g, sc in ((1, "nmlp0", mod[0][:, 32:40]), (2, "nmix1", mod[1][:, 8:16]),
                                 (3, "nmlp1", mod[1][:, 32:40]), (4, "kvn", kvm[:, 8:16]), (5, "n20", ada0[:, 0, 8:16]),
                                 (6, "n20", ada0[:, 1, 8:16]), (7, "n21", ada1[:, 8:16])):
                    gains(dve, j, V(g), sc)
                dve.wait_ge(*VE.last())
                dve.wait_ge(*VE.need(sem("x_again"), 16))
                add_to_x(dve, lambda m: mod[0][:, ds(16 + m, 1)])

        def norm_phase(gain_no, shift, names=()):
            phase_start()
            with nc.Block() as block:
                @block.vector
                def _(dve):
                    norm_dve(dve, lambda k: x_sb[:, k], lambda k: coef[:, gain_no, k:k + 1],
                             lambda k: shift[:, k:k + 1], hi=lambda k: hh[:, k], lo=lambda k: hl[:, k])

                @block.scalar
                def _(act):
                    norm_act(act, lambda k: x_sb[:, k], 7, lambda k: shift[:, k:k + 1], hi=lambda k: hh[:, k])

                @block.tensor
                def _(pe):
                    norm_pe(pe, 7)

        midh = [tiles(f"midh{b}", 32 + 16 * b, KT, F32R) for b in range(2)]
        midl = [tiles(f"midl{b}", 40 + 16 * b, KT, F32R) for b in range(2)]
        relu, rsq = tiles("relu", 64, 4), tiles("rsq", 68, 4)

        def mlp_phase(layer):
            order = [("up", 0), ("up", 1), ("down", 0), ("up", 2), ("down", 1), ("up", 3), ("down", 2), ("down", 3)]
            names = [f"mlp{layer}_{j}" for j in range(8)]
            phase_start()
            with nc.Block() as block:
                @block.sync
                def _(sp):
                    load_weights(sp, ahead(*names)[0])

                @block.gpsimd
                def _(pool):
                    split_weights(pool, ahead(*names)[1])

                @block.tensor
                def _(pe):
                    for name, (what, q) in zip(names, order):
                        if what == "up":
                            linear(pe, name, hh, hl)
                        else:
                            pe.wait_ge(*PE.need(sem("mid_ready"), KT))
                            linear(pe, name, midh[q % 2], midl[q % 2])

                @block.scalar
                def _(act):
                    for what, q in order:
                        if what == "down":
                            AC.skip(acc_ready, KT)
                            for b in range(NACC):
                                AC.skip(acc_free[b], KT // NACC)
                            turn["evac"] += KT
                            continue

                        def four(e, i):
                            for j in range(4):
                                b = bank()
                                e.wait_ge(*AC.need(acc_ready))
                                e.activation(relu[:, j], ps[:, b], ACT.Relu).then_inc(*AC.up(acc_free[b]))
                                e.wait_ge(*AC.need(acc_free[b]))
                                for w in AC.again(sem("mid_ready")):
                                    e.wait_ge(*w)
                                e.activation(rsq[:, j], relu[:, j], ACT.Square).then_inc(*AC.up(sem("squared")))
                                e.wait_ge(*AC.last())
                                settle(e)
                                e.activation(one_of(midh[q % 2], 4 * i + j), rsq[:, j],
                                             ACT.Copy).then_inc(*AC.up(sem("mid_high")))
                        AC.loop(act, 2, four)

                @block.vector
                def _(dve):
                    for what, q in order:
                        if what == "down":
                            add_to_x(dve, lambda m: mod[layer][:, ds(40 + m, 1)])
                            continue
                        VE.skip(acc_ready, KT)
                        turn["evac"] += KT

                        def four(e, i):
                            for j in range(4):
                                e.wait_ge(*VE.need(sem("mid_high")))
                                e.tensor_tensor(one_of(midl[q % 2], 4 * i + j), rsq[:, j],
                                                one_of(midh[q % 2], 4 * i + j).bitcast(F32),
                                                ALU.subtract).then_inc(*VE.up(sem("mid_ready")))
                        VE.loop(dve, 2, four)

        norm_phase(1, mod[0][:, 24:32])
        mlp_phase(0)

        kk_sb, q_sb, g_sb = tiles("kk_sb", 32, KT), tiles("q_sb", 48, KT), tiles("g_sb", 56, KT)
        vtok = tiles("vtok", 40, shape=[P, 4, D])
        f16 = tiles("f16", 64, shape=[16, 4, T])
        fneg = tiles("fneg", 68, shape=[16, T])
        ftok = fixed("ftok", [P, 4, 16])
        norm_phase(4, kvm[:, 0:8])
        phase_start()
        with nc.Block() as block:
            names = ("kvk", "kvf", "kvv")

            @block.sync
            def _(sp):
                load_weights(sp, ahead(*names)[0])

            @block.gpsimd
            def _(pool):
                split_weights(pool, ahead(*names)[1])

            @block.tensor
            def _(pe):
                linear(pe, "kvk", hh, hl)
                block_of(pe, firsts["kvf"][1], 0, hh, hl, KT, P)
                for j in range(4):
                    tokens_of(pe, firsts["kvv"][1] + j, 0, hh, hl)

            @block.scalar
            def _(act):
                for k in range(KT):
                    b = bank()
                    act.wait_ge(*AC.need(acc_ready))
                    act.activation(kk_sb[:, k], ps[:, b], ACT.Copy).then_inc(*AC.up(acc_free[b]))
                b = bank()
                act.wait_ge(*AC.need(acc_ready))
                act.activation(f16[:, 0], ps[:16, b], ACT.Identity, bias=V("fb")[:16]).then_inc(*AC.up(acc_free[b]))
                act.wait_ge(*AC.last())
                act.activation(f16[:, 1], f16[:, 0], ACT.Abs).then_inc(*AC.up(sem("f_z")))
                act.wait_ge(*AC.last())
                act.activation(f16[:, 1], f16[:, 1], ACT.Exp, scale=-1.0).then_inc(*AC.up(sem("f_z")))
                act.wait_ge(*AC.last())
                act.activation(f16[:, 1], f16[:, 1], ACT.Ln, bias=1.0).then_inc(*AC.up(sem("f_z")))

            @block.vector
            def _(dve):
                VE.skip(acc_ready, KT + 1)
                chain = sem("dve")
                dve.memset(f16[:, 3], 1.0).then_inc(*VE.up(chain))
                dve.wait_ge(*VE.need(sem("f_z"), 3))
                dve.tensor_scalar(f16[:, 2], f16[:, 0], 0.0, None, ALU.min).then_inc(*VE.up(chain))
                dve.wait_ge(*VE.last())
                dve.tensor_tensor(f16[:, 2], f16[:, 2], f16[:, 1], ALU.subtract).then_inc(*VE.up(chain))
                dve.wait_ge(*VE.last())
                dve.tensor_tensor_scan(f16[:, 0], f16[:, 3], f16[:, 2], 0.0, ALU.mult, ALU.add).then_inc(*VE.up(chain))
                dve.wait_ge(*VE.last())
                dve.tensor_scalar(fneg[:], f16[:, 0], -1.0, None, ALU.mult).then_inc(*VE.up(chain))
                turn["evac"] = KT + 1
                for j in range(4):
                    for t in range(4):
                        b = bank()
                        dve.wait_ge(*VE.need(acc_ready))
                        dve.tensor_copy(vtok[:, t, 256 * j:256 * j + 256],
                                        ps[:, b, :256]).then_inc(*VE.up(acc_free[b]))

        norm_phase(2, mod[1][:, 0:8])
        phase_start()
        with nc.Block() as block:
            @block.sync
            def _(sp):
                load_weights(sp, ahead("fq")[0])

            @block.gpsimd
            def _(pool):
                split_weights(pool, ahead("fq")[1])

            @block.tensor
            def _(pe):
                linear(pe, "fq", hh, hl)

            @block.scalar
            def _(act):
                for to, func in ((q_sb, ACT.Copy), (g_sb, ACT.Sigmoid)):
                    def four(e, i):
                        for j in range(4):
                            b = bank()
                            e.wait_ge(*AC.need(acc_ready))
                            settle(e)
                            e.activation(one_of(to, 4 * i + j), ps[:, b], func).then_inc(*AC.up(acc_free[b]))
                    AC.loop(act, 2, four)

        fall = tiles("fall", 8, 16)
        qk_sq = tiles("qk_sq", 72, 2)
        qk_rms = tiles("qk_rms", 30, shape=[P, 2, 64])
        rows = tiles("rows", 26, shape=[16, 2, T])
        phase_start()
        with nc.Block() as block:
            @block.tensor
            def _(pe):
                for t in range(4):
                    o = pe.transpose(ps[:, 7, 16 * t:16 * t + 16], f16[:, 0, P * t:P * t + P], ident[:16, :16])
                o.then_inc(*PE.up(sem("f_turned")))

                def two_heads(e, i):
                    for j in range(2):
                        e.wait_ge(*PE.need(sem("qk_squared")))
                        for t in range(4):
                            o = e.matmul(ps[:, 5 + j, ds(2 * i + 16 * t, 2)], qk_sq[:, j, P * t:P * t + P],
                                         head[:, 0:P:64], start=True, stop=True)
                        o.then_inc(*PE.up(sem("qk_sum")))
                PE.loop(pe, KT, two_heads)
                for h in range(16):
                    for w in PE.again(acc_free[h % 4]):
                        pe.wait_ge(*w)
                    pe.matmul(ps[:, h % 4], ident[:16, h:h + 1].broadcast_to([16, P]), fneg[:], start=True,
                              stop=True).then_inc(*PE.up(acc_ready))
                pe.wait_ge(*PE.need(sem("qk_inverse")))
                for j in range(2):
                    for t in range(4):
                        o = pe.transpose(ps[:16, 5 + j, P * t:P * t + P], qk_rms[:, j, 16 * t:16 * t + 16], ident)
                    o.then_inc(*PE.up(sem("qk_rows")))

            @block.scalar
            def _(act):
                def two_heads(e, i):
                    for j, src in enumerate((q_sb, kk_sb)):
                        e.wait_ge(sem("qk_sum"), book.base[sem("qk_sum")] + 2 * i + j - 1)
                        settle(e)
                        e.activation(qk_sq[:, j], one_of(src, i), ACT.Square).then_inc(*AC.up(sem("qk_squared")))
                AC.loop(act, KT, two_heads)
                act.wait_ge(sem("qk_sum"), book.base[sem("qk_sum")] + 2 * KT)
                act.activation(qk_rms[:], ps[:, 5:7, :64], ACT.Sqrt, bias=C("epsn"),
                               scale=1.0 / 64).then_inc(*AC.up(sem("qk_rms")))
                for h in range(16):
                    act.wait_ge(*AC.need(acc_ready))
                    act.activation(fall[:, h], ps[:, h % 4], ACT.Copy).then_inc(*AC.up(acc_free[h % 4]))
                act.wait_ge(*AC.need(sem("qk_rows"), 2))
                act.activation(rows[:], ps[:16, 5:7], ACT.Copy).then_inc(*AC.up(sem("rows_ready")))

            @block.vector
            def _(dve):
                dve.wait_ge(*VE.need(sem("f_turned")))
                dve.tensor_copy(ftok[:], ps[:, 7, :64].rearrange("p (t h) -> p t h", h=16)).then_inc(*VE.up(sem("dve")))
                dve.wait_ge(*VE.need(sem("qk_rms")))
                dve.reciprocal(qk_rms[:], qk_rms[:]).then_inc(*VE.up(sem("qk_inverse")))

        qn, kn = tiles("qn", 24, shape=[P, T]), tiles("kn", 25, shape=[P, T])
        vp = tiles("vp", 28, shape=[P, 4, P])
        otile = tiles("otile", 29, shape=[P, T])
        sc, pr = tiles("sc", 64, 4), tiles("pr", 68, 2)
        ptr = tiles("ptr", 70, 4)
        oh, ol = tiles("oh", 48, KT, F32R), tiles("ol", 32, KT, F32R)
        sm = fixed("sm", [P, 4, 3])
        qgs = fixed("qgs", [P, 1])
        ftp = fixed("ftp", [P, 4, 2])
        pair_sel = fixed("pair_sel", [16, P])
        items = [(h, t) for h in range(2) for t in range(4)]
        NI = len(items)
        score_bank = [0, 1, 2, 0, 1, 2, 0, 1]
        phase_start()
        scored, read, turned_read = sem("scores"), sem("scores_read"), sem("turned_read")
        with nc.Block() as block:
            @block.tensor
            def _(pe):
                def prepare(e):
                    e.wait_ge(*PE.need(sem("pair_ready")))
                    for j, b in enumerate((3, 7)):
                        o = e.matmul(ps[:, b], pair_sel[:], rows[:, j], start=True, stop=True)
                    o.then_inc(*PE.up(sem("scale_ready")))
                    e.wait_ge(*PE.need(sem("qk_normed")))

                def scores(e, i, n, free=None):
                    h, t = items[n]
                    rr = slice(64 * h, 64 * h + 64)
                    if free is not None:
                        e.wait_ge(read, book.base.get(read, 0) + NI * i + free + 1)
                    e.matmul(ps[:, score_bank[n], :P * (t + 1)], qn[rr, P * t:P * t + P], kn[rr, :P * (t + 1)],
                             start=True, stop=True).then_inc(*PE.up(scored))

                def turned(e, i, n):
                    h, t = items[n]
                    e.wait_ge(*PE.need(sem("p_ready")))
                    if n >= 2:
                        e.wait_ge(turned_read, book.base.get(turned_read, 0) + NI * i + n - 1)
                    for s in range(t + 1):
                        o = e.transpose(ps[:, 4 + n % 2, P * s:P * s + P], pr[:, n % 2, P * s:P * s + P], ident)
                    o.then_inc(*PE.up(sem("p_turned")))

                def values(e, i, h):
                    rr = slice(64 * h, 64 * h + 64)
                    if h == 0:
                        e.wait_ge(*PE.need(sem("v_copied")))
                        e.wait_ge(sem("o_gated"), book.base.get(sem("o_gated"), 0) + 2 * i)
                    e.wait_ge(turned_read, book.base.get(turned_read, 0) + NI * i + 4 * h + 4)
                    for s in range(4):
                        o = e.matmul(ps[rr, 6, P * s:], vp[:, s, rr], ptr[:, s, P * s:], start=s == 0, stop=s == 3)
                    o.then_inc(*PE.up(sem("o_done")))

                def turn_of(e, i, more=True):
                    scores(e, i, 2)
                    for n in range(NI):
                        if n + 3 < NI:
                            scores(e, i, n + 3, n)
                        elif more and n == 5:
                            prepare(e)
                        elif more:
                            scores(e, i, n - 6, n)
                        if n == 4:
                            values(e, i, 0)
                        turned(e, i, n)
                    values(e, i, 1)
                prepare(pe)
                scores(pe, 0, 0)
                scores(pe, 0, 1)
                PE.loop(pe, KT - 1, turn_of)
                turn_of(pe, KT - 1, more=False)

            @block.scalar
            def _(act):
                def select(e, i):
                    for h in range(2):
                        src = ident[:16, ds(2 * i + h, 1)] if not isinstance(i, int) else ident[:16, 2 * i + h:2 * i + h + 1]
                        o = e.activation(pair_sel[:, 64 * h:64 * h + 64], src.broadcast_to([16, 64]), ACT.Copy)
                    o.then_inc(*AC.up(sem("pair_ready")))

                def exp(e, n):
                    h, t = items[n]
                    w = P * (t + 1)
                    e.wait_ge(*AC.need(sem("max_ready")))
                    e.activation(pr[:, n % 2, :w], sc[:, n % 4, :w], ACT.Exp, bias=sm[:, n % 4, 0:1],
                                 accum_out=sm[:, n % 4, 1:2]).then_inc(*AC.up(sem("exp_done")))

                def turn_of(e, i, more=True):
                    for n, (h, t) in enumerate(items):
                        if n + 1 < NI:
                            exp(e, n + 1)
                        elif more:
                            exp(e, 0)
                        e.wait_ge(*AC.need(sem("p_turned")))
                        e.activation(ptr[:, 0:t + 1, P * t:P * t + P], ps[:, 4 + n % 2, :P * (t + 1)].rearrange(
                            "p (s t) -> p s t", t=P), ACT.Copy).then_inc(*AC.up(turned_read))
                        if n == 0:
                            e.activation(vp[:], vtok[:, :, ds(i * P, P)], ACT.Copy).then_inc(*AC.up(sem("v_copied")))
                        if n == 1 and more:
                            select(e, i + 1)
                select(act, 0)
                exp(act, 0)
                AC.loop(act, KT - 1, turn_of)
                turn_of(act, KT - 1, more=False)

            @block.vector
            def _(dve):
                chain = sem("dve")
                dve.tensor_scalar(qgs[:], V("qg", 0), 0.125, None, ALU.mult).then_inc(*VE.up(chain))
                dve.wait_ge(*VE.last())

                def step(e, o, s=chain):
                    o.then_inc(*VE.up(s))
                    e.wait_ge(*VE.last())

                def prepare(e, i):
                    e.tensor_copy(ftp[:], ftok[:, :, ds(2 * i, 2)]).then_inc(*VE.up(chain))
                    e.wait_ge(*VE.need(sem("scale_ready")))
                    e.scalar_tensor_tensor(qn[:], one_of(q_sb, i), qgs[:, 0:1], ps[:, 3], ALU.mult,
                                           ALU.mult).then_inc(*VE.up(chain))
                    step(e, e.scalar_tensor_tensor(kn[:], one_of(kk_sb, i), V("kg", 0), ps[:, 7], ALU.mult,
                                                   ALU.mult), sem("qk_normed"))

                def softmax(e, i, n):
                    h, t = items[n]
                    k, w = n % 4, P * (t + 1)
                    e.wait_ge(*VE.need(scored))
                    step(e, e.scalar_tensor_tensor(sc[:, k, :w], ps[:, score_bank[n], :w], ftp[:, t, h:h + 1],
                                                   one_of(fall, 2 * i + h)[:, :w], ALU.add, ALU.add), read)
                    step(e, e.tensor_tensor(sc[:, k, P * t:w], sc[:, k, P * t:w], C("causal"), ALU.add))
                    e.tensor_reduce(sm[:, k, 0:1], sc[:, k, :w], AX.X, ALU.max,
                                    negate=True).then_inc(*VE.up(sem("max_ready")))

                def divide(e, n):
                    h, t = items[n]
                    k, w = n % 4, P * (t + 1)
                    e.wait_ge(*VE.need(sem("exp_done")))
                    step(e, e.reciprocal(sm[:, k, 2:3], sm[:, k, 1:2]))
                    e.tensor_scalar(pr[:, n % 2, :w], pr[:, n % 2, :w], sm[:, k, 2:3], None,
                                    ALU.mult).then_inc(*VE.up(sem("p_ready")))

                def gate(e, i, h):
                    rr = slice(64 * h, 64 * h + 64)
                    e.wait_ge(*VE.need(sem("o_done")))
                    step(e, e.tensor_tensor(otile[rr], ps[rr, 6], one_of(g_sb, i)[rr], ALU.mult), sem("o_gated"))

                def turn_of(e, i, more=True):
                    for n in range(NI):
                        divide(e, n)
                        if n + 2 < NI:
                            softmax(e, i, n + 2)
                        elif more:
                            softmax(e, i + 1, n - 6)
                        if n == 5 and more:
                            prepare(e, i + 1)
                        if n == 5:
                            gate(e, i, 0)
                    gate(e, i, 1)
                    step(e, e.tensor_copy(one_of(oh, i), otile[:]))
                    step(e, e.tensor_tensor(one_of(ol, i), otile[:], one_of(oh, i).bitcast(F32), ALU.subtract))
                prepare(dve, 0)
                softmax(dve, 0, 0)
                softmax(dve, 0, 1)
                VE.loop(dve, KT - 1, turn_of)
                turn_of(dve, KT - 1, more=False)

        phase_start()
        with nc.Block() as block:
            @block.sync
            def _(sp):
                load_weights(sp, ahead("fo")[0])

            @block.gpsimd
            def _(pool):
                split_weights(pool, ahead("fo")[1])

            @block.tensor
            def _(pe):
                linear(pe, "fo", oh, ol)

            @block.vector
            def _(dve):
                add_to_x(dve, lambda m: mod[1][:, ds(16 + m, 1)])
        norm_phase(3, mod[1][:, 24:32])
        mlp_phase(1)

        def plain_norm(x, g, out_tiles):
            phase_start()
            with nc.Block() as block:
                @block.vector
                def _(dve):
                    norm_dve(dve, lambda k: x[:, k], lambda k: g[:, k:k + 1],
                             plain=lambda k: out_tiles[:, k])

                @block.scalar
                def _(act):
                    norm_act(act, lambda k: x[:, k], 7)

                @block.tensor
                def _(pe):
                    norm_pe(pe, 7)
        plain_norm(x_sb, V("final"), x_sb)

        h2h, h2l = (tiles(n, a, dt=F32R, shape=[P, KT, TA]) for n, a in (("h2h", 8), ("h2l", 20)))
        sq, rms, nt = (tiles(n, 60 + 2 * j, 2) for j, n in enumerate(("sq2", "rms2", "nt2")))
        ctx_sb = tiles("ctx_sb", 56, shape=[P, KT, TX])
        LAT = slice(TX, TA)
        for src, gain_no, shift, part, n in ((x_sb, 5, ada0[:, 0, 0:8], LAT, T), (ctx_sb, 6, ada0[:, 1, 0:8],
                                                                                   slice(0, TX), TX)):
            phase_start()
            with nc.Block() as block:
                @block.vector
                def _(dve):
                    norm_dve(dve, lambda k: src[:, k], lambda k: coef[:, gain_no, k:k + 1],
                             lambda k: shift[:, k:k + 1], n=n, hi=lambda k: h2h[:, k, part],
                             lo=lambda k: h2l[:, k, part])

                @block.scalar
                def _(act):
                    norm_act(act, lambda k: src[:, k], 7, lambda k: shift[:, k:k + 1], n=n, hi=lambda k: h2h[:, k, part])
                    if n == T:
                        act.dma_start(ctx_sb[:], A["cT"]).then_inc(*AC.up16(sem("ctx_loaded")))
                        act.wait_ge(*AC.last())

                @block.tensor
                def _(pe):
                    norm_pe(pe, 7, n=n)

        xm, qx, kx2 = (tiles(n, a, shape=[P, 4, TA]) for n, a in (("xm", 32), ("qx", 55), ("kx2", 61)))
        xch, xcl = tiles("xch", 38, dt=F32R, shape=[P, 4, TA]), tiles("xcl", 44, dt=F32R, shape=[P, 4, TA])
        xc = tiles("xc", 50, shape=[P, 2, TA])
        gacc = tiles("gacc", 53, shape=[P, TA])
        rowt = fixed("rowt", [P, NACC])
        ssb = tiles("ssb", 67, 6)
        vsb = tiles("vsb", 38, 6)
        d_s = nc.dram_tensor("d_s", (4, P, 6, T), F32, kind="Internal").ap()
        d_v = nc.dram_tensor("d_v", (4, P, 6, T), F32, kind="Internal").ap()
        d_x = nc.dram_tensor("d_x", (4, P, 4, T), F32, kind="Internal").ap()
        d_h = nc.dram_tensor("d_h", (4, P, 4, T), F32, kind="Internal").ap()
        spans = ((0, TX), (TX, T))
        KS = 512 ** -0.5
        phase_start()
        with nc.Block() as block:
            names = [f"{n}{h}" for n in ("xm", "q", "k", "gate") for h in range(4)]

            @block.sync
            def _(sp):
                load_weights(sp, ahead(*names)[0])

            @block.gpsimd
            def _(pool):
                split_weights(pool, ahead(*names)[1])

            acc_taken, per_head = sem("acc_taken"), 36

            def taken(i, h, n):
                return acc_taken, book.base.get(acc_taken, 0) + NACC + per_head * (2 * i + h) + n + 1

            @block.tensor
            def _(pe):
                def two_heads(e, i):
                    for h in range(2):
                        q0 = firsts["xm0"][1] + 4 * h
                        r0 = firsts["xm0"][0] + 5 * h
                        n = [0]

                        def bank_free():
                            n[0] += 1
                            s_, v = taken(i, h, n[0] - 1)
                            return [(s_, v - NACC)]

                        def tile_bank():
                            b = turn["acc"] % NACC
                            turn["acc"] += 1
                            for w in bank_free():
                                e.wait_ge(*w)
                            return b
                        for j in range(2):
                            block_of(e, q0 + j, 8 * i, h2h, h2l, KT, 256, tokens=spans, bank_free=bank_free)
                        e.wait_ge(*PE.need(sem("xc_ready"), 4))
                        for j in (2, 3):
                            block_of(e, q0 + j, 8 * i, xch, xcl, 4, 512, tokens=spans, bank_free=bank_free)
                        for s in range(6):
                            b = tile_bank()
                            for m in range(4):
                                o = e.transpose(ps[:, b, P * m:P * m + P], xm[:, m, P * s:P * s + P], ident)
                            o.then_inc(*PE.up(acc_ready))
                        e.wait_ge(*taken(i, h, 23))
                        r = r0 + 4
                        e.wait_ge(w_full[r % RAW], (r // 2 + 1 + 5 * i) * 16)
                        for w in PE.again(sem("gates_read")):
                            e.wait_ge(*w)
                        wg = wraw[:, r % RAW, :12 * P].rearrange("p (k c) -> p k c", k=12)
                        for b, (t0, nt_) in zip((4, 5), spans):
                            for j, src in enumerate((qx, kx2, xm)):
                                for m in range(4):
                                    o = e.matmul(ps[:, b, :nt_], wg[:, 4 * j + m], src[:, m, t0:t0 + nt_],
                                                 start=j == 0 and m == 0, stop=j == 2 and m == 3)
                        o.then_inc(w_cond, 1)
                        for s in range(6):
                            b = tile_bank()
                            for m in range(4):
                                o = e.matmul(ps[:, b], kx2[:, m, P * s:P * s + P], qx[:, m, LAT], start=m == 0,
                                             stop=m == 3)
                            o.then_inc(*PE.up(acc_ready))
                PE.loop(pe, 2, two_heads)

            @block.scalar
            def _(act):
                for j in range(NACC):
                    act.activation(rowt[:, j:j + 1], con[:, 0:1], ACT.Copy).then_inc(*AC.up(acc_taken))

                def two_heads(e, i):
                    for h in range(2):
                        def read_out(dst, n, **kw):
                            b = bank()
                            e.wait_ge(*AC.need(acc_ready))
                            e.activation(dst, ps[:, b, :n], ACT.Copy, **kw).then_inc(*AC.up(acc_taken))

                        def silu(m):
                            e.wait_ge(*AC.need(sem("conv_done")))
                            bias = vec[:, ds(vat["convb"][0] + 4 * (2 * i + h) + m, 1)]
                            settle(e)
                            e.activation(xc[:, m % 2], xc[:, m % 2], ACT.Silu, bias=bias).then_inc(*AC.up(sem("silu")))
                            e.wait_ge(sem("silu"), book.base.get(sem("silu"), 0) + 4 * (2 * i + h) + m + 1)
                            e.dma_start(d_x[ds(2 * i + h, 1), :, m].rearrange("a p t -> (a p) t"),
                                        xc[:, m % 2, LAT]).then_inc(*AC.up16(sem(f"skip_sent{m % 2}")))
                            e.activation(xch[:, m], xc[:, m % 2], ACT.Copy).then_inc(*AC.up(sem("xc_high")))
                        for m in range(4):
                            for t0, n in spans:
                                read_out(xm[:, m, t0:t0 + n], n)
                            if m == 1 and (h or not isinstance(i, int)):
                                e.wait_ge(sem("v_sent"), book.base.get(sem("v_sent"), 0) + 16 * (2 * i + h))
                            if m:
                                silu(m - 1)
                        silu(3)
                        for to, f in ((qx, 1.0), (kx2, KS)):
                            for m in range(4):
                                for t0, n in spans:
                                    read_out(to[:, m, t0:t0 + n], n, scale=f)
                        for s in range(6):
                            read_out(vsb[:, s], T)
                        e.wait_ge(*taken(i, h, 29))
                        e.dma_start(d_v[ds(2 * i + h, 1)].rearrange("a p s t -> (a p) s t"),
                                    vsb[:]).then_inc(*AC.up16(sem("v_sent")))
                        if h or not isinstance(i, int):
                            e.wait_ge(sem("s_sent"), book.base.get(sem("s_sent"), 0) + 16 * (2 * i + h))
                        for s in range(6):
                            read_out(ssb[:, s], T)
                        e.wait_ge(*taken(i, h, 35))
                        e.dma_start(d_s[ds(2 * i + h, 1)].rearrange("a p s t -> (a p) s t"),
                                    ssb[:]).then_inc(*AC.up16(sem("s_sent")))
                AC.loop(act, 2, two_heads)
                act.wait_ge(sem("v_sent"), book.base[sem("v_sent")] + 64)
                act.wait_ge(sem("s_sent"), book.base[sem("s_sent")] + 64)
                act.wait_ge(sem("skip_sent0"), book.base[sem("skip_sent0")] + 128)
                act.wait_ge(sem("skip_sent1"), book.base[sem("skip_sent1")] + 128)

            @block.vector
            def _(dve):
                chain = sem("dve")
                dve.memset(gacc[:], 0.0).then_inc(*VE.up(chain))
                dve.wait_ge(*VE.last())

                def two_heads(e, i):
                    for h in range(2):
                        def conv(m):
                            at = vat["convw"][0] + 9 * (4 * (2 * i + h) + m)
                            e.wait_ge(*taken(i, h, 2 * m + 1))
                            if m >= 2 or h or not isinstance(i, int):
                                s_ = sem(f"skip_sent{m % 2}")
                                e.wait_ge(s_, book.base.get(s_, 0) + 16 * (2 * (2 * i + h) + m // 2))
                            first = [True]

                            def tap(kh, kw, dst, src, center=False):
                                w = vec[:, ds(at + 3 * kh + kw, 1)]
                                if not first[0]:
                                    e.wait_ge(*VE.last())
                                if center:
                                    o = e.tensor_scalar(dst, src, w, None, ALU.mult)
                                else:
                                    o = e.scalar_tensor_tensor(dst, src, w, dst, ALU.mult, ALU.add)
                                first[0] = False
                                return o
                            y, z = xc[:, m % 2], xm[:, m]
                            tap(1, 1, y, z, True).then_inc(*VE.up(chain))
                            tap(1, 0, y[:, 1:TX], z[:, 0:TX - 1]).then_inc(*VE.up(chain))
                            tap(1, 2, y[:, 0:TX - 1], z[:, 1:TX]).then_inc(*VE.up(chain))
                            yg_ = y[:, LAT].rearrange("p (r c) -> p r c", c=64)
                            zg = z[:, LAT].rearrange("p (r c) -> p r c", c=64)
                            taps = [(a, b) for a in range(3) for b in range(3) if (a, b) != (1, 1)]
                            for kh, kw in taps:
                                r0, r1 = max(0, 1 - kh), 8 - max(0, kh - 1)
                                c0, c1 = max(0, 1 - kw), 64 - max(0, kw - 1)
                                o = tap(kh, kw, yg_[:, r0:r1, c0:c1],
                                        zg[:, r0 + kh - 1:r1 + kh - 1, c0 + kw - 1:c1 + kw - 1])
                                o.then_inc(*VE.up(sem("conv_done") if (kh, kw) == (2, 2) else chain))

                        def low(m):
                            e.wait_ge(*VE.need(sem("xc_high")))
                            e.tensor_tensor(xcl[:, m], xc[:, m % 2], xch[:, m].bitcast(F32),
                                            ALU.subtract).then_inc(*VE.up(sem("xc_ready")))
                            e.wait_ge(*VE.last())
                        conv(0)
                        conv(1)
                        low(0)
                        conv(2)
                        low(1)
                        conv(3)
                        low(2)
                        low(3)
                        e.wait_ge(w_cond, firsts["gate0"][1] + 2 * i + h + 1)
                        e.tensor_tensor(gacc[:, :TX], gacc[:, :TX], ps[:, 4, :TX], ALU.add).then_inc(*VE.up(chain))
                        e.tensor_tensor(gacc[:, LAT], gacc[:, LAT], ps[:, 5],
                                        ALU.add).then_inc(*VE.up(sem("gates_read")))
                        e.wait_ge(*VE.last())
                VE.loop(dve, 2, two_heads)

        gz, gl = tiles("gz", 55, shape=[P, TA]), tiles("gl", 57, shape=[P, TA])
        li, lf, bcum, gdir, mrun = (tiles(n, 59 + 3 * j, shape=[4, 2, TA]) for j, n in enumerate(
            ("li", "lf", "bcum", "gdir", "mrun")))
        one4 = tiles("one4", 50, shape=[4, TA])
        gnat = tiles("gnat", 32, shape=[4, 2, TA])
        nrow = tiles("nrow", 35, shape=[36, 2, T])
        nmax, nm = nrow[0:4], nrow[32:36]
        d_keep = nc.dram_tensor("d_keep", (P, KT, T), F32, kind="Internal").ap()
        gcol = fixed("gcol", [P, 2, 6, 4])
        phase_start()
        with nc.Block() as block:
            @block.sync
            def _(sp):
                sp.dma_start(d_keep, x_sb[:]).then_inc(*SP.up16(sem("x_kept")))
                sp.wait_ge(*SP.need(sem("x_kept"), 16))

            @block.scalar
            def _(act):
                act.wait_ge(*AC.need(sem("gz_ready")))
                act.activation(gl[:], gz[:], ACT.Abs).then_inc(*AC.up(sem("gl")))
                act.wait_ge(*AC.last())
                act.activation(gl[:], gl[:], ACT.Exp, scale=-1.0).then_inc(*AC.up(sem("gl")))
                act.wait_ge(*AC.last())
                act.activation(gl[:], gl[:], ACT.Ln, bias=1.0).then_inc(*AC.up(sem("gl")))

            @block.vector
            def _(dve):
                def step(o, s=None):
                    o.then_inc(*VE.up(s or sem("dve")))
                    dve.wait_ge(*VE.last())
                step(dve.tensor_scalar(gz[:], gacc[:], V("bif", 0), None, ALU.add), sem("gz_ready"))
                dve.memset(one4[:], 1.0).then_inc(*VE.up(sem("dve")))
                dve.wait_ge(*VE.need(sem("gl"), 3))
                step(dve.tensor_scalar(gacc[:], gz[:], 0.0, None, ALU.min))
                step(dve.tensor_tensor(gl[:], gacc[:], gl[:], ALU.subtract))

                def ordered(dst, src, d, parts=((0, TX), (TX, TA))):
                    for a, b in parts:
                        view = src[:, a:b]
                        step(dve.tensor_copy(dst[:, a:b], view[:, ::-1] if d else view))
                for d in range(2):
                    ordered(li[:, d], gz[64 * d:64 * d + 4], d)
                    ordered(lf[:, d], gl[64 * d + 32:64 * d + 36], d)
                    step(dve.tensor_tensor_scan(bcum[:, d], one4[:], lf[:, d], 0.0, ALU.mult, ALU.add))
                    step(dve.tensor_tensor(gdir[:, d], li[:, d], bcum[:, d], ALU.subtract))
                    step(dve.tensor_tensor_scan(mrun[:, d], gdir[:, d], gdir[:, d], 0.0, ALU.max, ALU.max))
                    step(dve.tensor_tensor(li[:, d], bcum[:, d], mrun[:, d], ALU.add))
                    ordered(gnat[:, d], gdir[:, d], d)
                    for dst, src in ((nmax, mrun), (nm, li)):
                        view = src[:, d, LAT]
                        step(dve.tensor_scalar(dst[:, d], view[:, ::-1] if d else view, -1.0, None, ALU.mult),
                             sem("gate_rows"))
                dve.wait_ge(*VE.need(sem("g_turned")))
                dve.tensor_copy(gcol[:].rearrange("p d s h -> p (d s h)"), ps[:, 7, :48]).then_inc(*VE.up(sem("dve")))

            @block.tensor
            def _(pe):
                pe.wait_ge(*PE.need(sem("gate_rows"), 4))
                for d in range(2):
                    for s in range(6):
                        o = pe.transpose(ps[:, 7, 24 * d + 4 * s:24 * d + 4 * s + 4], gnat[:, d, P * s:P * s + P],
                                         ident[:4, :4])
                o.then_inc(*PE.up(sem("g_turned")))

        sld, vld, pp = tiles("sld", 40, 6), tiles("vld", 46, 6), tiles("pp", 64, 6)
        sw = tiles("swf", 52, 6), tiles("swr", 58, 6)
        mb = tiles("mb", 32, 2)
        em = tiles("em", 6, 2)
        wt, hsq = tiles("wt", 4, 2), tiles("hsq", 38, 2)
        dev = tiles("dev", 34, 1)
        hb = tiles("hb0", 0, 4), tiles("hb1", 70, 4)
        HM = 4

        def region(d, s):
            if s < 2:
                return 0, T
            return (P * (s - 2), T) if d == 0 else (0, P * (s - 1))
        parts = [(s, d) for s in range(6) for d in range(2)]
        phase_start()
        with nc.Block() as block:
            @block.sync
            def _(sp):
                for i in range(HM):
                    if i:
                        sp.wait_ge(*SP.need(sem("sw_ready"), len(parts)))
                    sp.dma_start(sld[:], d_s[i]).then_inc(*SP.up16(sem("s_in")))
                    for m in range(4):
                        if i:
                            sp.wait_ge(*SP.need(sem("h_done")))
                        sp.dma_start(vld[:, :, P * m:P * m + P],
                                     d_v[i, :, :, P * m:P * m + P]).then_inc(*SP.up16(sem(f"v_in{m}")))

            @block.tensor
            def _(pe):
                def spread(i, n):
                    if n == 0 and i >= 2:
                        pe.wait_ge(*PE.need(sem("h_dev")))
                    if n >= 2 or (i == 1 and n == 0):
                        pe.wait_ge(*PE.need(sem("spread_taken"), 1 if n else 2))
                    rr = slice(32 * (n // 2), 32 * (n // 2) + 4)
                    one = ident[rr, 32 * (n // 2) + i:32 * (n // 2) + i + 1].broadcast_to([4, P])
                    pe.matmul(ps[:, 6 + n % 2], one, nrow[rr, n % 2], start=True, stop=True).then_inc(*PE.up(sem("spread")))

                def sums(i, some):
                    for s, d in some:
                        t0, t1 = region(d, s)
                        if i and (s, d) == (0, 0):
                            pe.wait_ge(*PE.need(sem("den_abs"), 2))
                        pe.wait_ge(*PE.need(sem("sw_ready")))
                        o = pe.matmul(ps[:, 4 + d, t0:t1], ones, sw[d][:, s, t0:t1], start=s == 0, stop=s == 5)
                        if s == 5:
                            o.then_inc(*PE.up(sem("den")))

                def values(m):
                    pe.wait_ge(*PE.need(sem(f"v_in{m}"), 16))
                    for s in range(6):
                        if m == 0:
                            pe.wait_ge(*PE.need(sem("p_ready2")))
                        o = pe.matmul(ps[:, m], vld[:, s, P * m:P * m + P], pp[:, s], start=s == 0, stop=s == 5)
                    o.then_inc(*PE.up(sem("h_done")))
                for n in range(4):
                    spread(0, n)
                sums(0, parts)
                for i in range(HM):
                    more = i + 1 < HM
                    if more:
                        spread(i + 1, 0)
                        spread(i + 1, 1)
                    values(0)
                    if more:
                        spread(i + 1, 2)
                        spread(i + 1, 3)
                    values(1)
                    if more:
                        sums(i + 1, parts[:6])
                    values(2)
                    if more:
                        sums(i + 1, parts[6:])
                    values(3)
                    pe.wait_ge(*(PE.need(sem("spread_taken"), 2) if more else PE.need(sem("h_dev"))))
                    for m in range(4):
                        pe.wait_ge(*PE.need(sem("h_taken")))
                        o = pe.matmul(ps[:, 6], ones, hb[i % 2][:, m], start=m == 0, stop=m == 3)
                    o.then_inc(*PE.up(sem("h_sum")))
                    for m in range(4):
                        pe.wait_ge(*PE.need(sem("h_squared")))
                        pe.matmul(ps[:, 7], ones, hsq[:, m % 2], start=m == 0,
                                  stop=m == 3).then_inc(*PE.up(sem("h_square_used")))

            @block.scalar
            def _(act):
                def spread_taken(n):
                    act.wait_ge(*AC.need(sem("spread")))
                    if n < 2:
                        act.activation(mb[:, n], ps[:, 6 + n], ACT.Copy).then_inc(*AC.up(sem("spread_taken")))
                    else:
                        act.activation(em[:, n - 2], ps[:, 4 + n], ACT.Exp).then_inc(*AC.up(sem("spread_taken")))

                def exps(a, b):
                    for n in range(a, b):
                        t0, t1 = region(parts[n][1], parts[n][0])
                        act.wait_ge(*AC.need(sem("w_log")))
                        act.activation(wt[:, n % 2, t0:t1], wt[:, n % 2, t0:t1], ACT.Exp).then_inc(*AC.up(sem("w_exp")))

                def magnitudes():
                    for d in range(2):
                        act.wait_ge(*AC.need(sem("den")))
                        act.activation(mb[:, d], ps[:, 4 + d], ACT.Abs).then_inc(*AC.up(sem("den_abs")))

                def result(i, m):
                    if m == 0 and i >= 2:
                        act.wait_ge(*AC.need(sem("h_sent"), 16))
                    act.wait_ge(*AC.need(sem("h_done")))
                    act.activation(hb[i % 2][:, m], ps[:, m], ACT.Copy).then_inc(*AC.up(sem("h_taken")))

                def send(i):
                    act.wait_ge(*AC.need(sem("h_normed")))
                    act.dma_start(d_h[i], hb[i % 2][:]).then_inc(*AC.up16(sem("h_sent")))
                for n in range(4):
                    spread_taken(n)
                exps(0, 12)
                magnitudes()
                for i in range(HM):
                    more = i + 1 < HM
                    if more:
                        act.wait_ge(*AC.need(sem("divisors")))
                        spread_taken(0)
                        spread_taken(1)
                        exps(0, 4)
                    result(i, 0)
                    if more:
                        act.wait_ge(*AC.need(sem("p_ready2"), 6))
                        spread_taken(2)
                        spread_taken(3)
                        exps(4, 12)
                    if i:
                        send(i - 1)
                    result(i, 1)
                    result(i, 2)
                    if more:
                        magnitudes()
                    result(i, 3)
                    for m in range(4):
                        act.wait_ge(*AC.need(sem("h_centred")))
                        if m >= 2:
                            act.wait_ge(*AC.need(sem("h_square_used")))
                        act.activation(hsq[:, m % 2], hb[i % 2][:, m], ACT.Square).then_inc(*AC.up(sem("h_squared")))
                    act.wait_ge(*AC.need(sem("h_square_used"), 2))
                    act.activation(dev[:, 0], ps[:, 7], ACT.Sqrt, bias=C("epsn"),
                                   scale=1.0 / 512).then_inc(*AC.up(sem("h_dev")))
                send(HM - 1)
                act.wait_ge(*AC.need(sem("h_sent"), 32))

            @block.vector
            def _(dve):
                def step(o, s=None):
                    o.then_inc(*VE.up(s or sem("dve")))
                    dve.wait_ge(*VE.last())

                def weights(i):
                    dve.wait_ge(*VE.need(sem("spread_taken"), 2))
                    dve.wait_ge(*VE.need(sem("s_in"), 16))

                    def log_weight(n):
                        s, d = parts[n]
                        t0, t1 = region(d, s)
                        dve.tensor_scalar(wt[:, n % 2, t0:t1], mb[:, d, t0:t1], gcol[:, d, s, i:i + 1], 0.0, ALU.add,
                                          ALU.min).then_inc(*VE.up(sem("w_log")))
                    log_weight(0)
                    for n, (s, d) in enumerate(parts):
                        t0, t1 = region(d, s)
                        if n + 1 < len(parts):
                            log_weight(n + 1)
                        dve.wait_ge(*VE.need(sem("w_exp")))
                        if s >= 2:
                            diag = slice(P * (s - 2), P * (s - 1))
                            step(dve.tensor_tensor(wt[:, n % 2, diag], wt[:, n % 2, diag], C(("fwd", "rev")[d]), ALU.mult))
                        step(dve.tensor_tensor(sw[d][:, s, t0:t1], wt[:, n % 2, t0:t1], sld[:, s, t0:t1], ALU.mult),
                             sem("sw_ready"))

                def divisors():
                    dve.wait_ge(*VE.need(sem("spread_taken"), 2))
                    for d in range(2):
                        dve.wait_ge(*VE.need(sem("den_abs")))
                        step(dve.tensor_tensor(em[:, d], em[:, d], mb[:, d], ALU.max))
                        step(dve.reciprocal(em[:, d], em[:, d]), sem("divisors") if d else None)

                def divided(last_values):
                    if last_values:
                        dve.wait_ge(*VE.need(sem("h_done"), 4))

                    for s in range(6):
                        f0, r1 = region(0, s)[0], region(1, s)[1]
                        step(dve.tensor_tensor(pp[:, s, f0:], sw[0][:, s, f0:], em[:, 0, f0:], ALU.mult))
                        if f0:
                            dve.tensor_tensor(pp[:, s, :f0], sw[1][:, s, :f0], em[:, 1, :f0],
                                              ALU.mult).then_inc(*VE.up(sem("dve")))
                        step(dve.tensor_tensor(sw[1][:, s, f0:r1], sw[1][:, s, f0:r1], em[:, 1, f0:r1], ALU.mult))
                        dve.tensor_tensor(pp[:, s, f0:r1], pp[:, s, f0:r1], sw[1][:, s, f0:r1],
                                          ALU.add).then_inc(*VE.up(sem("p_ready2")))

                def normed(i):
                    dve.wait_ge(*VE.need(sem("h_dev")))
                    step(dve.reciprocal(dev[:, 0], dev[:, 0]))
                    for m in range(4):
                        o = dve.scalar_tensor_tensor(hb[i % 2][:, m], hb[i % 2][:, m], V("lnw2", 4 * i + m),
                                                     dev[:, 0], ALU.mult, ALU.mult)
                        o.then_inc(*VE.up(sem("h_normed") if m == 3 else sem("dve")))
                weights(0)
                divisors()
                for i in range(HM):
                    divided(i > 0)
                    if i:
                        normed(i - 1)
                    if i + 1 < HM:
                        weights(i + 1)
                        divisors()
                    dve.wait_ge(*VE.need(sem("h_sum")))
                    for m in range(4):
                        dve.scalar_tensor_tensor(hb[i % 2][:, m], ps[:, 6], -1.0 / 512, hb[i % 2][:, m], ALU.mult,
                                                 ALU.add).then_inc(*VE.up(sem("h_centred")))
                    dve.wait_ge(*VE.last())
                normed(HM - 1)

        y_sb = tiles("y_sb", 32, 16)
        skip_sb = tiles("skip_sb", 48, 16)
        yh, yl = tiles("yh", 48, 16, F32R), tiles("yl", 32, 16, F32R)
        gt_, yz = tiles("gt_", 64, 4), tiles("yz", 68, 4)

        def gated(e, func, free=None):
            for j in range(4):
                b = bank()
                for w in free(j) if free else ():
                    e.wait_ge(*w)
                e.wait_ge(*AC.need(acc_ready))
                e.activation(gt_[:, j], ps[:, b], func).then_inc(*AC.up(acc_free[b]))

        phase_start()
        with nc.Block() as block:
            names = ("o",)

            @block.sync
            def _(sp):
                for h in range(4):
                    sp.dma_start(y_sb[:, 4 * h:4 * h + 4], d_h[h]).then_inc(*SP.up16(sem(f"y_in{h}")))
                    sp.dma_start(skip_sb[:, 4 * h:4 * h + 4], d_x[h]).then_inc(*SP.up16(sem(f"skip_in{h}")))
                sp.dma_start(x_sb[:], d_keep).then_inc(*SP.up16(sem("x_back")))
                load_weights(sp, ahead("o")[0])
                sp.wait_ge(*SP.need(sem("x_back"), 16))
                for h in range(4):
                    sp.wait_ge(*SP.need(sem(f"y_in{h}"), 16))
                    sp.wait_ge(*SP.need(sem(f"skip_in{h}"), 16))

            @block.gpsimd
            def _(pool):
                split_weights(pool, ahead("o")[1])

            @block.tensor
            def _(pe):
                linear(pe, "o", h2h, h2l, tokens=((TX, T),))

            @block.scalar
            def _(act):
                AC.loop(act, 4, lambda e, i: gated(e, ACT.Sigmoid, lambda j: AC.again(sem(f"gt_used{j}"))))

            @block.vector
            def _(dve):
                for h in range(4):
                    dve.wait_ge(*VE.need(sem(f"y_in{h}"), 16))
                    dve.wait_ge(*VE.need(sem(f"skip_in{h}"), 16))

                def four(e, i):
                    for j in range(4):
                        y = one_of(y_sb, 4 * i + j)
                        e.wait_ge(*VE.need(acc_free[j]))
                        e.tensor_tensor(y, y, gt_[:, j], ALU.mult).then_inc(*VE.up(sem(f"gt_used{j}")))
                        e.wait_ge(*VE.last())
                        e.scalar_tensor_tensor(y, one_of(skip_sb, 4 * i + j), vec[:, ds(vat["skip"][0] + 4 * i + j, 1)],
                                               y, ALU.mult, ALU.add).then_inc(*VE.up(sem("dve")))
                VE.loop(dve, 4, four)

        def silu_phase(name, xhi, xlo, **kw):
            phase_start()
            with nc.Block() as block:
                @block.sync
                def _(sp):
                    load_weights(sp, ahead(name)[0])

                @block.gpsimd
                def _(pool):
                    split_weights(pool, ahead(name)[1])

                @block.tensor
                def _(pe):
                    linear(pe, name, xhi, xlo, **kw)

                @block.scalar
                def _(act):
                    def four(e, i):
                        gated(e, ACT.Silu)
                        for j in range(4):
                            e.wait_ge(*AC.need(sem(f"gated{j}")))
                            settle(e)
                            e.activation(one_of(yh, 4 * i + j), yz[:, j], ACT.Copy).then_inc(*AC.up(sem("y_high")))
                    AC.loop(act, 4, four)

                @block.vector
                def _(dve):
                    def four(e, i):
                        for j in range(4):
                            e.wait_ge(*VE.need(acc_free[j]))
                            e.tensor_tensor(yz[:, j], one_of(y_sb, 4 * i + j), gt_[:, j],
                                            ALU.mult).then_inc(*VE.up(sem(f"gated{j}")))
                        for j in range(4):
                            e.wait_ge(*VE.need(sem("y_high")))
                            e.tensor_tensor(one_of(yl, 4 * i + j), yz[:, j], one_of(yh, 4 * i + j).bitcast(F32),
                                            ALU.subtract).then_inc(*VE.up(sem("dve")))
                        e.wait_ge(*VE.last())
                    VE.loop(dve, 4, four)

        def wide_out(name, gate):
            phase_start()
            with nc.Block() as block:
                @block.sync
                def _(sp):
                    load_weights(sp, ahead(name)[0])

                @block.gpsimd
                def _(pool):
                    split_weights(pool, ahead(name)[1])

                @block.tensor
                def _(pe):
                    q = firsts[name][1]

                    def pair(e, i):
                        for j in range(2):
                            open_bank = {}
                            for k in range(2):
                                block_of(e, q + 2 * j + k, 4 * i, yh, yl, KT, 256, k0=KT * k, first=k == 0,
                                         final=k == 1, open_bank=open_bank)
                    PE.loop(pe, 2, pair)

                @block.vector
                def _(dve):
                    add_to_x(dve, gate)
        silu_phase("z", h2h, h2l, tokens=((TX, T),))
        wide_out("mo", lambda m: ada0[:, 0, ds(16 + m, 1)])

        dch, dtok = tiles("dch", 24, shape=[P, 2, 512]), tiles("dtok", 64, shape=[P, 2, 4, T])
        u_sb, ucs = tiles("u_sb", 26, 4), tiles("ucs", 48, 8)
        sq, rms, nt = (tiles(n, 24 + 2 * j, 2) for j, n in enumerate(("sq", "rms", "nt")))
        norm_phase(7, ada1[:, 0:8])
        phase_start()
        with nc.Block() as block:
            f_taken, per_turn = sem("f_taken"), 16

            def ftaken(i, n):
                return f_taken, book.base.get(f_taken, 0) + NACC + per_turn * i + n + 1

            @block.sync
            def _(sp):
                sp.dma_start(dch[:].rearrange("p a c -> p (a c)"), A["dch"]).then_inc(*SP.up16(sem("dch_in")))
                sp.dma_start(dtok[:].rearrange("p a b c -> p (a b c)"), A["dtok"]).then_inc(*SP.up16(sem("dtok_in")))
                load_weights(sp, ahead("fu")[0])

            @block.gpsimd
            def _(pool):
                split_weights(pool, ahead("fu")[1])

            @block.tensor
            def _(pe):
                pe.wait_ge(*PE.need(sem("dch_in"), 16))
                pe.wait_ge(*PE.need(sem("dtok_in"), 16))

                def two_groups(e, i):
                    made, seen = [0], [-NACC - 1]

                    def wait_taken(n):
                        if n > seen[0]:
                            e.wait_ge(*ftaken(i, n))
                            seen[0] = n

                    def bank_free():
                        made[0] += 1
                        seen[0] = made[0] - 1 - NACC
                        return [ftaken(i, seen[0])]

                    def tile_bank(operand):
                        b = turn["acc"] % NACC
                        turn["acc"] += 1
                        made[0] += 1
                        wait_taken(max(made[0] - 1 - NACC, operand))
                        return b
                    for h in range(2):
                        block_of(e, firsts["fu"][1] + h, 2 * i, hh, hl, KT, 256, bank_free=bank_free)
                    for h in range(2):
                        for t in range(4):
                            b = tile_bank(2 * h + 1)
                            for k in range(2):
                                o = e.matmul(ps[:, b], u_sb[:, 2 * h + k, P * t:P * t + P], dch[:, k], start=k == 0,
                                             stop=k == 1)
                            o.then_inc(*PE.up(acc_ready))
                    for h in range(2):
                        for m in range(2):
                            b = tile_bank(4 + 4 * h)
                            for t in range(4):
                                wait_taken(4 + 4 * h + t)
                                for c in range(2):
                                    o = e.matmul(ps[:, b], ucs[:, 4 * h + t, 256 * c + P * m:256 * c + P * m + P],
                                                 dtok[:, c, t], start=t == 0 and c == 0, stop=t == 3 and c == 1)
                            o.then_inc(*PE.up(acc_ready))
                PE.loop(pe, 4, two_groups)

            @block.scalar
            def _(act):
                for j in range(NACC):
                    act.activation(rowt[:, j:j + 1], con[:, 0:1], ACT.Copy).then_inc(*AC.up(f_taken))

                def two_groups(e, i):
                    for n in range(per_turn):
                        b = bank()
                        e.wait_ge(*AC.need(acc_ready))
                        if n < 4:
                            to = u_sb[:, n]
                        elif n < 12:
                            to = ucs[:, n - 4]
                        else:
                            to = one_of(y_sb, 4 * i + n - 12)
                            settle(e)
                        e.activation(to, ps[:, b], ACT.Copy).then_inc(*AC.up(f_taken))
                AC.loop(act, 4, two_groups)
        silu_phase("fz", hh, hl)
        wide_out("fo2", lambda m: ada1[:, ds(16 + m, 1)])
        res = tiles("res", 32, KT)
        plain_norm(x_sb, V("normf"), res)

        phase_start()
        with nc.Block() as block:
            @block.sync
            def _(sp):
                sp.dma_start(out, res[:]).then_inc(*SP.up16(sem("out_written")))
                sp.wait_ge(*SP.need(sem("out_written"), 16))


def kernel(**inputs):
    import concourse.bacc as bacc
    from concourse.bass_utils import run_bass_kernel_spmd

    x = {k: np.asarray(v) for k, v in inputs.items()}
    arrays, plan, vat, cat = layout(x)
    nc = bacc.Bacc("TRN2", target_bir_lowering=False, num_devices=1)
    A = {n: nc.dram_tensor(n, a.shape, F32, kind="ExternalInput").ap() for n, a in arrays.items()}
    out = nc.dram_tensor("out", (P, KT, T), F32, kind="ExternalOutput").ap()
    program(nc, A, out, plan, vat, cat)
    r = run_bass_kernel_spmd(nc, [arrays], core_ids=[0])
    got = np.asarray(r.results[0]["out"])
    return np.ascontiguousarray(got.transpose(2, 1, 0).reshape(1, T, D))
```

```python
from contextlib import ExitStack

import numpy as np

import concourse.bass as bass
from concourse import mybir

F32 = mybir.dt.float32
F32R = mybir.dt.float32r
ACT = mybir.ActivationFunctionType
ALU = mybir.AluOpType
AX = mybir.AxisListType
ds = bass.ds

P = 128
T = 512
D = 1024
KT = D // P
TX = 256
TA = TX + T
NF = 4 * D // P
E2 = 2048
ET = E2 // P
CH = 64
NC = T // CH
BLK = 2048
RAW, SPL = 2, 2
COND_TURN = 10
NACC = 4
LAGGED = (*(f"{n}{j}" for n in ("kk_squared", "kk_summed", "scale_used", "centred", "bonus_used", "y_summed")
            for j in range(2)), "scale_spread",
          *(f"acc_free{b}" for b in range(NACC)), "mat_by_act", "mat_by_dve", "mid_ready", "qk_sum", "qk_sum",
          "o_gated", "gt_used0", "gt_used1", "gt_used2", "gt_used3")
HALF = 0.6065306597126334
NORM_EPS, GN_EPS = 1e-6, 64e-5


def cols(v):
    return np.ascontiguousarray(np.asarray(v).reshape(-1, P).T)


def blocks(w, width=256, kt=8):
    w = np.asarray(w)
    rows, n = w.shape
    b = w.reshape(rows // (P * kt), kt, P, n // width, width).transpose(3, 0, 2, 1, 4)
    b = b.reshape(-1, P, kt * width)
    out = np.zeros((b.shape[0], P, BLK), w.dtype)
    out[:, :, :kt * width] = b
    return out


def padded(w, rows, n):
    out = np.zeros((rows, n), np.asarray(w).dtype)
    out[:w.shape[0], :w.shape[1]] = w
    return out


def stream(x):
    def mlp(i):
        up, down = x["mlp_up"][i], x["mlp_down"][i]
        u = [blocks(up[:, D * q:D * (q + 1)]) for q in range(4)]
        d = [blocks(down[D * q:D * (q + 1)]) for q in range(4)]
        return [u[0], u[1], d[0], u[2], d[1], u[3], d[2], d[3]]
    lora_w = np.zeros((1, P, BLK), np.float32)
    lora_w[0, :64, :D] = x["rw_w2"][0]
    lora_w[0, 64:, D:] = x["rw_a2"][0]
    a1 = np.zeros((D, P), np.float32)
    a1[:, 64:] = x["rw_a1"][0]
    seq = [("raw", "mod0", blocks(x["mod_w"][0][:, :2 * D])),
           ("split", "wr", blocks(x["rw_wr"][0])),
           ("split", "w1", blocks(padded(x["rw_w1"][0], D, P), P)),
           ("split", "a1", blocks(a1, P)),
           ("split", "wk", blocks(x["rw_wk"][0])),
           ("split", "wv", blocks(x["rw_wv"][0])),
           ("split", "w2a2", lora_w),
           ("split", "g1", blocks(padded(x["rw_g1"][0], D, 256))),
           ("raw", "mod0b", blocks(x["mod_w"][0][:, 2 * D:])),
           ("raw", "mod1", blocks(x["mod_w"][1])),
           ("raw", "kvm", blocks(x["kv_mod_w"])),
           ("raw", "ada0", blocks(x["w_ada_2"][0])),
           ("raw", "ada1", blocks(x["w_ada_2"][1])),
           ("raw", "ada0c", blocks(x["w_ada_2"][0][:, :2 * D])),
           ("split", "g2", blocks(padded(x["rw_g2"][0], 256, D), D, 2)),
           ("split", "wo", blocks(x["rw_wo"][0]))]
    seq += [("split", f"mlp0_{j}", b) for j, b in enumerate(mlp(0))]
    kv = x["kv_w"]
    wqg = x["fx_wqg"][0]
    seq += [("split", "kvk", blocks(kv[:, :D])),
            ("split", "kvf", blocks(padded(kv[:, 2 * D:], D, P), P)),
            ("split", "kvv", blocks(kv[:, D:2 * D])),
            ("split", "fq", blocks(wqg)),
            ("split", "fo", blocks(x["fx_wo"][0]))]
    seq += [("split", f"mlp1_{j}", b) for j, b in enumerate(mlp(1))]
    w_in = x["m_w_in_2"][0]
    wif = np.asarray(x["m_w_if_2"][0])
    seq.append(("split", "xm0", blocks(w_in[:, :512])))
    for h in range(4):
        c, after = slice(512 * h, 512 * (h + 1)), slice(512 * (h + 1), 512 * (h + 2))
        gate = np.zeros((1, P, 12, P), wif.dtype)
        for t in range(3):
            for d in range(2):
                part = wif[d, t, c].reshape(4, P, 8).transpose(1, 0, 2)
                gate[0, :, 4 * t:4 * t + 4, 64 * d:64 * d + 4] = part[:, :, :4]
                gate[0, :, 4 * t:4 * t + 4, 64 * d + 32:64 * d + 36] = part[:, :, 4:]
        g = np.zeros((1, P, BLK), wif.dtype)
        g[:, :, :12 * P] = gate.reshape(1, P, -1)
        if h < 3:
            seq.append(("split", f"xm{h + 1}", blocks(w_in[:, after])))
        seq += [("split", f"q{h}", blocks(x["m_w_q_2"][0, h], 512, 4)),
                ("split", f"k{h}", blocks(x["m_w_k_2"][0, h], 512, 4)),
                ("raw", f"gate{h}", g)]
    f_in = x["f_w_in_2"][0]
    seq += [("split", "o", blocks(w_in[:, E2:2 * E2])),
            ("split", "z", blocks(w_in[:, 2 * E2:])),
            ("split", "mo", blocks(x["m_w_out_2"][0])),
            ("split", "fu", blocks(f_in[:, :E2])),
            ("split", "fz", blocks(f_in[:, E2:])),
            ("split", "fo2", blocks(x["f_w_out_2"][0]))]
    return seq


def vectors(x):
    v = {}
    for i in range(2):
        v[f"nmix{i}"] = cols(x["norm_mix_g"][i])
        v[f"nmlp{i}"] = cols(x["norm_mlp_g"][i])
        v[f"modb{i}"] = cols(x["mod_b"][i])
        v[f"adab{i}"] = cols(x["b_ada_2"][i])
        v[f"n2{i}"] = cols(x["norm_g_2"][i])
    v["c"] = cols(x["c"])
    v["c3"] = np.stack([cols(x["c"]), cols(x["c_2"]), cols(x["c_ctx_2"])], 1).reshape(P, -1)
    for j in range(6):
        v[f"mu{j}"] = cols(x["rw_mu"][0, j])
    v["w0"], v["a0"] = cols(x["rw_w0"][0]), cols(x["rw_a0"][0])
    pair = [cols(x[n][0]) for n in ("rw_kk", "rw_ka", "rw_rk", "rw_lnw", "rw_lnb")]
    v["pair"] = np.stack(pair, 2).reshape(P, -1)
    v["kvn"], v["kvmb"] = cols(x["kv_norm_g"]), cols(x["kv_mod_b"])
    v["kg"], v["qg"] = cols(np.tile(x["kv_kg"], 2)), cols(np.tile(x["fx_qg"][0], 2))
    v["fb"] = padded(np.asarray(x["kv_fb"])[:, None], P, 1)
    v["final"] = cols(x["final_g"])
    v["convw"] = np.asarray(x["m_conv_w_2"][0]).reshape(9, ET, P).transpose(2, 1, 0).reshape(P, -1)
    v["convb"] = cols(x["m_conv_b_2"][0])
    bias = np.zeros((P, 1), np.float32)
    for d in range(2):
        bias[64 * d:64 * d + 4, 0] = x["m_b_i_2"][0, d]
        bias[64 * d + 32:64 * d + 36, 0] = x["m_b_f_2"][0, d]
    v["bif"] = bias
    v["lnw2"], v["skip"] = cols(x["m_ln_w_2"][0]), cols(x["m_skip_2"][0])
    v["normf"] = cols(x["norm_f_2"])
    return v


def constants():
    c = {}
    i = np.arange(P)
    same = i[:, None] // 64 == i[None] // 64
    c["ident"] = np.eye(P)
    c["ones"] = np.ones((P, P))
    c["head"] = same * 1.0
    up, upi = same * (i[:, None] < i[None]), same * (i[:, None] <= i[None])
    c["mrec"] = np.concatenate([up, upi], 1)
    c["m16"] = i[:, None] // 16 == i[None] // 16
    c["mlow16"] = c["m16"] * (i[:, None] > i[None])
    c["keep"] = np.tile(np.arange(T) % CH != 0, (P, 1))
    c["causal"] = np.where(i[None] <= i[:, None], 0.0, -1e30)
    c["fwd"] = (i[:, None] <= i[None]) * 1.0
    c["rev"] = (i[:, None] >= i[None]) * 1.0
    c["epsn"] = np.full((P, 1), NORM_EPS)
    c["zero"] = np.zeros((P, 1))
    c["epsg"] = np.full((P, 1), GN_EPS)
    return {k: np.asarray(v, np.float32) for k, v in c.items()}


def dft_tables():
    a = 2 * np.pi * (np.arange(256)[:, None] * np.arange(256)[None] % 256) / 256
    ch = np.concatenate([np.cos(a), np.sin(a)], 1).reshape(2, P, 512).transpose(1, 0, 2)
    b = 2 * np.pi * (np.arange(T)[:, None] * np.arange(T)[None] % T) / T
    f = (T * 256) ** -0.5
    tok = np.stack([np.cos(b) * f, -np.sin(b) * f]).reshape(2, 4, P, T).transpose(2, 0, 1, 3)
    return ch.reshape(P, -1).astype(np.float32), tok.reshape(P, -1).astype(np.float32)


def layout(x):
    seq = stream(x)
    vec, con = vectors(x), constants()
    ch, tok = dft_tables()
    arrays = {
        "wst": np.concatenate([b for _, _, b in seq]),
        "vec": np.concatenate(list(vec.values()), 1),
        "con": np.concatenate(list(con.values()), 1),
        "xT": np.ascontiguousarray(np.asarray(x["x"])[0].T.reshape(KT, P, T).transpose(1, 0, 2)),
        "cT": np.ascontiguousarray(np.asarray(x["ctx_2"])[0].T.reshape(KT, P, TX).transpose(1, 0, 2)),
        "dch": ch, "dtok": tok,
    }
    plan = [(kind, name, b.shape[0]) for kind, name, b in seq]
    vat, cat = {}, {}
    for table, parts in ((vat, vec), (cat, con)):
        at = 0
        for k, a in parts.items():
            table[k] = (at, a.shape[1])
            at += a.shape[1]
    return arrays, plan, vat, cat


class Dry:

    def _same(self, *args, **kwargs):
        return self

    matmul = transpose = activation = tensor_tensor = tensor_scalar = scalar_tensor_tensor = _same
    tensor_copy = tensor_reduce = reciprocal = memset = dma_start = then_inc = wait_ge = nop = _same
    tensor_tensor_scan = affine_select = _same


class Engine:

    def __init__(self, book, name):
        self.book, self.name, self.latest = book, name, None
        self.made, self.took = {}, {}

    def up(self, sem):
        self.made[sem] = self.made.get(sem, 0) + 1
        self.latest = sem
        return sem, 1

    def up16(self, sem):
        self.made[sem] = self.made.get(sem, 0) + 16
        self.latest = sem
        return sem, 16

    def used(self, sem):
        return sem, self.book.base.get(sem, 0) + self.took[sem]

    def skip(self, sem, k):
        self.took[sem] = self.took.get(sem, 0) + k

    def last(self):
        return self.latest, self.book.base.get(self.latest, 0) + self.made[self.latest]

    def need(self, sem, k=1):
        self.took[sem] = self.took.get(sem, 0) + k
        return sem, self.book.base.get(sem, 0) + self.took[sem]

    def again(self, sem):
        n = self.took.get(sem, 0)
        self.took[sem] = n + 1
        if isinstance(n, int) and n == 0:
            return []
        return [(sem, self.book.base.get(sem, 0) + n)]

    def loop(self, e, n, body):
        made, took, latest = dict(self.made), dict(self.took), self.latest
        body(Dry(), 0)
        dm = {s: v - made.get(s, 0) for s, v in self.made.items()}
        dt = {s: v - took.get(s, 0) for s, v in self.took.items()}

        def at(start, step, i):
            return {s: start.get(s, 0) + (i * step[s] if step[s] else 0) for s in step}
        self.latest = latest
        with e.Fori(0, n) as i:
            self.made, self.took = at(made, dm, i), at(took, dt, i)
            body(e, i)
        self.made, self.took = at(made, dm, n), at(took, dt, n)


class Book:

    def __init__(self, nc, ctx):
        self.nc, self.ctx, self.base, self.sems = nc, ctx, {}, {}
        self.engines = [Engine(self, n) for n in ("pe", "act", "dve", "pool", "sp")]

    def sem(self, name):
        if name not in self.sems:
            self.sems[name] = self.ctx.enter_context(self.nc.semaphore(name))
        return self.sems[name]

    def phase(self):
        for g in self.engines:
            for s, n in g.made.items():
                self.base[s] = self.base.get(s, 0) + n
            g.made, g.took, g.latest = {}, {}, None


def program(nc, A, out, plan, vat, cat):
    ctx = ExitStack()
    with ctx:
        book = Book(nc, ctx)
        PE, AC, VE, GP, SP = book.engines
        sem = book.sem

        def fixed(name, shape, dt=F32):
            return ctx.enter_context(nc.sbuf_tensor(name, shape, dt))

        wraw = fixed("wraw", [P, RAW, BLK])
        ring_at = (nc.sbuf_base + 31) // 32 * 32
        fixed("split_ring", [P, 2 * SPL * BLK])
        whi, wlo = (nc.alloc_sbuf_tensor_at(n, [P, SPL, BLK], F32R, offset=ring_at + 4 * j * SPL * BLK)
                    for j, n in enumerate(("whi", "wlo")))
        scaled = nc.alloc_sbuf_tensor_at("scaled", [P, KT, 256], F32, offset=ring_at)
        csum = nc.alloc_sbuf_tensor_at("csum", [P, COND_TURN, 2, 256], F32, offset=ring_at + 4 * BLK)
        vec = fixed("vec_sb", [P, A["vec"].shape[1]])
        con = fixed("con_sb", [P, A["con"].shape[1]])
        started = fixed("started", [P, len(LAGGED)])
        cact = fixed("cact", [P, KT])
        cact3 = fixed("cact3", [P, 3, KT])
        mod = [fixed(f"mod{i}", [P, 48]) for i in range(2)]
        kvm = fixed("kvm", [P, 16])
        ada0 = fixed("ada0", [P, 2, 24])
        ada1 = fixed("ada1", [P, 24])
        coef = fixed("coef", [P, 8, KT])
        NT = nc.sbuf_bytes_remaining // 2048
        fence = nc.sbuf_base
        fixed("arena", [P, NT, T])
        off0 = (fence + 31) // 32 * 32
        named = {}

        def tiles(name, at, n=None, dt=F32, shape=None):
            shape = shape or [P, n, T]
            words = int(np.prod(shape[1:]))
            assert at * T + words <= NT * T, (name, at, words, NT)
            if name not in named:
                named[name] = nc.alloc_sbuf_tensor_at(name, shape, dt, offset=off0 + at * 2048)
            return named[name]

        ps = ctx.enter_context(nc.psum_tensor("ps", [P, 8, 512], F32))

        def V(name, i=None, n=1):
            at, width = vat[name]
            return vec[:, at:at + width] if i is None else vec[:, at + i:at + i + n]

        def C(name):
            at, width = cat[name]
            return con[:, at:at + width]

        ident, ones, head = C("ident"), C("ones"), C("head")

        raws = [kind for kind, _, n in plan for _ in range(n)]
        seqno, firsts, n_split, n_raw = [], {}, 0, 0
        for kind, name, n in plan:
            firsts[name] = (len(seqno), n_split if kind == "split" else n_raw)
            for _ in range(n):
                if kind == "split":
                    seqno.append(n_split)
                    n_split += 1
                else:
                    seqno.append(n_raw)
                    n_raw += 1
        split_at = [r for r, k in enumerate(raws) if k == "split"]
        firsts_raw = {m: f[0] for m, f in firsts.items()}
        w_full = [sem(f"w_loaded{s}") for s in range(RAW)]
        w_split, w_used, w_cond = sem("w_split"), sem("w_used"), sem("w_cond_used")
        sent = {"dma": 0, "pool": 0, "q": 0}

        def settle(e):
            e.nop(nofuse=True)

        def load_weights(sp, upto):
            upto = min(upto, len(raws))
            while sent["dma"] < upto:
                r = sent["dma"]
                if r < RAW:
                    sp.dma_start(wraw[:, r], A["wst"][r]).then_inc(w_full[r], 16)
                    sent["dma"] += 1
                    continue
                n = 1
                while r + n < upto and raws[r + n - RAW] == raws[r - RAW]:
                    n += 1
                free = w_split if raws[r - RAW] == "split" else w_cond
                turns, c0 = n // 2, seqno[r - RAW] + 1

                def one(k, i):
                    sp.wait_ge(free, c0 + k + 2 * i)
                    sp.dma_start(wraw[:, (r + k) % RAW], A["wst"][ds(r + k + 2 * i, 1)].rearrange(
                        "a p c -> (a p) c")).then_inc(w_full[(r + k) % RAW], 16)
                if turns > 1:
                    with sp.Fori(0, turns) as i:
                        one(0, i)
                        one(1, i)
                    rest = range(2 * turns, n)
                else:
                    rest = range(n)
                for k in rest:
                    one(k, 0)
                sent["dma"] += n

        def split_weights(pool, upto):
            upto = min(upto, n_split)
            while sent["pool"] < upto:
                q = sent["pool"]
                r = split_at[q]
                n = 1
                while q + n < upto and split_at[q + n] == r + n:
                    n += 1
                if q < SPL:
                    n = 1

                def one(k, i):
                    s, f = (q + k) % SPL, (r + k) % RAW
                    if q >= SPL:
                        pool.wait_ge(w_used, q + k + 2 * i)
                    pool.wait_ge(w_full[f], ((r + k) // 2 + 1 + i) * 16)
                    pool.tensor_tensor(whi[:, s], wraw[:, f], C("zero").broadcast_to([P, BLK]), ALU.add).then_inc(sem("w_high"), 1)
                    pool.wait_ge(sem("w_high"), q + k + 1 + 2 * i)
                    pool.tensor_tensor(wlo[:, s], wraw[:, f], whi[:, s].bitcast(F32),
                                       ALU.subtract).then_inc(w_split, 1)
                turns = n // 2
                if turns > 1:
                    with pool.Fori(0, turns) as i:
                        one(0, i)
                        one(1, i)
                    rest = range(2 * turns, n)
                else:
                    rest = range(n)
                for k in rest:
                    one(k, 0)
                sent["pool"] += n

        def ahead(*names):
            raw_end = max(firsts_raw[m] + c for _, m, c in plan if m in names)
            q_end = sum(1 for r in split_at if r < raw_end)
            if q_end < n_split and split_at[q_end] == raw_end:
                return raw_end + 3, q_end + 1
            return raw_end + 2, q_end

        acc_ready = sem("acc_ready")
        acc_free = [sem(f"acc_free{b}") for b in range(NACC)]
        turn = {"acc": 0}

        def block_of(e, q, i, xhi, xlo, nk, width, tokens=((0, T),), k0=0, first=True, final=True, m0=0, mn=None,
                     open_bank=None, tell=True, bank_free=None):
            s = q % SPL
            wh = whi[:, s, :nk * width].rearrange("p (k c) -> p k c", k=nk)
            wl = wlo[:, s, :nk * width].rearrange("p (k c) -> p k c", k=nk)
            e.wait_ge(w_split, q + i + 1)
            told = not tell
            for m in range(width // P if mn is None else mn):
                for a, (t0, nt) in enumerate(tokens):
                    if open_bank is None or first:
                        b = turn["acc"] % NACC
                        turn["acc"] += 1
                        for w in (bank_free() if bank_free else PE.again(acc_free[b])):
                            e.wait_ge(*w)
                        if open_bank is not None:
                            open_bank[m] = b
                    else:
                        b = open_bank[m]
                    mc = slice((m0 + m) * P, (m0 + m + 1) * P)
                    for k in range(nk):
                        passes = ((wh, xhi), (wh, xlo), (wl, xhi))
                        for j, (w, x) in enumerate(passes):
                            o = e.matmul(ps[:, b, :nt], w[:, k, mc], x[:, k0 + k, t0:t0 + nt],
                                         start=first and k == 0 and j == 0,
                                         stop=final and k == nk - 1 and j == 2)
                            if not told:
                                o.then_inc(w_used, 1)
                                told = True
                    if final:
                        o.then_inc(*PE.up(acc_ready))

        def tokens_of(e, q, i, xhi, xlo, nk=8, width=256):
            s = q % SPL
            wh = whi[:, s, :nk * width].rearrange("p (k c) -> p k c", k=nk)
            wl = wlo[:, s, :nk * width].rearrange("p (k c) -> p k c", k=nk)
            e.wait_ge(w_split, q + i + 1)
            for t in range(T // P):
                b = turn["acc"] % NACC
                turn["acc"] += 1
                for w in PE.again(acc_free[b]):
                    e.wait_ge(*w)
                tc = slice(t * P, (t + 1) * P)
                for k in range(nk):
                    for j, (w, x) in enumerate(((wh, xhi), (wl, xhi), (wh, xlo))):
                        o = e.matmul(ps[:, b, :width], x[:, k, tc], w[:, k, :], start=k == 0 and j == 0,
                                     stop=k == nk - 1 and j == 2)
                        if t == 0 and k == 0 and j == 0:
                            o.then_inc(w_used, 1)
                o.then_inc(*PE.up(acc_ready))

        def phase_start():
            book.phase()
            turn["acc"] = 0
            turn["evac"] = 0

        def bank():
            b = turn["evac"] % NACC
            turn["evac"] += 1
            return b

        sq, rms, nt = (tiles(n, 24 + 2 * j, 2) for j, n in enumerate(("sq", "rms", "nt")))
        hh, hl = tiles("hh", 8, KT, F32R), tiles("hl", 16, KT, F32R)

        def norm_pe(e, bank_no, n=T):
            e.wait_ge(*PE.need(sem("square_added"), KT - 1))
            e.matmul(ps[:, bank_no, :n], ones, rms[:, 1, :n], start=True, stop=True).then_inc(*PE.up(sem("square_sum")))

        def norm_act(e, src, bank_no, shift=None, n=T, hi=None):
            for k in range(KT):
                if k == 2 or k > 3:
                    e.wait_ge(*AC.need(sem("square_added")))
                e.activation(sq[:, k % 2, :n], src(k), ACT.Square).then_inc(*AC.up(sem("square")))
            e.wait_ge(*AC.need(sem("square_sum")))
            e.activation(rms[:, 0, :n], ps[:, bank_no, :n], ACT.Sqrt, bias=C("epsn"),
                         scale=1.0 / D).then_inc(*AC.up(sem("rms")))
            if hi is not None:
                for k in range(KT):
                    e.wait_ge(*AC.need(sem("scaled")))
                    e.activation(hi(k), nt[:, k % 2, :n], ACT.Identity,
                                 bias=shift(k)).then_inc(*AC.up(sem("rounded")))

        def norm_dve(e, src, gain, shift=None, n=T, hi=None, lo=None, plain=None):
            total = rms[:, 1, :n]
            e.wait_ge(*VE.need(sem("square")))
            for k in range(1, KT):
                e.wait_ge(*VE.need(sem("square")))
                e.tensor_tensor(total, sq[:, 0, :n] if k == 1 else total, sq[:, k % 2, :n],
                                ALU.add).then_inc(*VE.up(sem("square_added")))
                if k < KT - 1:
                    e.wait_ge(*VE.last())
            e.wait_ge(*VE.need(sem("rms")))
            e.reciprocal(rms[:, 1, :n], rms[:, 0, :n]).then_inc(*VE.up(sem("dve")))
            e.wait_ge(*VE.last())

            def low(k):
                e.wait_ge(*VE.need(sem("rounded")))
                e.scalar_tensor_tensor(lo(k), nt[:, k % 2, :n], shift(k), hi(k).bitcast(F32), ALU.add,
                                       ALU.subtract).then_inc(*VE.up(sem("x_ready")))
            for k in range(KT):
                if k >= 2 and not plain:
                    e.wait_ge(*VE.last())
                to = plain(k) if plain and shift is None else nt[:, k % 2, :n]
                o = e.scalar_tensor_tensor(to, src(k), gain(k), rms[:, 1, :n], ALU.mult, ALU.mult)
                if not plain:
                    o.then_inc(*VE.up(sem("scaled")))
                    if k:
                        low(k - 1)
                elif shift is None:
                    o.then_inc(*VE.up(sem("x_ready")))
                else:
                    o.then_inc(*VE.up(sem("dve")))
                    e.wait_ge(*VE.last())
                    e.tensor_scalar(plain(k), nt[:, k % 2, :n], shift(k), None,
                                    ALU.add).then_inc(*VE.up(sem("x_ready")))
                    e.wait_ge(*VE.last())
            if not plain:
                low(KT - 1)

        def cond_blocks(e, name, rhs, w, dst):
            r0, c0 = firsts[name]
            n = [c for _, m, c in plan if m == name][0]

            def two(i):
                for k in range(2):
                    e.wait_ge(w_full[(r0 + k) % RAW], ((r0 + k) // 2 + 1 + i) * 16)
                    slot = wraw[:, (r0 + k) % RAW].rearrange("p (k c) -> p k c", k=KT)
                    for m in range(2):
                        for t in range(KT):
                            o = e.matmul(dst[:, ds(i * 4 * w + (2 * k + m) * w, w)],
                                         slot[:, t, m * P:(m + 1) * P], rhs[:, t, :],
                                         start=t == 0, stop=t == KT - 1)
                    o.then_inc(w_cond, 1)
            with e.Fori(0, n // 2) as i:
                two(i)

        def gains(e, j, g, scale):
            e.scalar_tensor_tensor(coef[:, j], scale, 1.0, g, ALU.add, ALU.mult).then_inc(*VE.up(sem("dve")))

        x_sb = tiles("x", 0, KT)
        phase_start()
        with nc.Block() as block:
            @block.sync
            def _(sp):
                sp.dma_start(vec[:], A["vec"]).then_inc(*SP.up16(sem("vec_loaded")))
                sp.dma_start(con[:], A["con"]).then_inc(*SP.up16(sem("con_loaded")))
                sp.dma_start(x_sb[:], A["xT"]).then_inc(*SP.up16(sem("x_loaded")))
                load_weights(sp, ahead("mod0")[0])
                sp.wait_ge(sem("vec_loaded"), 16)
                sp.wait_ge(sem("con_loaded"), 16)
                sp.wait_ge(sem("x_loaded"), 16)

            @block.gpsimd
            def _(pool):
                for k, name in enumerate(LAGGED):
                    pool.memset(started[:, k:k + 1], 0.0).then_inc(*GP.up(sem(name)))
                split_weights(pool, ahead("mod0")[1])

            @block.scalar
            def _(act):
                act.wait_ge(*AC.need(sem("vec_loaded"), 16))
                act.activation(cact[:], V("c"), ACT.Silu).then_inc(*AC.up(sem("cond")))
                act.activation(cact3[:].rearrange("p c k -> p (c k)"), V("c3"),
                               ACT.Silu).then_inc(*AC.up(sem("cond")))

            @block.tensor
            def _(pe):
                pe.wait_ge(*PE.need(sem("cond"), 2))
                cond_blocks(pe, "mod0", cact[:].rearrange("p (k c) -> p k c", c=1), 1, ps[:, 7, :])

            @block.vector
            def _(dve):
                dve.wait_ge(w_cond, firsts["mod0"][1] + 8)
                dve.wait_ge(*VE.need(sem("vec_loaded"), 16))
                dve.tensor_tensor(mod[0][:, :16], ps[:, 7, :16], V("modb0", 0, 16), ALU.add).then_inc(*VE.up(sem("dve")))
        hpad = tiles("hpad", 8, shape=[P, KT, T + 1])
        phase_start()
        with nc.Block() as block:
            @block.vector
            def _(dve):
                dve.memset(hpad[:, :, 0:1], 0.0).then_inc(*VE.up(sem("dve")))
                gains(dve, 0, V("nmix0"), mod[0][:, 8:16])
                norm_dve(dve, lambda k: x_sb[:, k], lambda k: coef[:, 0, k:k + 1], lambda k: mod[0][:, k:k + 1],
                         plain=lambda k: hpad[:, k, 1:])

            @block.scalar
            def _(act):
                norm_act(act, lambda k: x_sb[:, k], 7)

            @block.tensor
            def _(pe):
                norm_pe(pe, 7)

        dif, mix = tiles("dif", 0, 2), tiles("mix", 2, 2)
        hid, hidh, hidl = tiles("hid", 4, 1), tiles("hidh", 5, 1, F32R), tiles("hidl", 6, 1, F32R)
        hidg = tiles("hidg", 0, 2)
        sgh, sgl = tiles("sgh", 4, 2, F32R), tiles("sgl", 6, 2, F32R)
        w_sb, a_sb, r_sb, k_sb, v_sb = (tiles(n, 33 + 8 * j, KT) for j, n in enumerate(
            ("w_sb", "a_sb", "r_sb", "k_sb", "v_sb")))
        A_, B_, C_ = ((tiles(f"mixh{n}", at, KT, F32R), tiles(f"mixl{n}", at + 8, KT, F32R))
                      for n, at in (("a", 17), ("b", 33), ("c", 57)))
        phase_start()
        with nc.Block() as block:
            names = ("wr", "w1", "a1", "wk", "wv", "w2a2", "g1")

            @block.sync
            def _(sp):
                load_weights(sp, ahead(*names)[0])

            @block.gpsimd
            def _(pool):
                split_weights(pool, ahead(*names)[1])

            @block.tensor
            def _(pe):
                def full(name, n, width, buf):
                    pe.wait_ge(*PE.need(sem("mix_ready"), KT))
                    for j in range(n):
                        block_of(pe, firsts[name][1] + j, 0, buf[0], buf[1], KT, width)
                full("wr", 4, 256, A_)
                full("w1", 1, P, B_)
                full("a1", 1, P, C_)
                full("wk", 4, 256, A_)
                full("wv", 4, 256, B_)
                pe.wait_ge(*PE.need(sem("hid_ready"), 2))
                q = firsts["w2a2"][1]
                block_of(pe, q, 0, hidh, hidl, 1, BLK, mn=8)
                block_of(pe, q, 0, hidh, hidl, 1, BLK, mn=8, m0=8, tell=False)
                full("g1", 1, 256, A_)

            @block.vector
            def _(dve):
                def mixing(j, buf, done):
                    if done:
                        dve.wait_ge(*VE.need(acc_ready, done))
                    for k in range(KT + 1):
                        if k < KT:
                            dve.tensor_tensor(dif[:, k % 2], hpad[:, k, :T], hpad[:, k, 1:],
                                              ALU.subtract).then_inc(*VE.up(sem("dve")))
                            dve.wait_ge(*VE.last())
                            dve.scalar_tensor_tensor(mix[:, k % 2], dif[:, k % 2], V(f"mu{j}", k), hpad[:, k, 1:],
                                                     ALU.mult, ALU.add).then_inc(*VE.up(sem("mixed")))
                        if k:
                            dve.wait_ge(*VE.need(sem("mix_high")))
                            dve.tensor_tensor(buf[1][:, k - 1], mix[:, (k - 1) % 2], buf[0][:, k - 1].bitcast(F32),
                                              ALU.subtract).then_inc(*VE.up(sem("mix_ready")))

                def hidden_low(x, lo, hi):
                    dve.wait_ge(*VE.need(sem("hid_high")))
                    dve.tensor_tensor(lo, x, hi.bitcast(F32), ALU.subtract).then_inc(*VE.up(sem("hid_ready")))
                mixing(0, A_, 0)
                mixing(1, B_, 0)
                mixing(4, C_, 0)
                mixing(2, A_, 8)
                for n in range(2):
                    rr = slice(64 * n, 64 * n + 64)
                    hidden_low(hid[rr, 0], hidl[rr, 0], hidh[rr, 0])
                mixing(3, B_, 1)
                mixing(5, A_, 1 + 8)
                for n in range(2):
                    hidden_low(hidg[:, n], sgl[:, n], sgh[:, n])

            @block.scalar
            def _(act):
                def high(buf, tiles_=range(KT)):
                    for k in tiles_:
                        act.wait_ge(*AC.need(sem("mixed")))
                        act.activation(buf[0][:, k], mix[:, k % 2], ACT.Copy).then_inc(*AC.up(sem("mix_high")))

                def read_out(dst, func, bias=0.0, rows=slice(0, P)):
                    b = bank()
                    act.wait_ge(*AC.need(acc_ready))
                    act.activation(dst, ps[rows, b], func, bias=bias).then_inc(*AC.up(acc_free[b]))

                def hidden(x, func, hi, rows=slice(0, P)):
                    read_out(x, func, rows=rows)
                    act.wait_ge(*AC.last())
                    act.activation(hi, x, ACT.Copy).then_inc(*AC.up(sem("hid_high")))
                high(A_)
                for k in range(KT):
                    high(B_ if k < 4 else C_, (2 * (k % 4), 2 * (k % 4) + 1))
                    read_out(r_sb[:, k], ACT.Copy)
                for n, func in enumerate((ACT.Tanh, ACT.Copy)):
                    rr = slice(64 * n, 64 * n + 64)
                    hidden(hid[rr, 0], func, hidh[rr, 0], rr)
                high(A_)
                for to, buf in ((k_sb, B_), (v_sb, A_)):
                    for k in range(KT):
                        if to is k_sb:
                            high(buf, (k,))
                            read_out(to[:, k], ACT.Copy)
                        else:
                            read_out(to[:, k], ACT.Copy)
                            high(buf, (k,))
                for k in range(KT):
                    read_out(w_sb[:, k], ACT.Sigmoid, V("w0", k))
                for k in range(KT):
                    read_out(a_sb[:, k], ACT.Sigmoid, V("a0", k))
                for n in range(2):
                    hidden(hidg[:, n], ACT.Sigmoid, sgh[:, n])

        w = iter(range(8, 33))

        def work(name, n=1, shape=None):
            at = [next(w) for _ in range(n)]
            assert at[-1] - at[0] == n - 1
            return tiles(name, at[0], n, shape=shape or [P, 4, P])
        ar = work("ar", 2, [P, 4, 2, P])
        abrb = work("abrb", 2, [P, 4, 2, P])
        akrk = work("akrk", 2, [P, 4, 2, P])
        xav = work("xav", 2, [P, 4, 2, P])
        fg = work("fg", 2, [P, 4, 2, P])
        bb, kb, bt, kt, vt, ad, adt, aot, pt, a2, a2t = (work(n) for n in (
            "bb", "kb", "bt", "kt", "vt", "ad", "adt", "aot", "pt", "a2", "a2t"))
        st = work("st", shape=[P, 2, P])
        wend = fixed("wend", [P, NC * KT])
        pair_sel = fixed("pair_sel", [16, P])
        (kraw, ksq, cum, prev), (ep, en, e3, kkn) = ([tiles(n, at + 2 * j, 2) for j, n in enumerate(names_)]
                                                     for at, names_ in ((10, ("kraw", "ksq", "cum", "prev")),
                                                                        (20, ("ep", "en", "e3", "kkn"))))
        gain = tiles("gain", 0, 2)
        inv, inv_row = tiles("inv", 2, shape=[P, 64]), tiles("inv_row", 3, shape=[16, T])
        tb, ysq, zb = (tiles(n, at, 2) for n, at in (("tb", 30), ("ysq", 12), ("zb", 0)))
        to_act, to_dve, ev_a, ev_v = sem("mat_for_act"), sem("mat_for_dve"), sem("mat_by_act"), sem("mat_by_dve")
        vs = tiles("vs", 73, shape=[P, 4, 2, CH])
        WKV_STEPS = ("GB", "GA", "BT", "GK", "AT", "KT", "VT", "A2", "A2T", "AV", "P2", "A4", "A4T", "P3", "A8", "P4",
                     "TD", "M", "MT", "Q", "M2", "T", "FG", "PHI", "E")
        WKV_DVE_STEPS = ("GB", "GA", "GK", "VT", "P2", "P3", "P4", "Q", "T", "PHI", "E")
        WKV_ACT = 2 * (2 * (len(WKV_STEPS) - len(WKV_DVE_STEPS)) + 1)
        WKV_DVE = 2 * (2 * len(WKV_DVE_STEPS) + 4)
        wkv_order = []
        for half in range(2):
            wkv_order += [(n, half, g) for n in WKV_STEPS for g in range(2)] + [("Y", half)]
            wkv_order += [("S", half, c) for c in range(4)]
        wkv_bank = {n: j % 7 for j, n in enumerate(wkv_order)}
        phase_start()

        def tile_of(buf, i):
            return buf[:, ds(i, 1)].rearrange("p a t -> p (a t)")

        def chunks(ap):
            return ap.rearrange("p (c t) -> p c t", t=CH)

        with nc.Block() as block:
            @block.sync
            def _(sp):
                load_weights(sp, ahead("ada0c")[0])

            @block.gpsimd
            def _(pool):
                r0, c0 = firsts["mod0b"]

                def turn_blocks(e, i, first, conds):
                    for k in range(COND_TURN):
                        r = r0 + k
                        e.wait_ge(w_full[r % RAW], (r // 2 + 1) * 16 + COND_TURN * 8 * (first + i))
                        w = wraw[:, r % RAW].rearrange("p (k c) -> p k c", k=KT)
                        c = cact3[:, conds[k]].rearrange("p (k a) -> p k a", a=1).broadcast_to([P, KT, 256])
                        e.tensor_tensor(scaled[:], w, c, ALU.mult).then_inc(w_cond, 1)
                        e.wait_ge(w_cond, c0 + k + 1 + COND_TURN * (first + i))
                        e.tensor_tensor(scaled[:, 0:4], scaled[:, 0:4], scaled[:, 4:8],
                                        ALU.add).then_inc(*GP.up(sem("cond_added")))
                        e.wait_ge(*GP.last())
                        if first:
                            e.wait_ge(sem("cond_taken"), COND_TURN * (first + i - 1) + k + 1)
                        e.tensor_tensor(csum[:, k], scaled[:, 0:2], scaled[:, 2:4],
                                        ALU.add).then_inc(*GP.up(sem("cond_summed")))
                        e.wait_ge(*GP.last())
                turn_blocks(pool, 0, 0, [0] * 10)
                GP.loop(pool, 3, lambda e, i: turn_blocks(e, i, 1, [0] * 10))
                turn_blocks(pool, 0, 4, [0] * 8 + [1] * 2)
                GP.loop(pool, 2, lambda e, i: turn_blocks(e, i, 5, [1] * 10))
                turn_blocks(pool, 0, 7, [1] * 2 + [2] * 8)
                pool.wait_ge(sem("cond_taken"), KT * COND_TURN)
                split_weights(pool, ahead("ada0c")[1])

            @block.tensor
            def _(pe):
                n_act, n_dve = WKV_ACT, WKV_DVE

                def turn_of(e, i):
                    ready, last, made = {}, {}, {"a": 0, "v": 0}
                    seen, wanted = {"a": 0, "v": 0}, []

                    def wait_for_wanted():
                        for to, s, tot in (("a", ev_a, n_act), ("v", ev_v, n_dve)):
                            latest = max([n for t, n in wanted if t == to] + [0])
                            if latest > seen[to]:
                                e.wait_ge(s, book.base.get(s, 0) + i * tot + latest)
                                seen[to] = latest
                        wanted.clear()

                    if not isinstance(i, int) or i:
                        e.wait_ge(ev_a, book.base.get(ev_a, 0) + i * n_act)
                        e.wait_ge(ev_v, book.base.get(ev_v, 0) + i * n_dve)

                    def unit(name, to, products, n=256, transpose=False):
                        b = wkv_bank[name]
                        if b in last:
                            wanted.append(last[b])
                        wait_for_wanted()
                        o = products(b)
                        made[to] += 1
                        ready[name] = last[b] = (to, made[to])
                        o.then_inc(*PE.up(to_act if to == "a" else to_dve))

                    def mats(name, to, g, out, *terms, after=()):
                        for a in after:
                            wanted.append(ready[a, half, g])

                        def go(b):
                            for c in range(2):
                                for j, (l, r) in enumerate(terms):
                                    rhs = r(2 * g + c)
                                    cw = out // 2
                                    o = e.matmul(ps[:, b, c * cw:(c + 1) * cw], l(2 * g + c), rhs,
                                                 start=j == 0, stop=j == len(terms) - 1)
                            return o
                        unit((name, half, g), to, go)

                    def turned(name, to, g, src, after=()):
                        for a in after:
                            wanted.append(ready[a, half, g])

                        def go(b):
                            for c in range(2):
                                o = e.transpose(ps[:, b, c * P:(c + 1) * P], src(2 * g + c), ident)
                            return o
                        unit((name, half, g), to, go)

                    taken = [0]

                    def cond_block():
                        k = taken[0]
                        taken[0] += 1
                        e.wait_ge(*PE.need(sem("cond_summed")))
                        for j in range(2):
                            for t in range(2):
                                o = e.matmul(ps[:, 7, ds(i * 2 * COND_TURN + 2 * k + j, 1)],
                                             csum[:, k, t, j * P:(j + 1) * P], ones[:, 0:1], start=t == 0, stop=t == 1)
                        o.then_inc(*PE.up(sem("cond_taken")))

                    def m(buf, part=None):
                        return (lambda c: buf[:, c]) if part is None else (lambda c: buf[:, c, part])
                    for half in range(2):
                        e.wait_ge(*PE.need(sem("bd_ready")))
                        e.wait_ge(*PE.need(sem("kb_ready")))

                        def arw(c):
                            return ar[:, c].rearrange("p a t -> p (a t)")

                        def vdup(c):
                            return vs[:, c].rearrange("p a t -> p (a t)")
                        G = range(2)
                        for g in G:
                            mats("GB", "v", g, 512, (m(bb), arw))
                        for g in G:
                            mats("GA", "v", g, 256, (m(ar, 0), m(bb)))
                        for g in G:
                            turned("BT", "a", g, m(bb))
                        for g in G:
                            mats("GK", "v", g, 512, (m(kb), arw))
                        cond_block()
                        for g in G:
                            turned("AT", "a", g, m(ar, 0))
                        for g in G:
                            turned("KT", "a", g, m(kb))
                        e.wait_ge(*PE.need(sem("v_twice")))
                        for g in G:
                            turned("VT", "v", g, vdup)
                        for g in G:
                            mats("A2", "a", g, 256, (m(adt), m(ad)), after=("GB", "GA"))
                        for g in G:
                            mats("A2T", "a", g, 256, (m(ad), m(adt)))
                        for g in G:
                            mats("AV", "a", g, 256, (m(akrk, 0), m(vt)), after=("GK", "VT"))
                        for g in G:
                            mats("P2", "v", g, 256, (m(a2), m(pt)), after=("A2",))
                        for g in G:
                            mats("A4", "a", g, 256, (m(a2t), m(a2)), after=("A2T",))
                        for g in G:
                            mats("A4T", "a", g, 256, (m(a2), m(a2t)))
                        cond_block()
                        for g in G:
                            mats("P3", "v", g, 256, (m(ad), m(pt)), after=("A4", "P2"))
                        for g in G:
                            mats("A8", "a", g, 256, (m(adt), m(ad)), after=("A4T",))
                        for g in G:
                            mats("P4", "v", g, 256, (m(a2), m(pt)), after=("A8", "P3"))
                        cond_block()
                        for g in G:
                            turned("TD", "a", g, m(pt), after=("P4",))
                        for g in G:
                            mats("M", "a", g, 256, (m(aot), m(a2t)), after=("TD",))
                        for g in G:
                            mats("MT", "a", g, 256, (m(a2t), m(aot)))
                        cond_block()
                        for g in G:
                            mats("Q", "v", g, 256, (m(ad), m(pt)), after=("M",))
                        for g in G:
                            mats("M2", "a", g, 256, (m(adt), m(ad)), after=("MT",))
                        for g in G:
                            mats("T", "v", g, 256, (m(a2), m(pt)), after=("M2", "Q"))
                        cond_block()
                        for g in G:
                            mats("FG", "a", g, 512, (m(pt), lambda c: xav[:, c].rearrange("p a t -> p (a t)")),
                                 after=("T", "AV", "AT"))
                        for g in G:
                            mats("PHI", "v", g, 256, (m(fg, 0), m(bt)), after=("FG", "BT"))
                        for g in G:
                            mats("E", "v", g, 256, (m(fg, 0), m(abrb, 1)))
                        yb = wkv_bank["Y", half]
                        if yb in last:
                            wanted.append(last[yb])
                        for g in G:
                            for name in ("KT", "PHI", "E"):
                                wanted.append(ready[name, half, g])
                        for c in range(4):
                            old = st[:, c % 2]
                            if c or half:
                                wanted.append(ready["S", half if c else half - 1, c - 1 if c else 3])

                            def state(b):
                                e.matmul(ps[:, b, :P], bt[:, c], fg[:, c, 1], start=True, stop=False)
                                e.matmul(ps[:, b, :P], kt[:, c], vt[:, c], start=False, stop=False)
                                return e.matmul(ps[:, b, :P], ad[:, c], old, start=False, stop=True)
                            unit(("S", half, c), "v", state)
                            yc = ps[:, yb, c * P:(c + 1) * P]
                            e.matmul(yc, fg[:, c, 1], abrb[:, c, 1], start=True, stop=False)
                            e.matmul(yc, vt[:, c], akrk[:, c, 1], start=False, stop=False)
                            o = e.matmul(yc, old, adt[:, c], start=False, stop=True)
                        o.then_inc(*PE.up(to_act))
                        made["a"] += 1
                        last[yb] = ("a", made["a"])
                    assert made == {"a": n_act, "v": n_dve}, made

                def head_squares(e, i, j, src, bank_no, s):
                    for t in range(4):
                        o = e.matmul(ps[:, bank_no, ds(2 * (2 * i + j) + 16 * t, 2)], src[:, j, P * t:P * t + P],
                                     head[:, 0:P:64], start=True, stop=True)
                    o.then_inc(*PE.up(s))

                def inverse_rows():
                    pe.wait_ge(*PE.need(sem("inverse")))
                    for t in range(4):
                        o = pe.transpose(ps[:16, 6, P * t:P * t + P], inv[:, 16 * t:16 * t + 16], ident)
                    o.then_inc(*PE.up(sem("rows_turned")))

                def spread(e, j):
                    e.wait_ge(*PE.need(sem("pair_ready")))
                    for w_ in PE.again(sem(f"scale_used{j}")):
                        e.wait_ge(*w_)
                    e.matmul(ps[:, j], pair_sel[:], inv_row[:], start=True, stop=True).then_inc(*PE.up(sem("scale_spread")))

                def kk_sums(e, i):
                    for j in range(2):
                        e.wait_ge(*PE.need(sem(f"kk_squared{j}")))
                        head_squares(e, i, j, ksq, 5, sem(f"kk_summed{j}"))
                PE.loop(pe, KT // 2, kk_sums)
                inverse_rows()
                PE.loop(pe, KT // 2, lambda e, i: (spread(e, 0), spread(e, 1)))
                PE.loop(pe, KT, turn_of)
                pe.wait_ge(ev_a, book.base.get(ev_a, 0) + KT * WKV_ACT)
                pe.wait_ge(ev_v, book.base.get(ev_v, 0) + KT * WKV_DVE)

                def y_sums(e, i):
                    for j in range(2):
                        for w_ in PE.again(sem(f"centred{j}")):
                            e.wait_ge(*w_)
                        e.matmul(ps[:, j], head, tile_of(w_sb, 2 * i + j), start=True,
                                 stop=True).then_inc(*PE.up(sem("mean_ready")))
                    for j in range(2):
                        e.wait_ge(*PE.need(sem("rk_ready")))
                        for w_ in PE.again(sem(f"bonus_used{j}")):
                            e.wait_ge(*w_)
                        e.matmul(ps[:, 2 + j], head, tb[:, j], start=True, stop=True).then_inc(*PE.up(sem("bonus_ready")))
                    for j in range(2):
                        e.wait_ge(*PE.need(sem("y_squared")))
                        head_squares(e, i, j, ysq, 5, sem(f"y_summed{j}"))
                PE.loop(pe, KT // 2, y_sums)
                inverse_rows()
                PE.loop(pe, KT // 2, lambda e, i: (spread(e, 0), spread(e, 1)))

            @block.scalar
            def _(act):
                def diagonal_k(e, i, half):
                    for h in range(2):
                        rr = slice(64 * h, 64 * h + 64)
                        settle(e)
                        o = e.activation(kb[rr, :, rr], chunks(tile_of(k_sb, i)[rr, 256 * half:256 * half + 256]), ACT.Copy)
                    o.then_inc(*AC.up(sem("kb_ready")))

                def turn_of(e, i, more=True):
                    b = wkv_bank
                    for half in range(2):
                        for a in range(2):
                            o = e.activation(vs[:, :, a], chunks(v_sb[:, ds(i, 1), half * 256:half * 256 + 256].rearrange(
                                "p a t -> p (a t)")), ACT.Copy)
                        o.then_inc(*AC.up(sem("v_twice")))
                        for name, to in (("BT", bt), ("AT", xav), ("KT", kt), ("A2", a2), ("A2T", a2t), ("AV", xav),
                                         ("A4", ad), ("A4T", adt), ("A8", a2), ("TD", a2t), ("M", ad), ("MT", adt),
                                         ("M2", a2), ("FG", fg)):
                            for g in range(2):
                                cc = slice(2 * g, 2 * g + 2)
                                n = 512 if name == "FG" else 256
                                if name == "FG":
                                    dst = to[:, cc].rearrange("p c a t -> p (c a t)")
                                elif name == "AT":
                                    dst = to[:, cc, 0]
                                elif name == "AV":
                                    dst = to[:, cc, 1]
                                else:
                                    dst = to[:, cc].rearrange("p c t -> p (c t)")
                                src = ps[:, b[name, half, g], :n]
                                if name in ("AT", "AV"):
                                    src = src.rearrange("p (c t) -> p c t", c=2)
                                e.wait_ge(*AC.need(to_act))
                                e.activation(dst, src, ACT.Copy).then_inc(*AC.up(ev_a))
                        if half == 0 or more:
                            diagonal_k(e, i + half, 1 - half)
                        e.wait_ge(*AC.need(to_act))
                        settle(e)
                        for h in range(2):
                            o = e.activation(chunks(tile_of(w_sb, i)[64 * h:64 * h + 64, half * 256:(half + 1) * 256]),
                                             ps[64 * h:64 * h + 64, b["Y", half]].rearrange(
                                                 "p (c t) -> p c t", c=4)[:, :, 64 * h:64 * h + 64], ACT.Copy)
                        o.then_inc(*AC.up(ev_a))

                def select(e, i, j):
                    e.wait_ge(sem("scale_spread"), book.base[sem("scale_spread")] + uses[0] + 2 * i + j)
                    settle(e)
                    for h in range(2):
                        o = e.activation(pair_sel[:, 64 * h:64 * h + 64],
                                         ident[:16, ds(4 * i + 2 * j + h, 1)].broadcast_to([16, 64]), ACT.Copy)
                    o.then_inc(*AC.up(sem("pair_ready")))

                def inverse_rows(s, eps):
                    act.wait_ge(*s)
                    act.activation(inv[:], ps[:, 5, :64], ACT.Sqrt, **eps).then_inc(*AC.up(sem("norms")))
                    act.wait_ge(*AC.need(sem("rows_turned")))
                    act.activation(inv_row[:], ps[:16, 6], ACT.Copy).then_inc(*AC.up(sem("none")))
                    act.wait_ge(*AC.last())

                def all_of(s):
                    return s, book.base.get(s, 0) + KT // 2

                uses = [0]

                def kk_squares(e, i):
                    for j in range(2):
                        e.wait_ge(*AC.need(sem("kk_raw")))
                        for w_ in AC.again(sem(f"kk_summed{j}")):
                            e.wait_ge(*w_)
                        e.activation(ksq[:, j], kraw[:, j], ACT.Square).then_inc(*AC.up(sem(f"kk_squared{j}")))
                AC.loop(act, KT // 2, kk_squares)
                act.wait_ge(*all_of(sem("kk_summed0")))
                inverse_rows(all_of(sem("kk_summed1")), {})

                def factors(e, i):
                    for j in range(2):
                        select(e, i, j)
                        e.wait_ge(*AC.need(sem("cum_ready")))
                        for to, src, f in ((ep, cum, -HALF), (en, cum, HALF), (e3, prev, -HALF)):
                            e.activation(to[:, j], src[:, j], ACT.Exp, scale=f).then_inc(*AC.up(sem("exp")))
                AC.loop(act, KT // 2, factors)
                act.wait_ge(*AC.need(sem("diagonals_clear")))
                diagonal_k(act, 0, 0)
                AC.loop(act, KT - 1, turn_of)
                turn_of(act, KT - 1, more=False)

                def y_squares(e, i):
                    for j in range(2):
                        e.wait_ge(*AC.need(sem(f"centred{j}")))
                        for w_ in AC.again(sem(f"y_summed{j}")):
                            e.wait_ge(*w_)
                        settle(e)
                        e.activation(ysq[:, j], tile_of(w_sb, 2 * i + j), ACT.Square).then_inc(*AC.up(sem("y_squared")))
                AC.loop(act, KT // 2, y_squares)
                act.wait_ge(*all_of(sem("y_summed0")))
                inverse_rows(all_of(sem("y_summed1")), {"bias": C("epsg"), "scale": 1.0 / 64})
                uses[0] = KT
                AC.loop(act, KT // 2, lambda e, i: (select(e, i, 0), select(e, i, 1)))

            @block.vector
            def _(dve):
                chain = sem("dve")
                at = vat["pair"][0]

                def pv(i, n):
                    return vec[:, ds(i * 5 + at + n, 1)]

                def own(e):
                    e.wait_ge(*VE.last())

                def inverse(eps):
                    dve.wait_ge(*VE.need(sem("norms")))
                    if eps:
                        dve.tensor_scalar(inv[:], inv[:], 1e-12, None, ALU.max).then_inc(*VE.up(chain))
                        dve.wait_ge(*VE.last())
                    dve.reciprocal(inv[:], inv[:]).then_inc(*VE.up(sem("inverse")))

                def kk_raw(e, i):
                    for j in range(2):
                        for w_ in VE.again(sem(f"kk_squared{j}")):
                            e.wait_ge(*w_)
                        e.tensor_scalar(kraw[:, j], tile_of(k_sb, 2 * i + j), pv(2 * i + j, 0), None,
                                        ALU.mult).then_inc(*VE.up(sem("kk_raw")))
                VE.loop(dve, KT // 2, kk_raw)
                inverse(True)

                def products(e, i):
                    for j in range(2):
                        wx = tile_of(w_sb, 2 * i + j)
                        e.tensor_tensor_scan(cum[:, j], C("keep"), wx, 0.0, ALU.mult, ALU.add).then_inc(*VE.up(chain))
                        own(e)
                        e.tensor_tensor(prev[:, j], cum[:, j], wx, ALU.subtract).then_inc(*VE.up(sem("cum_ready")))
                    for j in range(2):
                        g = 2 * i + j
                        kx, rx, wx, ax = (tile_of(z, g) for z in (k_sb, r_sb, w_sb, a_sb))
                        e.wait_ge(*VE.need(sem("scale_spread")))
                        e.scalar_tensor_tensor(kkn[:, j], kx, pv(g, 0), ps[:, j], ALU.mult,
                                               ALU.mult).then_inc(*VE.up(sem(f"scale_used{j}")))
                        e.tensor_scalar(gain[:, j], ax, -1.0, pv(g, 1), ALU.add, ALU.mult).then_inc(*VE.up(chain))
                        own(e)
                        e.scalar_tensor_tensor(kx, gain[:, j], 1.0, kx, ALU.add, ALU.mult).then_inc(*VE.up(chain))
                        e.tensor_tensor(ax, kkn[:, j], ax, ALU.mult).then_inc(*VE.up(chain))
                        e.wait_ge(*VE.need(sem("exp"), 3))
                        e.tensor_copy(wend[:, ds(NC * g, NC)], ep[:, j, CH - 1::CH]).then_inc(*VE.up(chain))
                        e.scalar_tensor_tensor(wx, kkn[:, j], -1.0, e3[:, j], ALU.mult, ALU.mult).then_inc(*VE.up(chain))
                        e.tensor_tensor(rx, rx, ep[:, j], ALU.mult).then_inc(*VE.up(chain))
                        own(e)
                        e.tensor_tensor(ax, ax, en[:, j], ALU.mult).then_inc(*VE.up(chain))
                        e.tensor_tensor(kx, kx, en[:, j], ALU.mult).then_inc(*VE.up(chain))
                        own(e)
                VE.loop(dve, KT // 2, products)
                for buf in (ar, bb, kb):
                    dve.memset(buf[:], 0.0).then_inc(*VE.up(sem("diagonals_clear") if buf is kb else chain))
                dve.wait_ge(*VE.last())

                def diagonal(e, i, half, n):
                    h, what = n % 2, n // 2
                    rr = slice(64 * h, 64 * h + 64)
                    src = chunks(tile_of((w_sb, r_sb, a_sb)[what], i)[rr, 256 * half:256 * half + 256])
                    dst = bb[rr, :, rr] if what == 2 else ar[rr, :, what, rr]
                    e.tensor_copy(dst, src).then_inc(*VE.up(sem("bd_ready") if n == 5 else chain))
                for n in range(6):
                    diagonal(dve, 0, 0, n)

                def turn_of(e, i, more=True):
                    b = wkv_bank

                    def step(o, s=chain):
                        o.then_inc(*VE.up(s))
                        e.wait_ge(*VE.last())

                    def taken(o):
                        o.then_inc(*VE.up(ev_v))
                    e.memset(st[:, 0], 0.0).then_inc(*VE.up(chain))
                    for half in range(2):
                        def cc(g):
                            return slice(2 * g, 2 * g + 2)

                        def src(name, g, n=256):
                            return ps[:, b[name, half, g], :n]

                        def bc(z, k, n):
                            return z.rearrange("p (a n) -> p a n", a=1).broadcast_to([P, k, n])

                        def add(name, g, to, other):
                            e.wait_ge(*VE.need(to_dve))
                            taken(e.tensor_tensor(to[:, cc(g)], src(name, g).rearrange("p (c t) -> p c t", c=2),
                                                  other, ALU.add))

                        def masked(name, g, to, mask):
                            e.wait_ge(*VE.need(to_dve))
                            return e.tensor_tensor(to, src(name, g).rearrange("p (c t) -> p c t", c=2), mask, ALU.mult)
                        for g in range(2):
                            e.wait_ge(*VE.need(to_dve))
                            step(e.tensor_tensor(abrb[:, cc(g)].rearrange("p c a t -> p c (a t)"),
                                                 src("GB", g, 512).rearrange("p (c t) -> p c t", c=2),
                                                 bc(C("mrec"), 2, 256), ALU.mult))
                            step(e.tensor_tensor(adt[:, cc(g)], abrb[:, cc(g), 0], bc(C("m16"), 2, P), ALU.mult))
                            e.tensor_tensor(aot[:, cc(g)], abrb[:, cc(g), 0], adt[:, cc(g)], ALU.subtract)
                            taken(e.tensor_tensor(pt[:, cc(g)], adt[:, cc(g)], bc(ident, 2, P), ALU.add))
                        for g in range(2):
                            taken(masked("GA", g, ad[:, cc(g)], bc(C("mlow16"), 2, P)))
                        for g in range(2):
                            e.wait_ge(*VE.need(to_dve))
                            taken(e.tensor_tensor(akrk[:, cc(g)].rearrange("p c a t -> p c (a t)"),
                                                  src("GK", g, 512).rearrange("p (c t) -> p c t", c=2),
                                                  bc(C("mrec"), 2, 256), ALU.mult))
                        for g in range(2):
                            taken(masked("VT", g, vt[:, cc(g)], bc(head, 2, P)))
                        for name in ("P2", "P3", "P4", "Q", "T"):
                            for g in range(2):
                                add(name, g, pt, pt[:, cc(g)])
                        for g in range(2):
                            add("PHI", g, ad, bc(ident, 2, P))
                        for g in range(2):
                            add("E", g, adt, ar[:, cc(g), 1])
                        for c in range(4):
                            e.wait_ge(*VE.need(to_dve))
                            taken(e.tensor_scalar(st[:, (c + 1) % 2], ps[:, b["S", half, c], :P],
                                                  wend[:, ds(NC * i + 4 * half + c, 1)], None, ALU.mult))
                            if c < 3 and (half == 0 or more):
                                diagonal(e, i + half, 1 - half, 2 * c)
                                diagonal(e, i + half, 1 - half, 2 * c + 1)
                        own(e)
                VE.loop(dve, KT - 1, turn_of)
                turn_of(dve, KT - 1, more=False)

                def centre(e, i):
                    for j in range(2):
                        rx, kx = (tile_of(z, 2 * i + j) for z in (r_sb, k_sb))
                        e.scalar_tensor_tensor(tb[:, j], rx, pv(2 * i + j, 2), kx, ALU.mult,
                                               ALU.mult).then_inc(*VE.up(sem("rk_ready")))
                    for j in range(2):
                        yx = tile_of(w_sb, 2 * i + j)
                        e.wait_ge(*VE.need(sem("mean_ready")))
                        e.scalar_tensor_tensor(yx, ps[:, j], -1.0 / 64, yx, ALU.mult,
                                               ALU.add).then_inc(*VE.up(sem(f"centred{j}")))
                    for j in range(2):
                        vx = tile_of(v_sb, 2 * i + j)
                        e.wait_ge(*VE.need(sem("bonus_ready")))
                        e.tensor_tensor(vx, ps[:, 2 + j], vx, ALU.mult).then_inc(*VE.up(sem(f"bonus_used{j}")))
                VE.loop(dve, KT // 2, centre)
                inverse(False)

                def finish(e, i):
                    for j in range(2):
                        e.wait_ge(*VE.need(sem("scale_spread")))
                        e.tensor_tensor(zb[:, j], tile_of(w_sb, 2 * i + j), ps[:, j],
                                        ALU.mult).then_inc(*VE.up(sem(f"scale_used{j}")))
                    own(e)
                    for j in range(2):
                        e.tensor_scalar(zb[:, j], zb[:, j], pv(2 * i + j, 3), pv(2 * i + j, 4), ALU.mult,
                                        ALU.add).then_inc(*VE.up(chain))
                    own(e)
                    for j in range(2):
                        e.tensor_tensor(tile_of(r_sb, 2 * i + j), zb[:, j], tile_of(v_sb, 2 * i + j),
                                        ALU.add).then_inc(*VE.up(chain))
                    own(e)
                VE.loop(dve, KT // 2, finish)

        def linear(e, name, xhi, xlo, part=(0, None), nk=8, width=256, **kw):
            n = [c for _, m, c in plan if m == name][0]
            lo, hi = part[0], part[1] or n
            q = firsts[name][1] + lo
            if hi - lo <= 2:
                for j in range(hi - lo):
                    block_of(e, q + j, 0, xhi, xlo, nk, width, **kw)
                return

            def two(f, i):
                for j in range(2):
                    block_of(f, q + j, 2 * i, xhi, xlo, nk, width, **kw)
            PE.loop(e, (hi - lo) // 2, two)

        def one_of(buf, i):
            return buf[:, ds(i, 1)].rearrange("p a t -> p (a t)")

        def add_to_x(e, gate, n=KT):
            def four(f, i):
                for j in range(4):
                    b = bank()
                    f.wait_ge(*VE.need(acc_ready))
                    xt = one_of(x_sb, 4 * i + j)
                    f.scalar_tensor_tensor(xt, ps[:, b], gate(4 * i + j), xt, ALU.mult,
                                           ALU.add).then_inc(*VE.up(acc_free[b]))
            VE.loop(e, n // 4, four)

        phase_start()
        yg = tiles("yg", 24, 2)
        with nc.Block() as block:
            names = ("g2", "wo")

            @block.sync
            def _(sp):
                load_weights(sp, ahead(*names)[0])

            @block.gpsimd
            def _(pool):
                split_weights(pool, ahead(*names)[1])

            @block.tensor
            def _(pe):
                block_of(pe, firsts["g2"][1], 0, sgh, sgl, 2, D)
                pe.wait_ge(*PE.need(sem("x_ready"), KT))
                linear(pe, "wo", hh, hl)

            @block.scalar
            def _(act):
                for k in range(KT):
                    act.wait_ge(*AC.need(acc_free[k % NACC]))
                    act.activation(hh[:, k], yg[:, k % 2], ACT.Copy).then_inc(*AC.up(sem("rounded")))
                act.dma_start(x_sb[:], A["xT"]).then_inc(*AC.up16(sem("x_again")))

            @block.vector
            def _(dve):
                for k in range(KT + 1):
                    if k < KT:
                        b = bank()
                        if k >= 2:
                            dve.wait_ge(*VE.last())
                        dve.wait_ge(*VE.need(acc_ready))
                        dve.tensor_tensor(yg[:, k % 2], ps[:, b], r_sb[:, k], ALU.mult).then_inc(*VE.up(acc_free[b]))
                    if k:
                        dve.wait_ge(*VE.need(sem("rounded")))
                        dve.tensor_tensor(hl[:, k - 1], yg[:, (k - 1) % 2], hh[:, k - 1].bitcast(F32),
                                          ALU.subtract).then_inc(*VE.up(sem("x_ready")))
                chain = sem("dve")
                cp = ps[:, 7]
                for to, src, bias in ((mod[0][:, 16:], cp[:, 0:32], V("modb0", 16, 32)),
                                      (mod[1][:], cp[:, 32:80], V("modb1")), (kvm[:], cp[:, 80:96], V("kvmb")),
                                      (ada0[:, 0], cp[:, 96:120], V("adab0")), (ada0[:, 1], cp[:, 144:168], V("adab0")),
                                      (ada1[:], cp[:, 120:144], V("adab1"))):
                    dve.tensor_tensor(to, src, bias, ALU.add).then_inc(*VE.up(chain))
                dve.wait_ge(*VE.last())
                for i in range(2):
                    for c in (16, 40):
                        dve.tensor_scalar(mod[i][:, c:c + 8], mod[i][:, c:c + 8], 1.0, None,
                                          ALU.add).then_inc(*VE.up(chain))
                for j, g, sc in ((1, "nmlp0", mod[0][:, 32:40]), (2, "nmix1", mod[1][:, 8:16]),
                                 (3, "nmlp1", mod[1][:, 32:40]), (4, "kvn", kvm[:, 8:16]), (5, "n20", ada0[:, 0, 8:16]),
                                 (6, "n20", ada0[:, 1, 8:16]), (7, "n21", ada1[:, 8:16])):
                    gains(dve, j, V(g), sc)
                dve.wait_ge(*VE.last())
                dve.wait_ge(*VE.need(sem("x_again"), 16))
                add_to_x(dve, lambda m: mod[0][:, ds(16 + m, 1)])

        def norm_phase(gain_no, shift, names=()):
            phase_start()
            with nc.Block() as block:
                @block.vector
                def _(dve):
                    norm_dve(dve, lambda k: x_sb[:, k], lambda k: coef[:, gain_no, k:k + 1],
                             lambda k: shift[:, k:k + 1], hi=lambda k: hh[:, k], lo=lambda k: hl[:, k])

                @block.scalar
                def _(act):
                    norm_act(act, lambda k: x_sb[:, k], 7, lambda k: shift[:, k:k + 1], hi=lambda k: hh[:, k])

                @block.tensor
                def _(pe):
                    norm_pe(pe, 7)

        midh = [tiles(f"midh{b}", 32 + 16 * b, KT, F32R) for b in range(2)]
        midl = [tiles(f"midl{b}", 40 + 16 * b, KT, F32R) for b in range(2)]
        relu, rsq = tiles("relu", 64, 4), tiles("rsq", 68, 4)

        def mlp_phase(layer):
            order = [("up", 0), ("up", 1), ("down", 0), ("up", 2), ("down", 1), ("up", 3), ("down", 2), ("down", 3)]
            names = [f"mlp{layer}_{j}" for j in range(8)]
            phase_start()
            with nc.Block() as block:
                @block.sync
                def _(sp):
                    load_weights(sp, ahead(*names)[0])

                @block.gpsimd
                def _(pool):
                    split_weights(pool, ahead(*names)[1])

                @block.tensor
                def _(pe):
                    for name, (what, q) in zip(names, order):
                        if what == "up":
                            linear(pe, name, hh, hl)
                        else:
                            pe.wait_ge(*PE.need(sem("mid_ready"), KT))
                            linear(pe, name, midh[q % 2], midl[q % 2])

                @block.scalar
                def _(act):
                    for what, q in order:
                        if what == "down":
                            AC.skip(acc_ready, KT)
                            for b in range(NACC):
                                AC.skip(acc_free[b], KT // NACC)
                            turn["evac"] += KT
                            continue

                        def four(e, i):
                            for j in range(4):
                                b = bank()
                                e.wait_ge(*AC.need(acc_ready))
                                e.activation(relu[:, j], ps[:, b], ACT.Relu).then_inc(*AC.up(acc_free[b]))
                                e.wait_ge(*AC.need(acc_free[b]))
                                for w in AC.again(sem("mid_ready")):
                                    e.wait_ge(*w)
                                e.activation(rsq[:, j], relu[:, j], ACT.Square).then_inc(*AC.up(sem("squared")))
                                e.wait_ge(*AC.last())
                                settle(e)
                                e.activation(one_of(midh[q % 2], 4 * i + j), rsq[:, j],
                                             ACT.Copy).then_inc(*AC.up(sem("mid_high")))
                        AC.loop(act, 2, four)

                @block.vector
                def _(dve):
                    for what, q in order:
                        if what == "down":
                            add_to_x(dve, lambda m: mod[layer][:, ds(40 + m, 1)])
                            continue
                        VE.skip(acc_ready, KT)
                        turn["evac"] += KT

                        def four(e, i):
                            for j in range(4):
                                e.wait_ge(*VE.need(sem("mid_high")))
                                e.tensor_tensor(one_of(midl[q % 2], 4 * i + j), rsq[:, j],
                                                one_of(midh[q % 2], 4 * i + j).bitcast(F32),
                                                ALU.subtract).then_inc(*VE.up(sem("mid_ready")))
                        VE.loop(dve, 2, four)

        norm_phase(1, mod[0][:, 24:32])
        mlp_phase(0)

        kk_sb, q_sb, g_sb = tiles("kk_sb", 32, KT), tiles("q_sb", 48, KT), tiles("g_sb", 56, KT)
        vtok = tiles("vtok", 40, shape=[P, 4, D])
        f16 = tiles("f16", 64, shape=[16, 4, T])
        fneg = tiles("fneg", 68, shape=[16, T])
        ftok = fixed("ftok", [P, 4, 16])
        norm_phase(4, kvm[:, 0:8])
        phase_start()
        with nc.Block() as block:
            names = ("kvk", "kvf", "kvv")

            @block.sync
            def _(sp):
                load_weights(sp, ahead(*names)[0])

            @block.gpsimd
            def _(pool):
                split_weights(pool, ahead(*names)[1])

            @block.tensor
            def _(pe):
                linear(pe, "kvk", hh, hl)
                block_of(pe, firsts["kvf"][1], 0, hh, hl, KT, P)
                for j in range(4):
                    tokens_of(pe, firsts["kvv"][1] + j, 0, hh, hl)

            @block.scalar
            def _(act):
                for k in range(KT):
                    b = bank()
                    act.wait_ge(*AC.need(acc_ready))
                    act.activation(kk_sb[:, k], ps[:, b], ACT.Copy).then_inc(*AC.up(acc_free[b]))
                b = bank()
                act.wait_ge(*AC.need(acc_ready))
                act.activation(f16[:, 0], ps[:16, b], ACT.Identity, bias=V("fb")[:16]).then_inc(*AC.up(acc_free[b]))
                act.wait_ge(*AC.last())
                act.activation(f16[:, 1], f16[:, 0], ACT.Abs).then_inc(*AC.up(sem("f_z")))
                act.wait_ge(*AC.last())
                act.activation(f16[:, 1], f16[:, 1], ACT.Exp, scale=-1.0).then_inc(*AC.up(sem("f_z")))
                act.wait_ge(*AC.last())
                act.activation(f16[:, 1], f16[:, 1], ACT.Ln, bias=1.0).then_inc(*AC.up(sem("f_z")))

            @block.vector
            def _(dve):
                VE.skip(acc_ready, KT + 1)
                chain = sem("dve")
                dve.memset(f16[:, 3], 1.0).then_inc(*VE.up(chain))
                dve.wait_ge(*VE.need(sem("f_z"), 3))
                dve.tensor_scalar(f16[:, 2], f16[:, 0], 0.0, None, ALU.min).then_inc(*VE.up(chain))
                dve.wait_ge(*VE.last())
                dve.tensor_tensor(f16[:, 2], f16[:, 2], f16[:, 1], ALU.subtract).then_inc(*VE.up(chain))
                dve.wait_ge(*VE.last())
                dve.tensor_tensor_scan(f16[:, 0], f16[:, 3], f16[:, 2], 0.0, ALU.mult, ALU.add).then_inc(*VE.up(chain))
                dve.wait_ge(*VE.last())
                dve.tensor_scalar(fneg[:], f16[:, 0], -1.0, None, ALU.mult).then_inc(*VE.up(chain))
                turn["evac"] = KT + 1
                for j in range(4):
                    for t in range(4):
                        b = bank()
                        dve.wait_ge(*VE.need(acc_ready))
                        dve.tensor_copy(vtok[:, t, 256 * j:256 * j + 256],
                                        ps[:, b, :256]).then_inc(*VE.up(acc_free[b]))

        norm_phase(2, mod[1][:, 0:8])
        phase_start()
        with nc.Block() as block:
            @block.sync
            def _(sp):
                load_weights(sp, ahead("fq")[0])

            @block.gpsimd
            def _(pool):
                split_weights(pool, ahead("fq")[1])

            @block.tensor
            def _(pe):
                linear(pe, "fq", hh, hl)

            @block.scalar
            def _(act):
                for to, func in ((q_sb, ACT.Copy), (g_sb, ACT.Sigmoid)):
                    def four(e, i):
                        for j in range(4):
                            b = bank()
                            e.wait_ge(*AC.need(acc_ready))
                            settle(e)
                            e.activation(one_of(to, 4 * i + j), ps[:, b], func).then_inc(*AC.up(acc_free[b]))
                    AC.loop(act, 2, four)

        fall = tiles("fall", 8, 16)
        qk_sq = tiles("qk_sq", 72, 2)
        qk_rms = tiles("qk_rms", 30, shape=[P, 2, 64])
        rows = tiles("rows", 26, shape=[16, 2, T])
        phase_start()
        with nc.Block() as block:
            @block.tensor
            def _(pe):
                for t in range(4):
                    o = pe.transpose(ps[:, 7, 16 * t:16 * t + 16], f16[:, 0, P * t:P * t + P], ident[:16, :16])
                o.then_inc(*PE.up(sem("f_turned")))

                def two_heads(e, i):
                    for j in range(2):
                        e.wait_ge(*PE.need(sem("qk_squared")))
                        for t in range(4):
                            o = e.matmul(ps[:, 5 + j, ds(2 * i + 16 * t, 2)], qk_sq[:, j, P * t:P * t + P],
                                         head[:, 0:P:64], start=True, stop=True)
                        o.then_inc(*PE.up(sem("qk_sum")))
                PE.loop(pe, KT, two_heads)
                for h in range(16):
                    for w in PE.again(acc_free[h % 4]):
                        pe.wait_ge(*w)
                    pe.matmul(ps[:, h % 4], ident[:16, h:h + 1].broadcast_to([16, P]), fneg[:], start=True,
                              stop=True).then_inc(*PE.up(acc_ready))
                pe.wait_ge(*PE.need(sem("qk_inverse")))
                for j in range(2):
                    for t in range(4):
                        o = pe.transpose(ps[:16, 5 + j, P * t:P * t + P], qk_rms[:, j, 16 * t:16 * t + 16], ident)
                    o.then_inc(*PE.up(sem("qk_rows")))

            @block.scalar
            def _(act):
                def two_heads(e, i):
                    for j, src in enumerate((q_sb, kk_sb)):
                        e.wait_ge(sem("qk_sum"), book.base[sem("qk_sum")] + 2 * i + j - 1)
                        settle(e)
                        e.activation(qk_sq[:, j], one_of(src, i), ACT.Square).then_inc(*AC.up(sem("qk_squared")))
                AC.loop(act, KT, two_heads)
                act.wait_ge(sem("qk_sum"), book.base[sem("qk_sum")] + 2 * KT)
                act.activation(qk_rms[:], ps[:, 5:7, :64], ACT.Sqrt, bias=C("epsn"),
                               scale=1.0 / 64).then_inc(*AC.up(sem("qk_rms")))
                for h in range(16):
                    act.wait_ge(*AC.need(acc_ready))
                    act.activation(fall[:, h], ps[:, h % 4], ACT.Copy).then_inc(*AC.up(acc_free[h % 4]))
                act.wait_ge(*AC.need(sem("qk_rows"), 2))
                act.activation(rows[:], ps[:16, 5:7], ACT.Copy).then_inc(*AC.up(sem("rows_ready")))

            @block.vector
            def _(dve):
                dve.wait_ge(*VE.need(sem("f_turned")))
                dve.tensor_copy(ftok[:], ps[:, 7, :64].rearrange("p (t h) -> p t h", h=16)).then_inc(*VE.up(sem("dve")))
                dve.wait_ge(*VE.need(sem("qk_rms")))
                dve.reciprocal(qk_rms[:], qk_rms[:]).then_inc(*VE.up(sem("qk_inverse")))

        qn, kn = tiles("qn", 24, shape=[P, T]), tiles("kn", 25, shape=[P, T])
        vp = tiles("vp", 28, shape=[P, 4, P])
        otile = tiles("otile", 29, shape=[P, T])
        sc, pr = tiles("sc", 64, 4), tiles("pr", 68, 2)
        ptr = tiles("ptr", 70, 4)
        oh, ol = tiles("oh", 48, KT, F32R), tiles("ol", 32, KT, F32R)
        sm = fixed("sm", [P, 4, 3])
        qgs = fixed("qgs", [P, 1])
        ftp = fixed("ftp", [P, 4, 2])
        items = [(h, t) for h in range(2) for t in range(4)]
        NI = len(items)
        score_bank = [0, 1, 2, 0, 1, 2, 0, 1]
        phase_start()
        scored, read, turned_read = sem("scores"), sem("scores_read"), sem("turned_read")
        with nc.Block() as block:
            @block.tensor
            def _(pe):
                def prepare(e):
                    e.wait_ge(*PE.need(sem("pair_ready")))
                    for j, b in enumerate((3, 7)):
                        o = e.matmul(ps[:, b], pair_sel[:], rows[:, j], start=True, stop=True)
                    o.then_inc(*PE.up(sem("scale_ready")))
                    e.wait_ge(*PE.need(sem("qk_normed")))

                def scores(e, i, n, free=None):
                    h, t = items[n]
                    rr = slice(64 * h, 64 * h + 64)
                    if free is not None:
                        e.wait_ge(read, book.base.get(read, 0) + NI * i + free + 1)
                    e.matmul(ps[:, score_bank[n], :P * (t + 1)], qn[rr, P * t:P * t + P], kn[rr, :P * (t + 1)],
                             start=True, stop=True).then_inc(*PE.up(scored))

                def turned(e, i, n):
                    h, t = items[n]
                    e.wait_ge(*PE.need(sem("p_ready")))
                    if n >= 2:
                        e.wait_ge(turned_read, book.base.get(turned_read, 0) + NI * i + n - 1)
                    for s in range(t + 1):
                        o = e.transpose(ps[:, 4 + n % 2, P * s:P * s + P], pr[:, n % 2, P * s:P * s + P], ident)
                    o.then_inc(*PE.up(sem("p_turned")))

                def values(e, i, h):
                    rr = slice(64 * h, 64 * h + 64)
                    if h == 0:
                        e.wait_ge(*PE.need(sem("v_copied")))
                        e.wait_ge(sem("o_gated"), book.base.get(sem("o_gated"), 0) + 2 * i)
                    e.wait_ge(turned_read, book.base.get(turned_read, 0) + NI * i + 4 * h + 4)
                    for s in range(4):
                        o = e.matmul(ps[rr, 6, P * s:], vp[:, s, rr], ptr[:, s, P * s:], start=s == 0, stop=s == 3)
                    o.then_inc(*PE.up(sem("o_done")))

                def turn_of(e, i, more=True):
                    scores(e, i, 2)
                    for n in range(NI):
                        if n + 3 < NI:
                            scores(e, i, n + 3, n)
                        elif more and n == 5:
                            prepare(e)
                        elif more:
                            scores(e, i, n - 6, n)
                        if n == 4:
                            values(e, i, 0)
                        turned(e, i, n)
                    values(e, i, 1)
                prepare(pe)
                scores(pe, 0, 0)
                scores(pe, 0, 1)
                PE.loop(pe, KT - 1, turn_of)
                turn_of(pe, KT - 1, more=False)

            @block.scalar
            def _(act):
                def select(e, i):
                    for h in range(2):
                        src = ident[:16, ds(2 * i + h, 1)] if not isinstance(i, int) else ident[:16, 2 * i + h:2 * i + h + 1]
                        o = e.activation(pair_sel[:, 64 * h:64 * h + 64], src.broadcast_to([16, 64]), ACT.Copy)
                    o.then_inc(*AC.up(sem("pair_ready")))

                def exp(e, n):
                    h, t = items[n]
                    w = P * (t + 1)
                    e.wait_ge(*AC.need(sem("max_ready")))
                    e.activation(pr[:, n % 2, :w], sc[:, n % 4, :w], ACT.Exp, bias=sm[:, n % 4, 0:1],
                                 accum_out=sm[:, n % 4, 1:2]).then_inc(*AC.up(sem("exp_done")))

                def turn_of(e, i, more=True):
                    for n, (h, t) in enumerate(items):
                        if n + 1 < NI:
                            exp(e, n + 1)
                        elif more:
                            exp(e, 0)
                        e.wait_ge(*AC.need(sem("p_turned")))
                        e.activation(ptr[:, 0:t + 1, P * t:P * t + P], ps[:, 4 + n % 2, :P * (t + 1)].rearrange(
                            "p (s t) -> p s t", t=P), ACT.Copy).then_inc(*AC.up(turned_read))
                        if n == 0:
                            e.activation(vp[:], vtok[:, :, ds(i * P, P)], ACT.Copy).then_inc(*AC.up(sem("v_copied")))
                        if n == 1 and more:
                            select(e, i + 1)
                select(act, 0)
                exp(act, 0)
                AC.loop(act, KT - 1, turn_of)
                turn_of(act, KT - 1, more=False)

            @block.vector
            def _(dve):
                chain = sem("dve")
                dve.tensor_scalar(qgs[:], V("qg", 0), 0.125, None, ALU.mult).then_inc(*VE.up(chain))
                dve.wait_ge(*VE.last())

                def step(e, o, s=chain):
                    o.then_inc(*VE.up(s))
                    e.wait_ge(*VE.last())

                def prepare(e, i):
                    e.tensor_copy(ftp[:], ftok[:, :, ds(2 * i, 2)]).then_inc(*VE.up(chain))
                    e.wait_ge(*VE.need(sem("scale_ready")))
                    e.scalar_tensor_tensor(qn[:], one_of(q_sb, i), qgs[:, 0:1], ps[:, 3], ALU.mult,
                                           ALU.mult).then_inc(*VE.up(chain))
                    step(e, e.scalar_tensor_tensor(kn[:], one_of(kk_sb, i), V("kg", 0), ps[:, 7], ALU.mult,
                                                   ALU.mult), sem("qk_normed"))

                def softmax(e, i, n):
                    h, t = items[n]
                    k, w = n % 4, P * (t + 1)
                    e.wait_ge(*VE.need(scored))
                    step(e, e.scalar_tensor_tensor(sc[:, k, :w], ps[:, score_bank[n], :w], ftp[:, t, h:h + 1],
                                                   one_of(fall, 2 * i + h)[:, :w], ALU.add, ALU.add), read)
                    step(e, e.tensor_tensor(sc[:, k, P * t:w], sc[:, k, P * t:w], C("causal"), ALU.add))
                    e.tensor_reduce(sm[:, k, 0:1], sc[:, k, :w], AX.X, ALU.max,
                                    negate=True).then_inc(*VE.up(sem("max_ready")))

                def divide(e, n):
                    h, t = items[n]
                    k, w = n % 4, P * (t + 1)
                    e.wait_ge(*VE.need(sem("exp_done")))
                    step(e, e.reciprocal(sm[:, k, 2:3], sm[:, k, 1:2]))
                    e.tensor_scalar(pr[:, n % 2, :w], pr[:, n % 2, :w], sm[:, k, 2:3], None,
                                    ALU.mult).then_inc(*VE.up(sem("p_ready")))

                def gate(e, i, h):
                    rr = slice(64 * h, 64 * h + 64)
                    e.wait_ge(*VE.need(sem("o_done")))
                    step(e, e.tensor_tensor(otile[rr], ps[rr, 6], one_of(g_sb, i)[rr], ALU.mult), sem("o_gated"))

                def turn_of(e, i, more=True):
                    for n in range(NI):
                        divide(e, n)
                        if n + 2 < NI:
                            softmax(e, i, n + 2)
                        elif more:
                            softmax(e, i + 1, n - 6)
                        if n == 5 and more:
                            prepare(e, i + 1)
                        if n == 5:
                            gate(e, i, 0)
                    gate(e, i, 1)
                    step(e, e.tensor_copy(one_of(oh, i), otile[:]))
                    step(e, e.tensor_tensor(one_of(ol, i), otile[:], one_of(oh, i).bitcast(F32), ALU.subtract))
                prepare(dve, 0)
                softmax(dve, 0, 0)
                softmax(dve, 0, 1)
                VE.loop(dve, KT - 1, turn_of)
                turn_of(dve, KT - 1, more=False)

        phase_start()
        with nc.Block() as block:
            @block.sync
            def _(sp):
                load_weights(sp, ahead("fo")[0])

            @block.gpsimd
            def _(pool):
                split_weights(pool, ahead("fo")[1])

            @block.tensor
            def _(pe):
                linear(pe, "fo", oh, ol)

            @block.vector
            def _(dve):
                add_to_x(dve, lambda m: mod[1][:, ds(16 + m, 1)])
        norm_phase(3, mod[1][:, 24:32])
        mlp_phase(1)

        def plain_norm(x, g, out_tiles):
            phase_start()
            with nc.Block() as block:
                @block.vector
                def _(dve):
                    norm_dve(dve, lambda k: x[:, k], lambda k: g[:, k:k + 1],
                             plain=lambda k: out_tiles[:, k])

                @block.scalar
                def _(act):
                    norm_act(act, lambda k: x[:, k], 7)

                @block.tensor
                def _(pe):
                    norm_pe(pe, 7)
        plain_norm(x_sb, V("final"), x_sb)

        h2h, h2l = (tiles(n, a, dt=F32R, shape=[P, KT, TA]) for n, a in (("h2h", 8), ("h2l", 20)))
        sq, rms, nt = (tiles(n, 60 + 2 * j, 2) for j, n in enumerate(("sq2", "rms2", "nt2")))
        ctx_sb = tiles("ctx_sb", 56, shape=[P, KT, TX])
        LAT = slice(TX, TA)
        d_keep = nc.dram_tensor("d_keep", (P, KT, T), F32, kind="Internal").ap()
        for src, gain_no, shift, part, n in ((x_sb, 5, ada0[:, 0, 0:8], LAT, T), (ctx_sb, 6, ada0[:, 1, 0:8],
                                                                                   slice(0, TX), TX)):
            phase_start()
            with nc.Block() as block:
                @block.sync
                def _(sp):
                    if n == TX:
                        sp.dma_start(d_keep, x_sb[:]).then_inc(*SP.up16(sem("x_kept")))
                        sp.wait_ge(*SP.need(sem("x_kept"), 16))

                @block.vector
                def _(dve):
                    norm_dve(dve, lambda k: src[:, k], lambda k: coef[:, gain_no, k:k + 1],
                             lambda k: shift[:, k:k + 1], n=n, hi=lambda k: h2h[:, k, part],
                             lo=lambda k: h2l[:, k, part])

                @block.scalar
                def _(act):
                    norm_act(act, lambda k: src[:, k], 7, lambda k: shift[:, k:k + 1], n=n, hi=lambda k: h2h[:, k, part])
                    if n == T:
                        act.dma_start(ctx_sb[:], A["cT"]).then_inc(*AC.up16(sem("ctx_loaded")))
                        act.wait_ge(*AC.last())

                @block.tensor
                def _(pe):
                    norm_pe(pe, 7, n=n)

        HM = 4
        xms = [tiles(f"xm{j}", at, shape=[P, 4, TA]) for j, at in enumerate((32, 0))]
        qx, kx2 = (tiles(n, a, shape=[P, 4, TA]) for n, a in (("qx", 55), ("kx2", 61)))
        xch, xcl = tiles("xch", 38, dt=F32R, shape=[P, 4, TA]), tiles("xcl", 44, dt=F32R, shape=[P, 4, TA])
        xc = tiles("xc", 50, shape=[P, 2, TA])
        gacc = tiles("gacc", 53, shape=[P, TA])
        rowt = fixed("rowt", [P, NACC])
        ssb = tiles("ssb", 67, 6)
        d_s = nc.dram_tensor("d_s", (4, P, 6, T), F32, kind="Internal").ap()
        d_v = nc.dram_tensor("d_v", (4, P, 6, T), F32, kind="Internal").ap()
        d_x = nc.dram_tensor("d_x", (4, P, 4, T), F32, kind="Internal").ap()
        d_h = nc.dram_tensor("d_h", (4, P, 4, T), F32, kind="Internal").ap()
        spans = ((0, TX), (TX, T))
        KS = 512 ** -0.5
        order = [("xm", 0, n) for n in range(8)]
        for h in range(HM):
            order += [("xm", h + 1, n) for n in range(8) if h + 1 < HM]
            order += [(what, h, n) for what, many in (("v", 6), ("q", 8), ("k", 8), ("s", 6)) for n in range(many)]
        place = {what: j for j, what in enumerate(order)}
        phase_start()
        with nc.Block() as block:
            names = [f"{n}{h}" for n in ("xm", "q", "k", "gate") for h in range(HM)]
            acc_taken = sem("acc_taken")

            def taken(what, h, n):
                return acc_taken, book.base.get(acc_taken, 0) + place[what, h, n] + 1

            @block.sync
            def _(sp):
                load_weights(sp, ahead(*names)[0])

            @block.gpsimd
            def _(pool):
                split_weights(pool, ahead(*names)[1])

            @block.tensor
            def _(pe):
                made = [0]

                def bank_free():
                    made[0] += 1
                    return [taken(*order[made[0] - 1 - NACC])] if made[0] > NACC else []

                def tile_bank():
                    b = turn["acc"] % NACC
                    turn["acc"] += 1
                    for w in bank_free():
                        pe.wait_ge(*w)
                    return b

                def xm_of(h):
                    for j in range(2):
                        block_of(pe, firsts[f"xm{h}"][1] + j, 0, h2h, h2l, KT, 256, tokens=spans, bank_free=bank_free)
                xm_of(0)
                for h in range(HM):
                    xm = xms[h % 2]
                    if h + 1 < HM:
                        xm_of(h + 1)
                    for s in range(6):
                        b = tile_bank()
                        for m in range(4):
                            o = pe.transpose(ps[:, b, P * m:P * m + P], xm[:, m, P * s:P * s + P], ident)
                        o.then_inc(*PE.up(acc_ready))
                    pe.wait_ge(*PE.need(sem("xc_ready"), 4))
                    for n in "qk":
                        block_of(pe, firsts[f"{n}{h}"][1], 0, xch, xcl, 4, 512, tokens=spans, bank_free=bank_free)
                    pe.wait_ge(*taken("k", h, 7))
                    r = firsts[f"gate{h}"][0]
                    pe.wait_ge(w_full[r % RAW], (r // 2 + 1) * 16)
                    if h:
                        pe.wait_ge(*PE.need(sem("gates_read")))
                    wg = wraw[:, r % RAW, :12 * P].rearrange("p (k c) -> p k c", k=12)
                    for b, (t0, nt_) in zip((4, 5), spans):
                        for j, src in enumerate((qx, kx2, xm)):
                            for m in range(4):
                                o = pe.matmul(ps[:, b, :nt_], wg[:, 4 * j + m], src[:, m, t0:t0 + nt_],
                                              start=j == 0 and m == 0, stop=j == 2 and m == 3)
                    o.then_inc(w_cond, 1)
                    for s in range(6):
                        b = tile_bank()
                        for m in range(4):
                            o = pe.matmul(ps[:, b], kx2[:, m, P * s:P * s + P], qx[:, m, LAT], start=m == 0,
                                          stop=m == 3)
                        o.then_inc(*PE.up(acc_ready))

            @block.scalar
            def _(act):
                def read_out(dst, n, **kw):
                    b = bank()
                    act.wait_ge(*AC.need(acc_ready))
                    act.activation(dst, ps[:, b, :n], ACT.Copy, **kw).then_inc(*AC.up(acc_taken))

                def xm_tile(h, m):
                    for t0, n in spans:
                        read_out(xms[h % 2][:, m, t0:t0 + n], n)

                def silu(h, m):
                    act.wait_ge(*AC.need(sem("conv_done")))
                    act.activation(xc[:, m % 2], xc[:, m % 2], ACT.Silu,
                                   bias=V("convb", 4 * h + m)).then_inc(*AC.up(sem("silu")))
                    act.wait_ge(*AC.last())
                    act.dma_start(d_x[h, :, m], xc[:, m % 2, LAT]).then_inc(*AC.up16(sem(f"skip_sent{m % 2}")))
                    act.activation(xch[:, m], xc[:, m % 2], ACT.Copy).then_inc(*AC.up(sem("xc_high")))
                for m in range(4):
                    xm_tile(0, m)
                for h in range(HM):
                    for m in range(4):
                        if h + 1 < HM:
                            xm_tile(h + 1, m)
                        silu(h, m)
                    if h:
                        act.wait_ge(*AC.need(sem("s_sent"), 16))
                    for s in range(6):
                        read_out(ssb[:, s], T)
                    act.wait_ge(*taken("v", h, 5))
                    act.dma_start(d_v[h], ssb[:]).then_inc(*AC.up16(sem("v_sent")))
                    for to, f in ((qx, 1.0), (kx2, KS)):
                        for m in range(4):
                            for t0, n in spans:
                                read_out(to[:, m, t0:t0 + n], n, scale=f)
                    act.wait_ge(*AC.need(sem("v_sent"), 16))
                    for s in range(6):
                        read_out(ssb[:, s], T)
                    act.wait_ge(*taken("s", h, 5))
                    act.dma_start(d_s[h], ssb[:]).then_inc(*AC.up16(sem("s_sent")))
                act.wait_ge(*AC.need(sem("s_sent"), 16))
                for j in range(2):
                    act.wait_ge(*AC.need(sem(f"skip_sent{j}"), 16 * 2 * HM))

            @block.vector
            def _(dve):
                chain = sem("dve")
                dve.memset(gacc[:], 0.0).then_inc(*VE.up(chain))
                dve.wait_ge(*VE.last())

                def conv(h, m):
                    dve.wait_ge(*taken("xm", h, 2 * m + 1))
                    if h or m >= 2:
                        dve.wait_ge(*VE.need(sem(f"skip_sent{m % 2}"), 16))
                    y, z = xc[:, m % 2], xms[h % 2][:, m]

                    def w(kh, kw):
                        return V("convw", 9 * (4 * h + m) + 3 * kh + kw)

                    def add(kh, kw, dst, src, s=chain):
                        dve.wait_ge(*VE.last())
                        dve.scalar_tensor_tensor(dst, src, w(kh, kw), dst, ALU.mult, ALU.add).then_inc(*VE.up(s))
                    dve.tensor_scalar(y, z, w(1, 1), None, ALU.mult).then_inc(*VE.up(chain))
                    add(1, 0, y[:, 1:TX], z[:, 0:TX - 1])
                    add(1, 2, y[:, 0:TX - 1], z[:, 1:TX])
                    yr = y[:, LAT].rearrange("p (r c) -> p r c", c=64)
                    zr = z[:, LAT].rearrange("p (r c) -> p r c", c=64)
                    for kh, kw in [(a, b) for a in range(3) for b in range(3) if (a, b) != (1, 1)]:
                        r0, r1 = max(0, 1 - kh), 8 - max(0, kh - 1)
                        c0, c1 = max(0, 1 - kw), 64 - max(0, kw - 1)
                        add(kh, kw, yr[:, r0:r1, c0:c1], zr[:, r0 + kh - 1:r1 + kh - 1, c0 + kw - 1:c1 + kw - 1],
                            sem("conv_done") if (kh, kw) == (2, 2) else chain)

                def low(m):
                    dve.wait_ge(*VE.need(sem("xc_high")))
                    dve.tensor_tensor(xcl[:, m], xc[:, m % 2], xch[:, m].bitcast(F32),
                                      ALU.subtract).then_inc(*VE.up(sem("xc_ready")))
                    dve.wait_ge(*VE.last())
                for h in range(HM):
                    conv(h, 0)
                    for m in range(1, 4):
                        conv(h, m)
                        low(m - 1)
                    low(3)
                    dve.wait_ge(w_cond, firsts[f"gate{h}"][1] + 1)
                    dve.tensor_tensor(gacc[:, :TX], gacc[:, :TX], ps[:, 4, :TX], ALU.add).then_inc(*VE.up(chain))
                    dve.tensor_tensor(gacc[:, LAT], gacc[:, LAT], ps[:, 5],
                                      ALU.add).then_inc(*VE.up(sem("gates_read")))
                    dve.wait_ge(*VE.last())

        gz, gl = tiles("gz", 55, shape=[P, TA]), tiles("gl", 57, shape=[P, TA])
        li, lf, bcum, gdir, mrun = (tiles(n, 59 + 3 * j, shape=[4, 2, TA]) for j, n in enumerate(
            ("li", "lf", "bcum", "gdir", "mrun")))
        one4 = tiles("one4", 50, shape=[4, TA])
        gnat = tiles("gnat", 32, shape=[4, 2, TA])
        nrow = tiles("nrow", 35, shape=[36, 2, T])
        nmax, nm = nrow[0:4], nrow[32:36]
        gcol = fixed("gcol", [P, 2, 6, 4])
        phase_start()
        with nc.Block() as block:
            @block.scalar
            def _(act):
                act.wait_ge(*AC.need(sem("gz_ready")))
                act.activation(gl[:], gz[:], ACT.Abs).then_inc(*AC.up(sem("gl")))
                act.wait_ge(*AC.last())
                act.activation(gl[:], gl[:], ACT.Exp, scale=-1.0).then_inc(*AC.up(sem("gl")))
                act.wait_ge(*AC.last())
                act.activation(gl[:], gl[:], ACT.Ln, bias=1.0).then_inc(*AC.up(sem("gl")))

            @block.vector
            def _(dve):
                def step(o, s=None):
                    o.then_inc(*VE.up(s or sem("dve")))
                    dve.wait_ge(*VE.last())
                step(dve.tensor_scalar(gz[:], gacc[:], V("bif", 0), None, ALU.add), sem("gz_ready"))
                dve.memset(one4[:], 1.0).then_inc(*VE.up(sem("dve")))
                dve.wait_ge(*VE.need(sem("gl"), 3))
                step(dve.tensor_scalar(gacc[:], gz[:], 0.0, None, ALU.min))
                step(dve.tensor_tensor(gl[:], gacc[:], gl[:], ALU.subtract))

                def ordered(dst, src, d, parts=((0, TX), (TX, TA))):
                    for a, b in parts:
                        view = src[:, a:b]
                        step(dve.tensor_copy(dst[:, a:b], view[:, ::-1] if d else view))
                for d in range(2):
                    ordered(li[:, d], gz[64 * d:64 * d + 4], d)
                    ordered(lf[:, d], gl[64 * d + 32:64 * d + 36], d)
                    step(dve.tensor_tensor_scan(bcum[:, d], one4[:], lf[:, d], 0.0, ALU.mult, ALU.add))
                    step(dve.tensor_tensor(gdir[:, d], li[:, d], bcum[:, d], ALU.subtract))
                    step(dve.tensor_tensor_scan(mrun[:, d], gdir[:, d], gdir[:, d], 0.0, ALU.max, ALU.max))
                    step(dve.tensor_tensor(li[:, d], bcum[:, d], mrun[:, d], ALU.add))
                    ordered(gnat[:, d], gdir[:, d], d)
                    for dst, src in ((nmax, mrun), (nm, li)):
                        view = src[:, d, LAT]
                        step(dve.tensor_scalar(dst[:, d], view[:, ::-1] if d else view, -1.0, None, ALU.mult),
                             sem("gate_rows"))
                dve.wait_ge(*VE.need(sem("g_turned")))
                dve.tensor_copy(gcol[:].rearrange("p d s h -> p (d s h)"), ps[:, 7, :48]).then_inc(*VE.up(sem("dve")))

            @block.tensor
            def _(pe):
                pe.wait_ge(*PE.need(sem("gate_rows"), 4))
                for d in range(2):
                    for s in range(6):
                        o = pe.transpose(ps[:, 7, 24 * d + 4 * s:24 * d + 4 * s + 4], gnat[:, d, P * s:P * s + P],
                                         ident[:4, :4])
                o.then_inc(*PE.up(sem("g_turned")))

        sld, vld, pp = tiles("sld", 40, 6), tiles("vld", 46, 6), tiles("pp", 64, 6)
        sw = tiles("swf", 52, 6), tiles("swr", 58, 6)
        mb = tiles("mb", 32, 2)
        em = tiles("em", 6, 2)
        wt, hsq = tiles("wt", 4, 2), tiles("hsq", 38, 2)
        dev = tiles("dev", 34, 1)
        hb = tiles("hb0", 0, 4), tiles("hb1", 70, 4)

        def region(d, s):
            if s < 2:
                return 0, T
            return (P * (s - 2), T) if d == 0 else (0, P * (s - 1))
        parts = [(s, d) for s in range(6) for d in range(2)]
        phase_start()
        with nc.Block() as block:
            @block.sync
            def _(sp):
                for i in range(HM):
                    if i:
                        sp.wait_ge(*SP.need(sem("sw_ready"), len(parts)))
                    sp.dma_start(sld[:], d_s[i]).then_inc(*SP.up16(sem("s_in")))
                    for m in range(4):
                        if i:
                            sp.wait_ge(*SP.need(sem("h_done")))
                        sp.dma_start(vld[:, :, P * m:P * m + P],
                                     d_v[i, :, :, P * m:P * m + P]).then_inc(*SP.up16(sem(f"v_in{m}")))

            @block.tensor
            def _(pe):
                def spread(i, n):
                    if n == 0 and i >= 2:
                        pe.wait_ge(*PE.need(sem("h_dev")))
                    if n >= 2 or (i == 1 and n == 0):
                        pe.wait_ge(*PE.need(sem("spread_taken"), 1 if n else 2))
                    rr = slice(32 * (n // 2), 32 * (n // 2) + 4)
                    one = ident[rr, 32 * (n // 2) + i:32 * (n // 2) + i + 1].broadcast_to([4, P])
                    pe.matmul(ps[:, 6 + n % 2], one, nrow[rr, n % 2], start=True, stop=True).then_inc(*PE.up(sem("spread")))

                def sums(i, some):
                    for s, d in some:
                        t0, t1 = region(d, s)
                        if i and (s, d) == (0, 0):
                            pe.wait_ge(*PE.need(sem("den_abs"), 2))
                        pe.wait_ge(*PE.need(sem("sw_ready")))
                        o = pe.matmul(ps[:, 4 + d, t0:t1], ones, sw[d][:, s, t0:t1], start=s == 0, stop=s == 5)
                        if s == 5:
                            o.then_inc(*PE.up(sem("den")))

                def values(m):
                    pe.wait_ge(*PE.need(sem(f"v_in{m}"), 16))
                    for s in range(6):
                        if m == 0:
                            pe.wait_ge(*PE.need(sem("p_ready2")))
                        o = pe.matmul(ps[:, m], vld[:, s, P * m:P * m + P], pp[:, s], start=s == 0, stop=s == 5)
                    o.then_inc(*PE.up(sem("h_done")))
                for n in range(4):
                    spread(0, n)
                sums(0, parts)
                for i in range(HM):
                    more = i + 1 < HM
                    if more:
                        spread(i + 1, 0)
                        spread(i + 1, 1)
                    values(0)
                    if more:
                        spread(i + 1, 2)
                        spread(i + 1, 3)
                    values(1)
                    if more:
                        sums(i + 1, parts[:6])
                    values(2)
                    if more:
                        sums(i + 1, parts[6:])
                    values(3)
                    pe.wait_ge(*(PE.need(sem("spread_taken"), 2) if more else PE.need(sem("h_dev"))))
                    for m in range(4):
                        pe.wait_ge(*PE.need(sem("h_taken")))
                        o = pe.matmul(ps[:, 6], ones, hb[i % 2][:, m], start=m == 0, stop=m == 3)
                    o.then_inc(*PE.up(sem("h_sum")))
                    for m in range(4):
                        pe.wait_ge(*PE.need(sem("h_squared")))
                        pe.matmul(ps[:, 7], ones, hsq[:, m % 2], start=m == 0,
                                  stop=m == 3).then_inc(*PE.up(sem("h_square_used")))

            @block.scalar
            def _(act):
                def spread_taken(n):
                    act.wait_ge(*AC.need(sem("spread")))
                    if n < 2:
                        act.activation(mb[:, n], ps[:, 6 + n], ACT.Copy).then_inc(*AC.up(sem("spread_taken")))
                    else:
                        act.activation(em[:, n - 2], ps[:, 4 + n], ACT.Exp).then_inc(*AC.up(sem("spread_taken")))

                def exps(a, b):
                    for n in range(a, b):
                        t0, t1 = region(parts[n][1], parts[n][0])
                        act.wait_ge(*AC.need(sem("w_log")))
                        act.activation(wt[:, n % 2, t0:t1], wt[:, n % 2, t0:t1], ACT.Exp).then_inc(*AC.up(sem("w_exp")))

                def magnitudes():
                    for d in range(2):
                        act.wait_ge(*AC.need(sem("den")))
                        act.activation(mb[:, d], ps[:, 4 + d], ACT.Abs).then_inc(*AC.up(sem("den_abs")))

                def result(i, m):
                    if m == 0 and i >= 2:
                        act.wait_ge(*AC.need(sem("h_sent"), 16))
                    act.wait_ge(*AC.need(sem("h_done")))
                    act.activation(hb[i % 2][:, m], ps[:, m], ACT.Copy).then_inc(*AC.up(sem("h_taken")))

                def send(i):
                    act.wait_ge(*AC.need(sem("h_normed")))
                    act.dma_start(d_h[i], hb[i % 2][:]).then_inc(*AC.up16(sem("h_sent")))
                for n in range(4):
                    spread_taken(n)
                exps(0, 12)
                magnitudes()
                for i in range(HM):
                    more = i + 1 < HM
                    if more:
                        act.wait_ge(*AC.need(sem("divisors")))
                        spread_taken(0)
                        spread_taken(1)
                        exps(0, 4)
                    result(i, 0)
                    if more:
                        act.wait_ge(*AC.need(sem("p_ready2"), 6))
                        spread_taken(2)
                        spread_taken(3)
                        exps(4, 12)
                    if i:
                        send(i - 1)
                    result(i, 1)
                    result(i, 2)
                    if more:
                        magnitudes()
                    result(i, 3)
                    for m in range(4):
                        act.wait_ge(*AC.need(sem("h_centred")))
                        if m >= 2:
                            act.wait_ge(*AC.need(sem("h_square_used")))
                        act.activation(hsq[:, m % 2], hb[i % 2][:, m], ACT.Square).then_inc(*AC.up(sem("h_squared")))
                    act.wait_ge(*AC.need(sem("h_square_used"), 2))
                    act.activation(dev[:, 0], ps[:, 7], ACT.Sqrt, bias=C("epsn"),
                                   scale=1.0 / 512).then_inc(*AC.up(sem("h_dev")))
                send(HM - 1)
                act.wait_ge(*AC.need(sem("h_sent"), 32))

            @block.vector
            def _(dve):
                def step(o, s=None):
                    o.then_inc(*VE.up(s or sem("dve")))
                    dve.wait_ge(*VE.last())

                def weights(i):
                    dve.wait_ge(*VE.need(sem("spread_taken"), 2))
                    dve.wait_ge(*VE.need(sem("s_in"), 16))

                    def log_weight(n):
                        s, d = parts[n]
                        t0, t1 = region(d, s)
                        dve.tensor_scalar(wt[:, n % 2, t0:t1], mb[:, d, t0:t1], gcol[:, d, s, i:i + 1], 0.0, ALU.add,
                                          ALU.min).then_inc(*VE.up(sem("w_log")))
                    log_weight(0)
                    for n, (s, d) in enumerate(parts):
                        t0, t1 = region(d, s)
                        if n + 1 < len(parts):
                            log_weight(n + 1)
                        dve.wait_ge(*VE.need(sem("w_exp")))
                        if s >= 2:
                            diag = slice(P * (s - 2), P * (s - 1))
                            step(dve.tensor_tensor(wt[:, n % 2, diag], wt[:, n % 2, diag], C(("fwd", "rev")[d]), ALU.mult))
                        step(dve.tensor_tensor(sw[d][:, s, t0:t1], wt[:, n % 2, t0:t1], sld[:, s, t0:t1], ALU.mult),
                             sem("sw_ready"))

                def divisors():
                    dve.wait_ge(*VE.need(sem("spread_taken"), 2))
                    for d in range(2):
                        dve.wait_ge(*VE.need(sem("den_abs")))
                        step(dve.tensor_tensor(em[:, d], em[:, d], mb[:, d], ALU.max))
                        step(dve.reciprocal(em[:, d], em[:, d]), sem("divisors") if d else None)

                def divided(last_values):
                    if last_values:
                        dve.wait_ge(*VE.need(sem("h_done"), 4))

                    for s in range(6):
                        f0, r1 = region(0, s)[0], region(1, s)[1]
                        step(dve.tensor_tensor(pp[:, s, f0:], sw[0][:, s, f0:], em[:, 0, f0:], ALU.mult))
                        if f0:
                            dve.tensor_tensor(pp[:, s, :f0], sw[1][:, s, :f0], em[:, 1, :f0],
                                              ALU.mult).then_inc(*VE.up(sem("dve")))
                        step(dve.tensor_tensor(sw[1][:, s, f0:r1], sw[1][:, s, f0:r1], em[:, 1, f0:r1], ALU.mult))
                        dve.tensor_tensor(pp[:, s, f0:r1], pp[:, s, f0:r1], sw[1][:, s, f0:r1],
                                          ALU.add).then_inc(*VE.up(sem("p_ready2")))

                def normed(i):
                    dve.wait_ge(*VE.need(sem("h_dev")))
                    step(dve.reciprocal(dev[:, 0], dev[:, 0]))
                    for m in range(4):
                        o = dve.scalar_tensor_tensor(hb[i % 2][:, m], hb[i % 2][:, m], V("lnw2", 4 * i + m),
                                                     dev[:, 0], ALU.mult, ALU.mult)
                        o.then_inc(*VE.up(sem("h_normed") if m == 3 else sem("dve")))
                weights(0)
                divisors()
                for i in range(HM):
                    divided(i > 0)
                    if i:
                        normed(i - 1)
                    if i + 1 < HM:
                        weights(i + 1)
                        divisors()
                    dve.wait_ge(*VE.need(sem("h_sum")))
                    for m in range(4):
                        dve.scalar_tensor_tensor(hb[i % 2][:, m], ps[:, 6], -1.0 / 512, hb[i % 2][:, m], ALU.mult,
                                                 ALU.add).then_inc(*VE.up(sem("h_centred")))
                    dve.wait_ge(*VE.last())
                normed(HM - 1)

        y_sb = tiles("y_sb", 32, 16)
        skip_sb = tiles("skip_sb", 48, 16)
        yh, yl = tiles("yh", 48, 16, F32R), tiles("yl", 32, 16, F32R)
        gt_, yz = tiles("gt_", 64, 4), tiles("yz", 68, 4)

        def gated(e, func, free=None):
            for j in range(4):
                b = bank()
                for w in free(j) if free else ():
                    e.wait_ge(*w)
                e.wait_ge(*AC.need(acc_ready))
                e.activation(gt_[:, j], ps[:, b], func).then_inc(*AC.up(acc_free[b]))

        phase_start()
        with nc.Block() as block:
            names = ("o",)

            @block.sync
            def _(sp):
                for h in range(4):
                    sp.dma_start(y_sb[:, 4 * h:4 * h + 4], d_h[h]).then_inc(*SP.up16(sem(f"y_in{h}")))
                    sp.dma_start(skip_sb[:, 4 * h:4 * h + 4], d_x[h]).then_inc(*SP.up16(sem(f"skip_in{h}")))
                sp.dma_start(x_sb[:], d_keep).then_inc(*SP.up16(sem("x_back")))
                load_weights(sp, ahead("o")[0])
                sp.wait_ge(*SP.need(sem("x_back"), 16))
                for h in range(4):
                    sp.wait_ge(*SP.need(sem(f"y_in{h}"), 16))
                    sp.wait_ge(*SP.need(sem(f"skip_in{h}"), 16))

            @block.gpsimd
            def _(pool):
                split_weights(pool, ahead("o")[1])

            @block.tensor
            def _(pe):
                linear(pe, "o", h2h, h2l, tokens=((TX, T),))

            @block.scalar
            def _(act):
                AC.loop(act, 4, lambda e, i: gated(e, ACT.Sigmoid, lambda j: AC.again(sem(f"gt_used{j}"))))

            @block.vector
            def _(dve):
                for h in range(4):
                    dve.wait_ge(*VE.need(sem(f"y_in{h}"), 16))
                    dve.wait_ge(*VE.need(sem(f"skip_in{h}"), 16))

                def four(e, i):
                    for j in range(4):
                        y = one_of(y_sb, 4 * i + j)
                        e.wait_ge(*VE.need(acc_free[j]))
                        e.tensor_tensor(y, y, gt_[:, j], ALU.mult).then_inc(*VE.up(sem(f"gt_used{j}")))
                        e.wait_ge(*VE.last())
                        e.scalar_tensor_tensor(y, one_of(skip_sb, 4 * i + j), vec[:, ds(vat["skip"][0] + 4 * i + j, 1)],
                                               y, ALU.mult, ALU.add).then_inc(*VE.up(sem("dve")))
                VE.loop(dve, 4, four)

        def silu_phase(name, xhi, xlo, **kw):
            phase_start()
            with nc.Block() as block:
                @block.sync
                def _(sp):
                    load_weights(sp, ahead(name)[0])

                @block.gpsimd
                def _(pool):
                    split_weights(pool, ahead(name)[1])

                @block.tensor
                def _(pe):
                    linear(pe, name, xhi, xlo, **kw)

                @block.scalar
                def _(act):
                    def four(e, i):
                        gated(e, ACT.Silu)
                        for j in range(4):
                            e.wait_ge(*AC.need(sem(f"gated{j}")))
                            settle(e)
                            e.activation(one_of(yh, 4 * i + j), yz[:, j], ACT.Copy).then_inc(*AC.up(sem("y_high")))
                    AC.loop(act, 4, four)

                @block.vector
                def _(dve):
                    def four(e, i):
                        for j in range(4):
                            e.wait_ge(*VE.need(acc_free[j]))
                            e.tensor_tensor(yz[:, j], one_of(y_sb, 4 * i + j), gt_[:, j],
                                            ALU.mult).then_inc(*VE.up(sem(f"gated{j}")))
                        for j in range(4):
                            e.wait_ge(*VE.need(sem("y_high")))
                            e.tensor_tensor(one_of(yl, 4 * i + j), yz[:, j], one_of(yh, 4 * i + j).bitcast(F32),
                                            ALU.subtract).then_inc(*VE.up(sem("dve")))
                        e.wait_ge(*VE.last())
                    VE.loop(dve, 4, four)

        def wide_out(name, gate):
            phase_start()
            with nc.Block() as block:
                @block.sync
                def _(sp):
                    load_weights(sp, ahead(name)[0])

                @block.gpsimd
                def _(pool):
                    split_weights(pool, ahead(name)[1])

                @block.tensor
                def _(pe):
                    q = firsts[name][1]

                    def pair(e, i):
                        for j in range(2):
                            open_bank = {}
                            for k in range(2):
                                block_of(e, q + 2 * j + k, 4 * i, yh, yl, KT, 256, k0=KT * k, first=k == 0,
                                         final=k == 1, open_bank=open_bank)
                    PE.loop(pe, 2, pair)

                @block.vector
                def _(dve):
                    add_to_x(dve, gate)
        silu_phase("z", h2h, h2l, tokens=((TX, T),))
        wide_out("mo", lambda m: ada0[:, 0, ds(16 + m, 1)])

        dch, dtok = tiles("dch", 24, shape=[P, 2, 512]), tiles("dtok", 64, shape=[P, 2, 4, T])
        u_sb, ucs = tiles("u_sb", 26, 4), tiles("ucs", 48, 8)
        sq, rms, nt = (tiles(n, 24 + 2 * j, 2) for j, n in enumerate(("sq", "rms", "nt")))
        norm_phase(7, ada1[:, 0:8])
        phase_start()
        with nc.Block() as block:
            f_taken, per_turn = sem("f_taken"), 16

            def ftaken(i, n):
                return f_taken, book.base.get(f_taken, 0) + NACC + per_turn * i + n + 1

            @block.sync
            def _(sp):
                sp.dma_start(dch[:].rearrange("p a c -> p (a c)"), A["dch"]).then_inc(*SP.up16(sem("dch_in")))
                sp.dma_start(dtok[:].rearrange("p a b c -> p (a b c)"), A["dtok"]).then_inc(*SP.up16(sem("dtok_in")))
                load_weights(sp, ahead("fu")[0])

            @block.gpsimd
            def _(pool):
                split_weights(pool, ahead("fu")[1])

            @block.tensor
            def _(pe):
                pe.wait_ge(*PE.need(sem("dch_in"), 16))
                pe.wait_ge(*PE.need(sem("dtok_in"), 16))

                def two_groups(e, i):
                    made, seen = [0], [-NACC - 1]

                    def wait_taken(n):
                        if n > seen[0]:
                            e.wait_ge(*ftaken(i, n))
                            seen[0] = n

                    def bank_free():
                        made[0] += 1
                        seen[0] = made[0] - 1 - NACC
                        return [ftaken(i, seen[0])]

                    def tile_bank(operand):
                        b = turn["acc"] % NACC
                        turn["acc"] += 1
                        made[0] += 1
                        wait_taken(max(made[0] - 1 - NACC, operand))
                        return b
                    for h in range(2):
                        block_of(e, firsts["fu"][1] + h, 2 * i, hh, hl, KT, 256, bank_free=bank_free)
                    for h in range(2):
                        for t in range(4):
                            b = tile_bank(2 * h + 1)
                            for k in range(2):
                                o = e.matmul(ps[:, b], u_sb[:, 2 * h + k, P * t:P * t + P], dch[:, k], start=k == 0,
                                             stop=k == 1)
                            o.then_inc(*PE.up(acc_ready))
                    for h in range(2):
                        for m in range(2):
                            b = tile_bank(4 + 4 * h)
                            for t in range(4):
                                wait_taken(4 + 4 * h + t)
                                for c in range(2):
                                    o = e.matmul(ps[:, b], ucs[:, 4 * h + t, 256 * c + P * m:256 * c + P * m + P],
                                                 dtok[:, c, t], start=t == 0 and c == 0, stop=t == 3 and c == 1)
                            o.then_inc(*PE.up(acc_ready))
                PE.loop(pe, 4, two_groups)

            @block.scalar
            def _(act):
                for j in range(NACC):
                    act.activation(rowt[:, j:j + 1], con[:, 0:1], ACT.Copy).then_inc(*AC.up(f_taken))

                def two_groups(e, i):
                    for n in range(per_turn):
                        b = bank()
                        e.wait_ge(*AC.need(acc_ready))
                        if n < 4:
                            to = u_sb[:, n]
                        elif n < 12:
                            to = ucs[:, n - 4]
                        else:
                            to = one_of(y_sb, 4 * i + n - 12)
                            settle(e)
                        e.activation(to, ps[:, b], ACT.Copy).then_inc(*AC.up(f_taken))
                AC.loop(act, 4, two_groups)
        silu_phase("fz", hh, hl)
        wide_out("fo2", lambda m: ada1[:, ds(16 + m, 1)])
        res = tiles("res", 32, KT)
        plain_norm(x_sb, V("normf"), res)

        phase_start()
        with nc.Block() as block:
            @block.sync
            def _(sp):
                sp.dma_start(out, res[:]).then_inc(*SP.up16(sem("out_written")))
                sp.wait_ge(*SP.need(sem("out_written"), 16))


def kernel(**inputs):
    import concourse.bacc as bacc
    from concourse.bass_utils import run_bass_kernel_spmd

    x = {k: np.asarray(v) for k, v in inputs.items()}
    arrays, plan, vat, cat = layout(x)
    nc = bacc.Bacc("TRN2", target_bir_lowering=False, num_devices=1)
    A = {n: nc.dram_tensor(n, a.shape, F32, kind="ExternalInput").ap() for n, a in arrays.items()}
    out = nc.dram_tensor("out", (P, KT, T), F32, kind="ExternalOutput").ap()
    program(nc, A, out, plan, vat, cat)
    r = run_bass_kernel_spmd(nc, [arrays], core_ids=[0])
    got = np.asarray(r.results[0]["out"])
    return np.ascontiguousarray(got.transpose(2, 1, 0).reshape(1, T, D))
```
